# Optimizing a Trainium2 kernel written in Bass

```python
import jax
import jax.numpy as jnp
from jax import lax
import numpy as np

D_MODEL = 1024
BATCH = 1
SEQ = 256
DEPTH = 2
DEC_BATCH = 8
DEC_SEQ = 1
PAST_LEN = 1024
PAGE_SIZE = 128

BRANCH_W = D_MODEL // 2
HEAD_DIM = 64
ROPE_THETA = 500000.0
EPS = 1e-6
NEG = -1e30
FORCE = 1e9
Q_BLOCK = 128

HG_HEADS = 4
HG_K = BRANCH_W // HG_HEADS
HG_V = BRANCH_W // HG_HEADS
HG_CHUNK = 64

DSA_HEADS = BRANCH_W // HEAD_DIM
DSA_KV_HEADS = 2
IDX_HEADS = 8
IDX_DIM = 64
DSA_TOPK = 256

NSA_HEADS = BRANCH_W // HEAD_DIM
NSA_KV_HEADS = 2
CMP_BLOCK = 32
CMP_STRIDE = 16
CMP_HIDDEN = HEAD_DIM
SEL_BLOCK = 64
SEL_TOPN = 16
WINDOW = 512

DSA_KV_W = DSA_KV_HEADS * HEAD_DIM
NSA_KV_W = NSA_KV_HEADS * HEAD_DIM
IN_SPLITS = (
    HG_HEADS * HG_K, HG_HEADS * HG_K, HG_HEADS * HG_V, BRANCH_W,
    DSA_HEADS * HEAD_DIM, DSA_KV_W, DSA_KV_W, IDX_HEADS * IDX_DIM, IDX_DIM, IDX_HEADS, BRANCH_W,
    NSA_HEADS * HEAD_DIM, NSA_KV_W, NSA_KV_W, NSA_KV_W, NSA_KV_W, NSA_KV_W, NSA_KV_W, NSA_HEADS * 3, BRANCH_W,
    D_MODEL, D_MODEL, D_MODEL,
)
IN_COLS = sum(IN_SPLITS)
CACHE_SPLITS = (DSA_KV_W, DSA_KV_W, IDX_DIM, NSA_KV_W, NSA_KV_W, NSA_KV_W, NSA_KV_W)
CACHE_W = sum(CACHE_SPLITS)
WIN_W = 2 * NSA_KV_W

kernel_name = 'hybrid_hgrn2_dsa_nsa_step'

def _split(z, widths):
    cuts = [int(c) for c in np.cumsum(widths)[:-1]]
    return jnp.split(z, cuts, axis=-1)

def _rms(x, g):
    x32 = x.astype(jnp.float32)
    y = x32 * lax.rsqrt(jnp.mean(x32 * x32, axis=-1, keepdims=True) + EPS)
    return (y * g.astype(jnp.float32)).astype(x.dtype)

def _rope(x, pos):
    half = (x.shape[-1] // 4) // 2
    inv = ROPE_THETA ** (-jnp.arange(half, dtype=jnp.float32) / half)
    ang = pos.astype(jnp.float32)[:, None] * inv[None, :]
    cos = jnp.cos(ang)[:, None, :].astype(x.dtype)
    sin = jnp.sin(ang)[:, None, :].astype(x.dtype)
    x1, x2, xp = x[..., :half], x[..., half:2 * half], x[..., 2 * half:]
    return jnp.concatenate([x1 * cos - x2 * sin, x1 * sin + x2 * cos, xp], axis=-1)

def _map_query_blocks(fn, qpos, *arrs):
    lq = qpos.shape[0]
    qb = min(Q_BLOCK, lq)
    pad = (-lq) % qb
    nb = (lq + pad) // qb
    qpos_b = jnp.pad(qpos, (0, pad), mode='edge').reshape(nb, qb)
    blocks = []
    for a in arrs:
        a = jnp.pad(a, [(0, 0), (0, pad)] + [(0, 0)] * (a.ndim - 2), mode='edge')
        blocks.append(jnp.moveaxis(a.reshape(a.shape[0], nb, qb, *a.shape[2:]), 1, 0))
    out = lax.map(lambda args: fn(*args), (qpos_b, *blocks))
    out = jnp.moveaxis(out, 0, 1)
    return out.reshape(out.shape[0], nb * qb, *out.shape[3:])[:, :lq]

def _hgrn2(q, k, v, logf, s0):
    B, L, H, _ = q.shape
    c = min(HG_CHUNK, L)
    pad = (-L) % c
    n = (L + pad) // c

    def chunks(a):
        a = jnp.pad(a.astype(jnp.float32), ((0, 0), (0, pad), (0, 0), (0, 0)))
        return a.reshape(B, n, c, H, a.shape[-1]).transpose(1, 0, 3, 2, 4)

    tril = jnp.tril(jnp.ones((c, c), dtype=bool))

    def step(S, inp):
        qc, kc, vc, gc = inp
        b = jnp.cumsum(gc, axis=2)
        diff = b[:, :, :, None, :] - b[:, :, None, :, :]
        decay = jnp.exp(jnp.where(tril[:, :, None], diff, -jnp.inf))
        A = jnp.einsum('bhtk,bhsk,bhtsk->bhts', qc, kc, decay)
        o = jnp.einsum('bhts,bhsv->bhtv', A, vc) + jnp.einsum('bhtk,bhkv->bhtv', qc * jnp.exp(b), S)
        bl = b[:, :, -1:, :]
        S = jnp.exp(bl[:, :, 0, :, None]) * S + jnp.einsum('bhsk,bhsv->bhkv', kc * jnp.exp(bl - b), vc)
        return S, o

    S, o = lax.scan(step, s0.astype(jnp.float32), (chunks(q), chunks(k), chunks(v), chunks(logf)))
    o = o.transpose(1, 0, 3, 2, 4).reshape(B, n * c, H, v.shape[-1])[:, :L]
    return o, S

def _dsa_attend(q, iq, iw, qpos, k, v, ik):
    lk = k.shape[1]
    n_top = min(DSA_TOPK, lk // 4)
    kpos = jnp.arange(lk, dtype=jnp.int32)
    g = DSA_HEADS // DSA_KV_HEADS
    take = jax.vmap(lambda a, i: a[i])

    def block(qp, qb, iqb, iwb):
        bq, t = qb.shape[:2]
        dots = jnp.einsum('bthd,bsd->bths', iqb, ik, preferred_element_type=jnp.float32) * IDX_DIM ** -0.5
        score = jnp.einsum('bth,bths->bts', iwb.astype(jnp.float32), jax.nn.relu(dots))
        score = jnp.where(kpos[None, None, :] <= qp[None, :, None], score, NEG)
        sel = lax.top_k(score, n_top)[1]
        kg, vg = take(k, sel), take(v, sel)
        qg = qb.reshape(bq, t, DSA_KV_HEADS, g, HEAD_DIM)
        s = jnp.einsum('btkgd,btjkd->btkgj', qg, kg, preferred_element_type=jnp.float32) * HEAD_DIM ** -0.5
        s = jnp.where((sel <= qp[None, :, None])[:, :, None, None, :], s, NEG)
        o = jnp.einsum('btkgj,btjkd->btkgd', jax.nn.softmax(s, axis=-1), vg.astype(jnp.float32))
        return o.reshape(bq, t, DSA_HEADS * HEAD_DIM)

    return _map_query_blocks(block, qpos, q, iq, iw)

def _compress(kv, pe, w1, b1, w2):
    B, lk, h, d = kv.shape
    n_cmp = (lk - CMP_BLOCK) // CMP_STRIDE + 1
    idx = jnp.arange(n_cmp)[:, None] * CMP_STRIDE + jnp.arange(CMP_BLOCK)[None, :]
    blk = kv[:, idx] + pe[:, None, :]
    blk = jnp.swapaxes(blk, 2, 3).reshape(B, n_cmp, h, CMP_BLOCK * d)
    return jax.nn.silu(blk @ w1 + b1) @ w2

def _nsa_cmp_sel(q, qpos, ck, cv, sk, sv):
    B, lk = sk.shape[:2]
    n_cmp = ck.shape[1]
    n_sel = -(-lk // SEL_BLOCK)
    n_top = min(SEL_TOPN, n_sel)
    g = NSA_HEADS // NSA_KV_HEADS
    scale = HEAD_DIM ** -0.5
    c_start = jnp.arange(n_cmp, dtype=jnp.int32) * CMP_STRIDE
    c_end = c_start + CMP_BLOCK - 1
    s_start = jnp.arange(n_sel, dtype=jnp.int32) * SEL_BLOCK
    cover = jnp.clip(jnp.minimum(c_start[:, None] + CMP_BLOCK, s_start[None, :] + SEL_BLOCK)
                     - jnp.maximum(c_start[:, None], s_start[None, :]), 0, None).astype(jnp.float32) / CMP_BLOCK
    padk = ((0, 0), (0, n_sel * SEL_BLOCK - lk), (0, 0), (0, 0))
    skb = jnp.pad(sk, padk).reshape(B, n_sel, SEL_BLOCK, NSA_KV_HEADS, HEAD_DIM).transpose(0, 3, 1, 2, 4)
    svb = jnp.pad(sv, padk).reshape(B, n_sel, SEL_BLOCK, NSA_KV_HEADS, HEAD_DIM).transpose(0, 3, 1, 2, 4)
    heads_idx = jnp.arange(NSA_KV_HEADS)[None, :, None]
    take_blocks = jax.vmap(lambda a, i: a[heads_idx, i])

    def block(qp, qb):
        bq, t = qb.shape[:2]
        qg = qb.reshape(bq, t, NSA_KV_HEADS, g, HEAD_DIM)
        cvalid = (c_end[None, :] <= qp[:, None])[None, :, None, None, :]
        s = jnp.einsum('btkgd,bckd->btkgc', qg, ck, preferred_element_type=jnp.float32) * scale
        p = jnp.where(cvalid, jax.nn.softmax(jnp.where(cvalid, s, NEG), axis=-1), 0.0)
        o_cmp = jnp.einsum('btkgc,bckd->btkgd', p, cv.astype(jnp.float32))
        imp = jnp.einsum('btkgc,cj->btkj', p, cover)
        tb = (qp // SEL_BLOCK)[:, None]
        blk = jnp.arange(n_sel, dtype=jnp.int32)[None, :]
        forced = ((blk == 0) | (blk == tb) | (blk == tb - 1))[None, :, None, :]
        causal = (s_start[None, :] <= qp[:, None])[None, :, None, :]
        imp = jnp.where(causal, jnp.where(forced, FORCE, imp), NEG)
        sel = lax.top_k(imp, n_top)[1]
        kg = take_blocks(skb, sel).reshape(bq, t, NSA_KV_HEADS, n_top * SEL_BLOCK, HEAD_DIM)
        vg = take_blocks(svb, sel).reshape(bq, t, NSA_KV_HEADS, n_top * SEL_BLOCK, HEAD_DIM)
        kpos = (sel[..., None] * SEL_BLOCK + jnp.arange(SEL_BLOCK, dtype=jnp.int32)).reshape(
            bq, t, NSA_KV_HEADS, n_top * SEL_BLOCK)
        s2 = jnp.einsum('btkgd,btkjd->btkgj', qg, kg, preferred_element_type=jnp.float32) * scale
        s2 = jnp.where((kpos <= qp[None, :, None, None])[:, :, :, None, :], s2, NEG)
        o_sel = jnp.einsum('btkgj,btkjd->btkgd', jax.nn.softmax(s2, axis=-1), vg.astype(jnp.float32))
        return jnp.stack([o_cmp, o_sel], axis=2).reshape(bq, t, 2, NSA_HEADS, HEAD_DIM)

    return _map_query_blocks(block, qpos, q)

def _window_attend(q, qpos, k, v, kpos0):
    qb_len = min(Q_BLOCK, qpos.shape[0])
    band = WINDOW + qb_len
    padw = ((0, 0), (WINDOW, qb_len), (0, 0), (0, 0))
    kp, vp = jnp.pad(k, padw), jnp.pad(v, padw)
    g = NSA_HEADS // NSA_KV_HEADS

    def block(qp, qb):
        bq, t = qb.shape[:2]
        start = qp[0] - kpos0
        kb = lax.dynamic_slice_in_dim(kp, start, band, axis=1)
        vb = lax.dynamic_slice_in_dim(vp, start, band, axis=1)
        pos = qp[0] - WINDOW + jnp.arange(band, dtype=jnp.int32)
        valid = (pos[None, :] >= kpos0) & (pos[None, :] <= qp[:, None]) & (qp[:, None] - pos[None, :] < WINDOW)
        qg = qb.reshape(bq, t, NSA_KV_HEADS, g, HEAD_DIM)
        s = jnp.einsum('btkgd,bskd->btkgs', qg, kb, preferred_element_type=jnp.float32) * HEAD_DIM ** -0.5
        s = jnp.where(valid[None, :, None, None, :], s, NEG)
        o = jnp.einsum('btkgs,bskd->btkgd', jax.nn.softmax(s, axis=-1), vb.astype(jnp.float32))
        return o.reshape(bq, t, NSA_HEADS, HEAD_DIM)

    return _map_query_blocks(block, qpos, q)

def _layer(x, pos0, past_rows, win_rows, s0, lb, norm_g, w_in, hg_onorm_g, dsa_qk_g, idx_k_g,
           nsa_qk_g, cmp_pe, cmp_w1, cmp_b1, cmp_w2, w_branch, w_out):
    B, L, _ = x.shape
    dt = x.dtype
    qpos = pos0 + jnp.arange(L, dtype=jnp.int32)
    h = _rms(x, norm_g)
    (hq, hf, hi, hgate,
     dq, dk, dv, iq, ik, iw, dgate,
     nq, nck, ncv, nsk, nsv, nwk, nwv, nbg, ngate,
     ma, mb, mc) = _split(h @ w_in, IN_SPLITS)

    lbh = lb.reshape(HG_HEADS, HG_K).astype(jnp.float32)
    fr = hf.reshape(B, L, HG_HEADS, HG_K).astype(jnp.float32)
    f = lbh + (1.0 - lbh) * jax.nn.sigmoid(fr)
    logf = jnp.log(f)
    hk = (1.0 - lbh) * jax.nn.sigmoid(-fr)
    hqa = jax.nn.silu(hq).reshape(B, L, HG_HEADS, HG_K)
    hv = hi.reshape(B, L, HG_HEADS, HG_V)
    if s0 is None:
        s0 = jnp.zeros((B, HG_HEADS, HG_K, HG_V), jnp.float32)
    ho, s_new = _hgrn2(hqa, hk, hv, logf, s0)
    ho = _rms(ho.astype(dt), hg_onorm_g.reshape(HG_HEADS, HG_V)).reshape(B, L, BRANCH_W)
    y_a = ho * jax.nn.silu(hgate)

    dq_h = _rope(_rms(dq.reshape(B, L, DSA_HEADS, HEAD_DIM), dsa_qk_g[0]), qpos)
    dk_h = _rope(_rms(dk.reshape(B, L, DSA_KV_HEADS, HEAD_DIM), dsa_qk_g[1]), qpos)
    iq_h = _rope(iq.reshape(B, L, IDX_HEADS, IDX_DIM), qpos)
    ik_h = _rope(_rms(ik, idx_k_g)[:, :, None, :], qpos)[:, :, 0]
    nq_h = _rope(_rms(nq.reshape(B, L, NSA_HEADS, HEAD_DIM), nsa_qk_g[0]), qpos)
    nck_h = _rope(_rms(nck.reshape(B, L, NSA_KV_HEADS, HEAD_DIM), nsa_qk_g[1]), qpos)
    nsk_h = _rope(_rms(nsk.reshape(B, L, NSA_KV_HEADS, HEAD_DIM), nsa_qk_g[2]), qpos)
    nwk_h = _rope(_rms(nwk.reshape(B, L, NSA_KV_HEADS, HEAD_DIM), nsa_qk_g[3]), qpos)
    flat = lambda a: a.reshape(B, L, -1)
    rows = jnp.concatenate([flat(dk_h), dv, ik_h, flat(nck_h), ncv, flat(nsk_h), nsv], axis=-1)
    full = rows if past_rows is None else jnp.concatenate([past_rows.astype(dt), rows], axis=1)
    lk = full.shape[1]
    fdk, fdv, fik, fck, fcv, fsk, fsv = _split(full, CACHE_SPLITS)
    kvh = lambda a, n: a.reshape(B, lk, n, HEAD_DIM)

    yb = _dsa_attend(dq_h, iq_h, iw * IDX_HEADS ** -0.5, qpos,
                     kvh(fdk, DSA_KV_HEADS), kvh(fdv, DSA_KV_HEADS), fik)
    y_b = yb.astype(dt) * jax.nn.silu(dgate)

    ck = _compress(kvh(fck, NSA_KV_HEADS), cmp_pe[0], cmp_w1[0], cmp_b1[0], cmp_w2[0])
    cv = _compress(kvh(fcv, NSA_KV_HEADS), cmp_pe[1], cmp_w1[1], cmp_b1[1], cmp_w2[1])
    o_cs = _nsa_cmp_sel(nq_h, qpos, ck, cv, kvh(fsk, NSA_KV_HEADS), kvh(fsv, NSA_KV_HEADS))
    wrows = jnp.concatenate([flat(nwk_h), nwv], axis=-1)
    wfull = wrows if win_rows is None else jnp.concatenate([win_rows.astype(dt), wrows], axis=1)
    lw = wfull.shape[1]
    wk, wv = jnp.split(wfull, 2, axis=-1)
    o_w = _window_attend(nq_h, qpos, wk.reshape(B, lw, NSA_KV_HEADS, HEAD_DIM),
                         wv.reshape(B, lw, NSA_KV_HEADS, HEAD_DIM), pos0 + L - lw)
    gb = jax.nn.sigmoid(nbg.reshape(B, L, NSA_HEADS, 3).astype(jnp.float32))
    o_c = gb[..., 0:1] * o_cs[:, :, 0] + gb[..., 1:2] * o_cs[:, :, 1] + gb[..., 2:3] * o_w
    y_c = o_c.reshape(B, L, BRANCH_W).astype(dt) * jax.nn.silu(ngate)

    ys = jnp.stack([y_a, y_b, y_c], axis=2)
    gates = jax.nn.sigmoid(jnp.stack([ma, mb, mc], axis=2))
    m = jnp.sum(gates * jnp.einsum('blnc,ncd->blnd', ys, w_branch), axis=2)
    y = x + m @ w_out
    return y, rows, wfull[:, -min(WINDOW, lw):], s_new.astype(dt)

def setup_inputs(seed: int = 0) -> dict:
    key = jax.random.key(seed)
    ks = jax.random.split(key, 20)
    nrm = lambda k, shape, scale: scale * jax.random.normal(k, shape, jnp.float32)
    n_pages = PAST_LEN // PAGE_SIZE
    n_used = DEC_BATCH * n_pages
    n_phys = n_used + (n_used + 3) // 4
    page_table = jax.random.permutation(ks[2], n_phys)[:n_used].reshape(DEC_BATCH, n_pages).astype(jnp.int32)
    wc = min(WINDOW, PAST_LEN)
    return {
        'x_prompt': nrm(ks[0], (BATCH, SEQ, D_MODEL), 1.0),
        'x_sample': nrm(ks[1], (DEC_BATCH, DEC_SEQ, D_MODEL), 1.0),
        'cache_kv': nrm(ks[3], (DEPTH, n_phys, PAGE_SIZE, CACHE_W), 1.0),
        'page_table': page_table,
        'state_win': nrm(ks[4], (DEPTH, DEC_BATCH, wc, WIN_W), 1.0),
        'state_hgrn': nrm(ks[5], (DEPTH, DEC_BATCH, HG_HEADS, HG_K, HG_V), 0.3),
        'norm_g': 1.0 + nrm(ks[6], (DEPTH, D_MODEL), 0.02),
        'w_in': nrm(ks[7], (DEPTH, D_MODEL, IN_COLS), D_MODEL ** -0.5),
        'hgrn_lb_logits': nrm(ks[8], (DEPTH, HG_HEADS * HG_K), 0.5),
        'hgrn_onorm_g': 1.0 + nrm(ks[9], (DEPTH, HG_HEADS * HG_V), 0.02),
        'dsa_qk_norm_g': 1.0 + nrm(ks[10], (DEPTH, 2, HEAD_DIM), 0.02),
        'dsa_idx_k_norm_g': 1.0 + nrm(ks[11], (DEPTH, IDX_DIM), 0.02),
        'nsa_qk_norm_g': 1.0 + nrm(ks[12], (DEPTH, 4, HEAD_DIM), 0.02),
        'nsa_cmp_pe': nrm(ks[13], (DEPTH, 2, CMP_BLOCK, HEAD_DIM), 0.1),
        'nsa_cmp_w1': nrm(ks[14], (DEPTH, 2, CMP_BLOCK * HEAD_DIM, CMP_HIDDEN), (CMP_BLOCK * HEAD_DIM) ** -0.5),
        'nsa_cmp_b1': nrm(ks[15], (DEPTH, 2, CMP_HIDDEN), 0.01),
        'nsa_cmp_w2': nrm(ks[16], (DEPTH, 2, CMP_HIDDEN, HEAD_DIM), CMP_HIDDEN ** -0.5),
        'w_branch': nrm(ks[17], (DEPTH, 3, BRANCH_W, D_MODEL), BRANCH_W ** -0.5),
        'w_out': nrm(ks[18], (DEPTH, D_MODEL, D_MODEL), D_MODEL ** -0.5),
    }

def reference(x_prompt, x_sample, cache_kv, page_table, state_win, state_hgrn, norm_g, w_in,
              hgrn_lb_logits, hgrn_onorm_g, dsa_qk_norm_g, dsa_idx_k_norm_g, nsa_qk_norm_g,
              nsa_cmp_pe, nsa_cmp_w1, nsa_cmp_b1, nsa_cmp_w2, w_branch, w_out):
    lb_soft = jax.nn.softmax(hgrn_lb_logits.astype(jnp.float32), axis=0)
    lbs = jnp.cumsum(lb_soft, axis=0) - lb_soft[0]
    n_seq, n_pages = page_table.shape
    xp, xs = x_prompt, x_sample
    p_rows, p_win, p_hg, s_rows, s_win, s_hg = [], [], [], [], [], []
    for l in range(DEPTH):
        lw = (norm_g[l], w_in[l], hgrn_onorm_g[l], dsa_qk_norm_g[l], dsa_idx_k_norm_g[l], nsa_qk_norm_g[l],
              nsa_cmp_pe[l], nsa_cmp_w1[l], nsa_cmp_b1[l], nsa_cmp_w2[l], w_branch[l], w_out[l])
        past = cache_kv[l][page_table].reshape(n_seq, n_pages * PAGE_SIZE, CACHE_W)
        xp, pr, pw, ph = _layer(xp, 0, None, None, None, lbs[l], *lw)
        xs, sr, sw, sh = _layer(xs, PAST_LEN, past, state_win[l], state_hgrn[l], lbs[l], *lw)
        p_rows.append(pr)
        p_win.append(pw)
        p_hg.append(ph)
        s_rows.append(sr)
        s_win.append(sw)
        s_hg.append(sh)
    return (xp, xs, jnp.stack(p_rows), jnp.stack(p_win), jnp.stack(p_hg),
            jnp.stack(s_rows), jnp.stack(s_win), jnp.stack(s_hg))


_drawn_inputs = setup_inputs


def setup_inputs(seed=0):
    import zlib

    import numpy as np

    out = dict(_drawn_inputs(seed))
    spreads = {}
    factors = {'hgrn_onorm_g': 5.776,
     'dsa_qk_norm_g': 7.088,
     'dsa_idx_k_norm_g': 6.094,
     'nsa_qk_norm_g': 4.405,
     'nsa_cmp_pe': 5.228,
     'nsa_cmp_b1': 43.758}
    for name, (base, spread) in spreads.items():
        noise = np.random.default_rng([zlib.crc32(name.encode()), seed]).standard_normal(out[name].shape)
        drawn = base * np.exp(spread * noise) if base else spread * noise
        out[name] = jnp.asarray(drawn.astype(out[name].dtype))
    for name, factor in factors.items():
        out[name] = (out[name] * factor).astype(out[name].dtype)
    return out
```

```python
import numpy as np
import concourse.bass as bass
from concourse import mybir
from contextlib import ExitStack

F32 = mybir.dt.float32
I32 = mybir.dt.int32
ALU = mybir.AluOpType
ACT = mybir.ActivationFunctionType
AXX = mybir.AxisListType.X

D = 1024
LP = 256
NS = 8
LT = LP + NS
DEPTH = 2
PAST = 1024
PAGE = 128
NPG = PAST // PAGE
BW = D // 2
HD = 64
NH = 8
KD = D // 128
TOPK_P, TOPK_S = 64, 256
CB, CS = 32, 16
NCP = (LP - CB) // CS + 1
NCS = (PAST - CB) // CS + 1
SB = 64
NSEL = PAST // SB + 1
WIN = 512
CW = 832
NEG, FORCE, TAKEN = -1e30, 1e9, -3e38
EPS = 1e-6
SCALE = HD ** -0.5
GB = 4
ROWS = GB * NH

C_HQ, C_HF, C_HI, C_HG = 0, 512, 1024, 1536
C_DQ, C_DK, C_IQ, C_IK, C_DG = 2048, 2560, 2816, 3328, 3400
C_NQ, C_NCK, C_NSK, C_NWK, C_NBG, C_NG, C_MA = 3912, 4424, 4680, 4936, 5192, 5216, 5728

Z_IQ, Z_DQ, Z_NQ, Z_IK, Z_DK, Z_NCK, Z_NSK, Z_NWK, Z_NCV, Z_IW, Z_NBG, Z_HF, Z_HQ = (
    0, 4, 8, 12, 13, 14, 15, 16, 17, 18, 19, 20, 24)
NZ = 28

def _pair(name, col, z, g):
    segs = [(col + 128 * g, 128), (col + 256 + 128 * g, 128)]
    return (name, segs, [("T", z + 2 * g, 0, 128), ("T", z + 2 * g + 1, 128, 128)])


SLABS = [
    _pair("iq0", C_IQ, Z_IQ, 0), _pair("iq1", C_IQ, Z_IQ, 1),
    ("ikw", [(C_IK, HD), (C_IK, HD + NH)], [("T", Z_IK, 0, 128), ("T", Z_IW, 128, NH)]),
    ("dkv", [(C_DK, 256)], [("T", Z_DK, 0, 128), ("V", "rows", 128, 128, 128)]),
    ("n1", [(C_NCK, 256)], [("T", Z_NCK, 0, 128), ("T", Z_NCV, 128, 128)]),
    ("n2", [(C_NSK, 256)], [("T", Z_NSK, 0, 128), ("V", "rows", 128, 128, 704)]),
    ("n3", [(C_NWK, 256)], [("T", Z_NWK, 0, 128), ("V", "win", 128, 128, 128)]),
    ("n4", [(C_NBG, 24)], [("T", Z_NBG, 0, 24)]),
    _pair("dq0", C_DQ, Z_DQ, 0), _pair("dq1", C_DQ, Z_DQ, 1),
    _pair("nq0", C_NQ, Z_NQ, 0), _pair("nq1", C_NQ, Z_NQ, 1),
    ("hf0", [(C_HF, 256)], [("T", Z_HF, 0, 128), ("T", Z_HF + 1, 128, 128)]),
    ("hf1", [(C_HF + 256, 256)], [("T", Z_HF + 2, 0, 128), ("T", Z_HF + 3, 128, 128)]),
    ("hq0", [(C_HQ, 256)], [("T", Z_HQ, 0, 128), ("T", Z_HQ + 1, 128, 128)]),
    ("hq1", [(C_HQ + 256, 256)], [("T", Z_HQ + 2, 0, 128), ("T", Z_HQ + 3, 128, 128)]),
    ("hi0", [(C_HI, 256)], [("V", "hv", 0, 256, 0)]),
    ("hi1", [(C_HI + 256, 256)], [("V", "hv", 0, 256, 256)]),
]
GROUPS = {"iq": (Z_IQ, 4, False, None), "k": (Z_IK, 5, True, [2, 1, 4, 5, 6]),
          "dq": (Z_DQ, 4, True, [0] * 4), "nq": (Z_NQ, 4, True, [3] * 4)}
FRONT = ["iq0", "iq1", "ikw", "dkv", "n1", "iq", "n2", "n3", "n4", "k", "dq0", "dq1", "nq0", "dq", "nq1", "nq"]
BACK = ["hf0", "hf1", "hq0", "hq1", "hi0", "hi1"]

GATE_SLABS = []
for _a in range(3):
    GATE_SLABS += [(f"g{_a}{i}", "gate", _a, i) for i in range(2)]
    GATE_SLABS += [(f"m{_a}{i}", "mix", _a, i) for i in range(4)]
    GATE_SLABS += [(f"b{_a}{i}", "branch", _a, i) for i in range(2)]
OUT_SLABS = [(f"o{i}", "out", 0, i) for i in range(4)]
STREAM = ([n for n in FRONT + BACK if n not in GROUPS] + [s[0] for s in GATE_SLABS] + [s[0] for s in OUT_SLABS])
NSLOT = 3
SLAB_OF = {s[0]: s for s in SLABS}


def slab_dmas(name):
    if name in SLAB_OF:
        return len(SLAB_OF[name][1])
    if name[0] == "g":
        return 1 if name[1] == "0" else 2
    if name[0] == "b":
        return 1 if name[1] == "0" else 2
    return 1


SLOT_AT, SLOT_USES, SLOT_DMAS = {}, [0] * NSLOT, [0] * NSLOT
for _i, _n in enumerate(STREAM):
    _s = _i % NSLOT
    SLOT_USES[_s] += 1
    SLOT_DMAS[_s] += slab_dmas(_n)
    SLOT_AT[_n] = (_s, SLOT_USES[_s], SLOT_DMAS[_s])

JOB_AT, LAST_JOB, NJOB = {}, {}, 0
for _n in FRONT + BACK:
    if _n in SLAB_OF:
        for _j, _job in enumerate(SLAB_OF[_n][2]):
            JOB_AT[_n, _j] = NJOB
            NJOB += 2 if _job[0] == "V" else 1
        LAST_JOB[_n] = NJOB
LAST_USE = {}
for _n, _kind, _a, _i in GATE_SLABS + OUT_SLABS:
    LAST_USE[_n] = {"gate": f"g {_a} {2 * _i + 1}", "mix": f"m {_a} {2 * _i + 1}", "branch": f"b {_a} {4 * _i + 3}",
                    "out": f"o {3 * _i + 2}"}[_kind]

CONST = {}
_off = 0
for _name, _w in (("ident", 128), ("head_ones", 128), ("ones", 128), ("rot", 128), ("cos", LT), ("sin", LT),
                  ("levels", 8 * 128), ("causal", 384), ("cmp_add", 2 * NCP), ("cmp_mul", 2 * NCP),
                  ("chunk_reset", LP), ("own4", GB * ROWS), ("seq8", 64), ("own_s", 2 * NS), ("expand", 2 * ROWS),
                  ("cover", NSEL), ("group_sum", ROWS), ("not_forced", NSEL), ("forced", NSEL), ("order", NSEL)):
    CONST[_name] = (_off, _w)
    _off += _w
NCONST = _off


def constants():
    c = {n: np.zeros((128, w), np.float32) for n, (_, w) in CONST.items()}
    p = np.arange(128)
    c["ident"][:] = np.eye(128)
    c["head_ones"][:] = p[:, None] // HD == p[None, :] // HD
    c["ones"][:] = 1
    half = HD // 8
    for b in (0, HD):
        for i in range(half):
            c["rot"][b + half + i, b + i] = -1
            c["rot"][b + i, b + half + i] = 1
    pos = np.concatenate([np.arange(LP), np.full(NS, PAST)]).astype(np.float32)
    inv = np.float32(500000.0) ** (-np.arange(half, dtype=np.float32) / half)
    ang = (pos[None, :] * inv[:, None]).astype(np.float32).astype(np.float64)
    c["cos"][:] = 1
    for b in (0, HD):
        for r in (0, half):
            c["cos"][b + r:b + r + half] = np.cos(ang)
            c["sin"][b + r:b + r + half] = np.sin(ang)
    s, t = p[:, None], p[None, :]
    lv = c["levels"].reshape(128, 8, 128)
    for i in range(7):
        w = 1 << i
        lv[:, i] = (s // (2 * w) == t // (2 * w)) & (s % (2 * w) < w) & (t % (2 * w) >= w)
    lv[:, 7] = s == t
    q, k = p[:, None], np.arange(LP)[None, :]
    c["causal"][:, :128] = np.where(k[:, :128] <= q, 0, NEG)
    c["causal"][:, 128:] = np.where(k <= q + 128, 0, NEG)
    end = np.arange(NCP) * CS + CB - 1
    for i in range(2):
        ok = end[None, :] <= q + 128 * i
        c["cmp_add"][:, i * NCP:(i + 1) * NCP] = np.where(ok, 0, NEG)
        c["cmp_mul"][:, i * NCP:(i + 1) * NCP] = ok
    c["chunk_reset"][:] = (np.arange(LP) % 64 != 0)
    c["own4"][:] = (np.arange(GB)[:, None] == np.arange(ROWS)[None, :] // NH).reshape(1, -1)
    c["seq8"][:NS] = np.arange(NS)[:, None] == np.arange(64)[None, :] // NH
    for g in range(2):
        for r in range(ROWS):
            c["own_s"][r, g * NS + g * GB + r // NH] = 1
            c["expand"][g * GB + r // NH, g * ROWS + r] = 1
    cs, ss = np.arange(NCS) * CS, np.arange(NSEL) * SB
    c["cover"][:NCS] = np.clip(np.minimum(cs[:, None] + CB, ss[None, :] + SB)
                               - np.maximum(cs[:, None], ss[None, :]), 0, None) / CB
    r = np.arange(ROWS)
    c["group_sum"][:ROWS] = r[:, None] // 4 == r[None, :] // 4
    forced = np.isin(np.arange(NSEL), (0, NSEL - 2, NSEL - 1))
    c["not_forced"][:] = ~forced
    c["forced"][:] = forced * FORCE
    c["order"][:] = np.arange(NSEL) + 1
    return np.concatenate([c[n] for n in CONST], axis=1)


def branch_gate_rows():
    m = np.zeros((24, 3, 4, 128), np.float32)
    for h in range(NH):
        for c in range(3):
            m[h * 3 + c, c, h % 4, (h // 4) * HD:(h // 4 + 1) * HD] = 1
    return m.reshape(24, 12 * 128)


def hybrid_step(nc, x_prompt, x_sample, cache_kv, page_table, state_win, state_hgrn, norm_g, w_in,
                hgrn_lb_logits, hgrn_onorm_g, dsa_qk_norm_g, dsa_idx_k_norm_g, nsa_qk_norm_g, nsa_cmp_pe,
                nsa_cmp_w1, nsa_cmp_b1, nsa_cmp_w2, w_branch, w_out, const, gate_rows,
                y_prompt, y_sample, p_rows, p_win, p_hgrn, s_rows, s_win, s_hgrn):
    ctx = ExitStack()
    with ctx:
        def sb(name, shape, dt=F32):
            return ctx.enter_context(nc.sbuf_tensor(name, shape, dt))

        def sem(name):
            return ctx.enter_context(nc.semaphore(name))

        ctx.enter_context(nc.allow_non_contiguous_dma(reason="gains and biases of a few hundred elements"))
        cst = sb("cst", [128, NCONST])
        xp = sb("xp", [128, 2, D])
        xs = sb("xs", [NS, D])
        hT = sb("hT", [128, KD, LT])
        slab = sb("slab", [128, NSLOT, 2048])
        w1 = sb("w1", [128, CB, 128])
        w2 = sb("w2", [128, 2, 128])
        Y = sb("Y", [128, 3, 4, LT])
        QF = sb("QF", [128, 3, 64])
        QC = sb("QC", [128, 2, GB * (ROWS + NH)])
        iwB = sb("iwB", [128, 64])
        work = sb("work", [NS, PAST + 8])
        top8 = sb("top8", [128, 8])
        kn = sb("kn", [128, 3, NS])
        vn = sb("vn", [NS, 3, 128])
        gbs = sb("gbs", [128, 12, NS])
        gx = sb("gx", [128, KD])
        gains = sb("gains", [128, 7])
        gains_row = sb("gains_row", [8, HD])
        gho = sb("gho", [128, 4])
        pe_row = sb("pe_row", [CB, 2, HD])
        peT = sb("peT", [128, 2, CB])
        b1 = sb("b1", [128, 2])
        hbias = sb("hbias", [128, 2])
        lbl = sb("lbl", [128, DEPTH + 1, 4])
        lb = sb("lb", [128, 4])
        lb1 = sb("lb1", [128, 4])
        pt = sb("pt", [1, NS * NPG], I32)
        st = sb("st", [128, 64])
        spare = sb("spare", [128, 1])
        epsb = sb("epsb", [128, 1])
        sa = sb("sa", [128, 64])
        ARENA = 28432
        arena = sb("arena", [128, ARENA])

        def at(off, *shape, rows=128):
            n = int(np.prod(shape))
            assert off + n <= ARENA, (off, shape)
            v = arena[0:rows, off:off + n]
            if len(shape) == 2:
                v = v.rearrange("p (a b) -> p a b", a=shape[0])
            if len(shape) == 3:
                v = v.rearrange("p (a b c) -> p a b c", a=shape[0], b=shape[1])
            if len(shape) == 4:
                v = v.rearrange("p (a b c d) -> p a b c d", a=shape[0], b=shape[1], c=shape[2])
            return v

        Z = at(0, NZ, LT)
        row = at(7392, 3, CW)
        wrow = at(9888, 3, 2 * 128)
        HK = at(12192, 512)[0:NS]
        VD = at(12704, NS, 128)[0:NS]
        HSQ = at(18208, 4, LT)
        HV = at(10656, 3, BW)
        RL = at(12192, 2, 384)
        acc = at(12960, 384)
        msk = at(13728, 384)
        ikst = at(14112, 2, NPG, HD)
        ikT = at(15136, 2, PAST, rows=HD)
        RD = at(17184, 2, 64)
        idxT = at(17312, NPG, NS)
        iwD = at(17376, NS, NH)[0:NS]
        iwP = at(17440, 2, NH)
        i2 = at(17456, 64)[0:NS]
        SQ = at(18208, 5, LT)
        T1 = at(19528, 5, LT)
        T2 = at(20848, 5, LT)
        S = at(14112, NS, 4, 128)
        E_ = at(18208, 4, LP)
        D_ = at(19232, 4, LP)
        M_ = at(20256, 2, 1024)
        cb = at(22304, 4, LP)
        kT = at(23360, 4, LT)
        fT = at(24416, 4, LT)
        AT = at(25472, 3, 4, 128)
        SX = at(18208, 2, 1536)
        PT = at(21280, 3, 512)
        OC = at(22816, 3, 4, LP)
        SC = at(25888, 2, NH, NCP)
        SC2 = at(26128, 2, NH, NCP)
        hidP = at(26368, 2, 16)
        ckP = at(26400, 16)
        cvP = at(26416, 128)
        ehP = at(26544, 16)
        PTC = at(10656, NH, LP)
        nbs = at(14112, LT)
        gsel = at(14376, 12, 128)
        V = at(0, GB, NPG, 2, 128)
        cT = at(8192, 2, GB, PAST)
        Vw = at(16384, GB, 4, 128)
        kst = at(18432, 4, 512)
        kws = at(20480, 4, 128)
        KT = at(20992, 2, 2, 128)
        KTw = at(21504, 4, 128)
        scT = at(22016, 20, GB, NH)
        SS = at(22656, 3, 1032)
        PTd = at(25752, 20, ROWS)
        PTx = at(26392, 20, ROWS)
        hid = at(27032, 2, GB, 63)
        eh = at(27536, GB, 63)
        ckd = at(27788, GB, 63)
        CV = at(22656, GB, 128)
        PTc = at(28040, ROWS)
        PTcx = at(28072, GB, ROWS)
        sc4 = at(28200, 64)
        dr = at(28264, 64)
        pn8 = at(28328, 3, ROWS)[0:NS]
        sig = at(0, KD, LT)
        mT = at(2112, KD, LT)
        gz = at(4224, 4, LT)
        mtmp = at(5280, 2, LT)
        yo = at(5808, 3, D)

        def K(name, rows=128):
            o, w = CONST[name]
            return cst[0:rows, o:o + w]

        ident, head_ones, ones, rot = K("ident"), K("head_ones"), K("ones"), K("rot")
        lvl = K("levels").rearrange("p (l t) -> p l t", l=8).bitcast(I32)
        causal = K("causal")
        ps = ctx.enter_context(nc.psum_tensor("ps", [128, 8, 512], F32))


        all_steps = []

        class Steps:

            def __init__(self, name, steps, lead=0):
                self.sem, self.steps, self.done, self.lead = sem(name), list(steps), 0, lead
                self.n = len(self.steps)
                all_steps.append(self)

            def __call__(self, r, step):
                return r * self.n + (self.steps.index(step) + 1 + self.lead * self.n)

            def before(self, r, step):
                assert self.lead
                return r * self.n + (self.steps.index(step) + 1)

            def mark(self, step):
                assert self.steps[self.done % len(self.steps)] == step, (step, self.steps, self.done)
                self.done += 1
                return 1

        consts_in, x_in, pages_in, small_in = sem("consts_in"), sem("x_in"), sem("pages_in"), sem("small_in")
        w1_in, w2_in, S_in, gsel_in, v_in = sem("w1_in"), sem("w2_in"), sem("S_in"), sem("gsel_in"), sem("v_in")
        slab_in = [sem(f"slab_in{i}") for i in range(NSLOT)]
        ik_in = [sem(f"ik_in{i}") for i in range(2)]
        page_in = [sem(f"page_in{i}") for i in range(4)]
        win_in, rows_out, hg_out, y_out, win_out = (sem("win_in"), sem("rows_out"), sem("hg_out"), sem("y_out"),
                                                    sem("win_out"))
        init_done = sem("init_done")
        waited = sem("waited")
        x_ready = sem("x_ready")
        lb_v, lb_a = sem("lb_v"), sem("lb_a")
        proj_ready, proj_free = sem("proj_ready"), sem("proj_free")
        norm_a = Steps("norm_a", ["rstd"])
        norm_v = Steps("norm_v", ["diag", "small"] + [f"hT {k}" for k in range(KD)])
        norm_p = Steps("norm_p", ["small"] + [f"xT {k}" for k in range(KD)])
        grp_a = Steps("grp_a", ["sq k", "rs k", "sq dq", "rs dq", "sq nq", "rs nq"])
        grp_p = Steps("grp_p", ["rot iq", "ss k", "rot k", "ss dq", "rot dq", "ss nq", "rot nq"])
        grp_v = Steps("grp_v", ["zr iq", "zn k", "zr k", "zn dq", "zr dq", "zn nq", "zr nq"])
        rows_p = Steps("rows_p", ["rows"])
        rows_a = Steps("rows_a", ["rows"])
        pidx_p = Steps("pidx_p", ["iw"] + [f"dot {h}" for h in range(NH)])
        pidx_a = Steps("pidx_a", ["iw"] + [f"relu {h}" for h in range(NH)])
        pidx_v = Steps("pidx_v", [f"acc {h}" for h in range(NH)] + ["mask"])
        sidx_v = Steps("sidx_v", ["qf", "iwd", "new", "left out"])
        sidx_p = Steps("sidx_p", ["iwb", "new", "flat"])
        sidx_a = Steps("sidx_a", ["iwb", "new", "flat"])
        skey_p = Steps("skey_p", ["T 0", "T 1", "dot 0", "dot 1"], lead=1)
        skey_a = Steps("skey_a", ["T 0", "T 1", "relu 0", "relu 1"])
        skey_v = Steps("skey_v", ["sum 0", "sum 1"], lead=1)
        LV = list(range(9))
        hg_a = Steps("hg_a", ["exp", "ln"] + [f"e {i}" for i in LV] + ["far", "o", "kfT", "sfin", "kd", "od", "sq", "rs"])
        hg_v = Steps("hg_v", ["f", "d 0", "a diag"] + sum([[f"d {i + 1}"] * (i < 8) + [f"m {i}"]
                     + [f"a {i - 1}"] * (1 <= i <= 7) for i in LV], []) + sum([[f"vd {h}", f"sn {h}"] for h in range(4)], []) + ["done"])
        hg_p = Steps("hg_p", ["a diag"] + [f"a {i}" for i in range(8)] + ["o", "kfT", "sfin", "kd"]
                     + [f"kv {h}" for h in range(4)] + ["od", "ss"])
        U = list(range(6))
        at_p = Steps("at_p", ["s 0"] + sum([[f"s {u + 1}"] * (u < 5) + [f"t {u}", f"o {u}"] for u in U], []))
        at_a = Steps("at_a", ["e 0"] + sum([[f"e {u + 1}"] * (u < 5) + [f"pt {u}"] for u in U], []))
        at_v = Steps("at_v", ["s 0"] + sum([[f"s {u + 1}"] * (u < 5) + [f"n {u}"] + [f"ev {u - 1}"] * (u > 0)
                                            for u in U], []) + ["ev 5"])
        cp_p = Steps("cp_p", ["h 0", "out 0", "h 1", "out 1", "s", "t", "o"] + [f"gb {i}" for i in range(12)])
        cp_v = Steps("cp_v", ["h 0", "hid 0", "h 1", "hid 1", "s", "n", "nb", "ev"] + [f"gb {i}" for i in range(12)]
                     + ["prompt done"])
        cp_a = Steps("cp_a", ["e 0", "out 0", "e 1", "out 1", "e", "t", "nb"])
        pg_p = Steps("pg_p", sum([[f"T {i}"] + [f"s {i - 1}"] * (i > 0) for i in range(NPG)], []) + ["s 7", "T win", "s win"], lead=1)
        pg_a = Steps("pg_a", [f"T {i}" for i in range(NPG)] + ["T win"])
        pg_v = Steps("pg_v", [f"T {i}" for i in range(NPG)] + ["s"], lead=1)
        G_ = (0, 1)
        dc_p = Steps("dc_p", ["h 0", "ck", "h 1", "cv", "s cmp", "t cmp", "imp", "group imp", "flat", "new", "PT",
                              "oT"])
        dc_v = Steps("dc_v", ["h 0", "hid 0", "h 1", "hid 1", "s cmp", "n cmp", "ptx cmp", "imp", "drop", "masked", "new p",
                              "scaled", "ev"] )
        dc_a = Steps("dc_a", ["e 0", "ck", "e 1", "cv", "e cmp", "t cmp", "flat", "e", "PT"])
        dx_v = Steps("dx_v", [f"x {b}" for b in range(GB)])
        dx_p = Steps("dx_p", [f"x {b}" for b in range(GB)])
        ga_p = Steps("ga_p", sum([[f"g {a} {j}" for j in range(4)] + [f"m {a} {d}" for d in range(KD)]
                                  + [f"b {a} {d}" for d in range(KD)] for a in range(3)], []) + [f"o {i}" for i in range(12)])
        ga_a = Steps("ga_a", sum([[f"g {a} {j}" for j in range(4)] + [f"m {a} {d}" for d in range(KD)]
                                  for a in range(3)], []))
        ga_v = Steps("ga_v", sum([[f"y {a} {j}" for j in range(4)] + [f"b {a} {d}" for d in range(KD)]
                                  for a in range(3)], []) + [f"o {i}" for i in range(12)])

        block = ctx.enter_context(nc.Block())
        cosb = lambda n: K("cos").unsqueeze(1).to_broadcast([128, n, LT])
        sinb = lambda n: K("sin").unsqueeze(1).to_broadcast([128, n, LT])
        halves = (slice(0, HD), slice(HD, 128))
        seq_cols = slice(LP, LT)
        attn = [(0, Z_DQ, Z_DK), (1, Z_NQ, Z_NSK), (2, Z_NQ, Z_NWK)]

        def values(a, t):
            return (row[:, t, 128:256], row[:, t, 704:832], wrow[:, t, 128:256])[a]

        def slab_view(name):
            slot = SLOT_AT[name][0]
            k = 4 if name[0] == "b" else KD
            return slab[:, slot, :].rearrange("p (k c) -> p k c", k=k)

        def pair_half(v, g, src):
            return (v.rearrange("p k (j g c) -> p k j g c", j=2, g=2)[:, :, :, g, :],
                    src.rearrange("p k (j c) -> p k j c", j=2))

        def slab_sources(name, l):
            v = slab_view(name)
            wl = w_in[bass.ds(l, 1), :, :].rearrange("a (p k) c -> p (a k) c", k=KD)
            if name in SLAB_OF:
                out, o = [], 0
                for g, (col, width) in enumerate(SLAB_OF[name][1]):
                    src = wl[:, :, col:col + width]
                    if name[:2] in ("iq", "dq", "nq"):
                        out.append(pair_half(v, g, src))
                    else:
                        out.append((v[:, :, o:o + width], src))
                    o += width
                return out
            a, i = int(name[1]) if name[0] != "o" else 0, int(name[-1])
            if name[0] == "g":
                if a == 0:
                    c = C_HG + 256 * i
                    return [(v[:, :, :], wl[:, :, c:c + 256])]
                c = (C_DG, C_NG)[a - 1] + 128 * i
                return [pair_half(v, g, wl[:, :, c + 256 * g:c + 256 * g + 128]) for g in range(2)]
            if name[0] == "m":
                c = C_MA + D * a + 256 * i
                return [(v[:, :, :], wl[:, :, c:c + 256])]
            if name[0] == "b":
                wb = w_branch[bass.ds(l, 1), a, :, 512 * i:512 * i + 512]
                if a == 0:
                    return [(v[:, :, :], wb.rearrange("a (j p) d -> p (a j) d", j=4))]
                w = wb.rearrange("a (g j p) d -> g p (a j) d", g=2, j=4)
                return [(v[h, :, :], w[g]) for g, h in enumerate(halves)]
            wo = w_out[bass.ds(l, 1), :, 256 * i:256 * i + 256]
            return [(v[:, :, :], wo.rearrange("a (k p) c -> p (a k) c", k=KD))]

        def holds(engine):
            engine.sem_inc(waited, 1)

        @block.sync
        def _(sp):
            sp.dma_start(cst[:, :], const).then_inc(consts_in, 16)
            sp.dma_start(xp[:, :, :], x_prompt[0].rearrange("(t p) d -> p t d", t=2)).then_inc(x_in, 16)
            sp.dma_start(xs[:, :], x_sample.rearrange("s o d -> s (o d)")).then_inc(x_in, 16)
            for i in range(DEPTH):
                sp.dma_start(lbl[:, i, :], hgrn_lb_logits[i].rearrange("(h k) -> k h", h=4)).then_inc(x_in, 16)
            sp.dma_start(pt[:, :], page_table.rearrange("(o a) b -> o (a b)", o=1)).then_inc(pages_in, 16)
            sp.wait_ge(pages_in, 16)
            sp.wait_ge(init_done, 2)
            with sp.Fori(0, DEPTH) as l:
                l1 = bass.ds(l, 1)

                def send(name):
                    slot = SLOT_AT[name][0]
                    at_ = STREAM.index(name)
                    if at_ >= NSLOT:
                        old = STREAM[at_ - NSLOT]
                        if old in SLAB_OF:
                            sp.wait_ge(proj_ready, l * NJOB + LAST_JOB[old])
                        else:
                            sp.wait_ge(ga_p.sem, ga_p(l, LAST_USE[old]))
                        holds(sp)
                    for dst, src in slab_sources(name, l):
                        sp.dma_start(dst, src).then_inc(slab_in[slot], 16)

                sp.wait_ge(x_ready, l + 1)
                sp.dma_start(gx[:, :], norm_g[l1, :].rearrange("a (p k) -> p (a k)", k=KD)).then_inc(small_in, 16)
                sp.dma_start(gho[:, :], hgrn_onorm_g[l1, :].rearrange("a (h v) -> v (a h)", h=4)).then_inc(small_in, 16)
                sp.dma_start(gains_row[0:2, :], dsa_qk_norm_g[l1].rearrange("a g d -> (a g) d")).then_inc(small_in, 16)
                sp.dma_start(gains_row[2:3, :], dsa_idx_k_norm_g[l1]).then_inc(small_in, 16)
                sp.dma_start(gains_row[3:7, :], nsa_qk_norm_g[l1].rearrange("a g d -> (a g) d")).then_inc(small_in, 16)
                sp.dma_start(pe_row[:, :, :], nsa_cmp_pe[l1].rearrange("a k s d -> s (a k) d")).then_inc(small_in, 16)
                for h in halves:
                    sp.dma_start(b1[h, :], nsa_cmp_b1[l1].rearrange("a k d -> d (a k)")).then_inc(small_in, 16)
                    sp.dma_start(w2[h, :, h], nsa_cmp_w2[l1].rearrange("a k c d -> c (a k) d")).then_inc(small_in, 16)
                for name in FRONT:
                    if name in SLAB_OF:
                        send(name)
                with sp.Fori(0, NS // 2) as s2:
                    r = l * (NS // 2) + s2
                    for u in range(2):
                        for i in range(NPG):
                            if i == 0:
                                holds(sp)
                            page = sp.value_load(pt[0:1, bass.ds((s2 * 2 + u) * NPG + i, 1)], min_val=0, max_val=cache_kv.shape[1] - 1)
                            if i == 0:
                                sp.wait_ge(skey_p.sem, skey_p.before(r, f"T {u}"))
                            src = cache_kv[l1, bass.ds(page, 1), :, :].rearrange("a b p c -> p (a b) c")[:, 0, 256:320]
                            sp.dma_start(ikst[:, u, i, :], src).then_inc(ik_in[u], 16)
                for name in BACK:
                    if name in SLAB_OF:
                        send(name)
                sp.wait_ge(sidx_v.sem, sidx_v(l, "new"))
                for h in range(4):
                    sp.dma_start(S[:, :, h, :], state_hgrn[l1, :, h].rearrange("a s k v -> k (a s) v")).then_inc(S_in, 16)

                def send_w1(kv):
                    for h in halves:
                        sp.dma_start(w1[h, :, h], nsa_cmp_w1[l1, kv].rearrange("a (s d) c -> d (a s) c", d=HD)).then_inc(w1_in, 16)

                send_w1(0)
                sp.wait_ge(cp_p.sem, cp_p(l, "h 0"))
                send_w1(1)
                sp.wait_ge(hg_out, l * 32 + 32)
                sp.dma_start(gsel[0:24], gate_rows.rearrange("r (n c) -> r n c", n=12)).then_inc(gsel_in, 16)
                sp.wait_ge(cp_v.sem, cp_v(l, "prompt done"))
                sp.wait_ge(rows_out, l * 96 + 96)
                for g in range(2):
                    if g:
                        sp.wait_ge(dc_v.sem, dc_v(l * 2 + g - 1, "ev"))
                    holds(sp)
                    with sp.Fori(0, GB) as b:
                        s = g * GB + b
                        r = (l * 2 + g) * GB + b
                        b1_ = bass.ds(b, 1)
                        for i in range(NPG):
                            page = sp.value_load(pt[0:1, bass.ds(s * NPG + i, 1)], min_val=0, max_val=cache_kv.shape[1] - 1)
                            pg = cache_kv[l1, bass.ds(page, 1), :, :].rearrange("a b p c -> p (a b) c")
                            sp.wait_ge(pg_p.sem, pg_p(r, f"T {i - 4}") if i >= 4 else pg_p.before(r, f"T {i + 4}"))
                            sp.dma_start(kst[:, i % 4, 0:128], pg[:, 0, 0:128]).then_inc(page_in[i % 4], 16)
                            sp.dma_start(kst[:, i % 4, 128:512], pg[:, 0, 320:704]).then_inc(page_in[i % 4], 16)
                            sp.dma_start(V[:, b1_, i, 0, :].rearrange("p a c -> p (a c)"), pg[:, 0, 128:256]).then_inc(v_in, 16)
                            sp.dma_start(V[:, b1_, i, 1, :].rearrange("p a c -> p (a c)"), pg[:, 0, 704:832]).then_inc(v_in, 16)
                        sw = state_win[l1, bass.ds(s, 1), :, :].rearrange("a b (t p) c -> p (a b t) c", t=4)
                        sp.wait_ge(pg_p.sem, pg_p.before(r, "T win"))
                        sp.dma_start(kws[:, :, :], sw[:, :, 0:128]).then_inc(win_in, 16)
                        sp.dma_start(Vw[:, b1_, :, :].rearrange("p a t c -> p (a t) c"), sw[:, :, 128:256]).then_inc(v_in, 16)
                    sp.wait_ge(dc_p.sem, dc_p(l * 2, "h 1")) if g else sp.wait_ge(cp_p.sem, cp_p(l, "h 1"))
                    send_w1(0)
                    sp.wait_ge(dc_p.sem, dc_p(l * 2 + g, "h 0"))
                    send_w1(1)
                for name in STREAM[len(SLABS):]:
                    send(name)
            sp.wait_ge(y_out, 32)

        @block.gpsimd
        def _(pool):
            nc.gpsimd.memset(w1[:, :, :], 0.0)
            nc.gpsimd.memset(w2[:, :, :], 0.0)
            nc.gpsimd.memset(QF[:, :, :], 0.0)
            nc.gpsimd.memset(QC[:, :, :], 0.0)
            pool.drain().then_inc(init_done, 1)
            with pool.Fori(0, DEPTH) as l:
                l1 = bass.ds(l, 1)
                one = lambda ap: ap.rearrange("a t c -> (a t) c")
                pool.wait_ge(rows_a.sem, rows_a(l, "rows"))
                for t in range(2):
                    pool.dma_start(one(p_rows[l1, 0, t * 128:t * 128 + 128, :]), row[:, t, :]).then_inc(rows_out, 16)
                    pool.dma_start(one(p_win[l1, 0, t * 128:t * 128 + 128, :]), wrow[:, t, :]).then_inc(rows_out, 16)
                pool.dma_start(one(s_rows[l1, :, 0, :]), row[0:NS, 2, :]).then_inc(rows_out, 16)
                pool.dma_start(one(s_win[l1, :, WIN - 1, :]), wrow[0:NS, 2, :]).then_inc(rows_out, 16)
                pool.dma_start(s_win[l1, :, 0:WIN - 1, :].rearrange("a s w c -> (a s) w c"),
                               state_win[l1, :, 1:WIN, :].rearrange("a s w c -> (a s) w c")).then_inc(win_out, 16)
                pool.wait_ge(hg_a.sem, hg_a(l, "sfin"))
                holds(pool)
                pool.dma_start(p_hgrn[l1, 0].rearrange("a h k v -> k (a h) v"), cb[:, :, 0:128]).then_inc(hg_out, 16)
                pool.wait_ge(hg_v.sem, hg_v(l, "sn 3"))
                pool.dma_start(s_hgrn[l1].rearrange("a s h k v -> k (a s) h v"), S[:, :, :, :]).then_inc(hg_out, 16)
            pool.wait_ge(rows_out, DEPTH * 96)
            pool.wait_ge(win_out, DEPTH * 16)
            pool.wait_ge(hg_out, DEPTH * 32)
            pool.wait_ge(x_ready, DEPTH + 1)
            pool.dma_start(y_prompt[0].rearrange("(t p) d -> p t d", t=2), xp[:, :, :]).then_inc(y_out, 16)
            pool.dma_start(y_sample.rearrange("s o d -> s (o d)"), xs[:, :]).then_inc(y_out, 16)
            pool.wait_ge(y_out, 32)

        def is_T(job):
            return job[0] != "V"

        @block.tensor
        def _(pe):
            mm = nc.tensor.matmul
            pe.wait_ge(consts_in, 16)
            pe.wait_ge(init_done, 2)
            for steps in (skey_p, pg_p):
                pe.sem_inc(steps.sem, steps.n)
            with pe.Fori(0, DEPTH) as l:
                pe.wait_ge(small_in, l * 160 + 160)
                pe.wait_ge(x_ready, l + 1)
                holds(pe)
                nc.tensor.transpose(ps[0:HD, 7, 0:7], gains_row[0:7, :], ident[0:7, 0:7])
                for kv in range(2):
                    last = nc.tensor.transpose(ps[0:HD, 7, 8 + CB * kv:8 + CB * (kv + 1)], pe_row[:, kv, :], ident[0:CB, 0:CB])
                last.then_inc(norm_p.sem, norm_p.mark("small"))
                pe.wait_ge(norm_v.sem, norm_v(l, "small"))
                xpk = xp[:, :, :].rearrange("p t (c k) -> p t k c", k=KD)
                xsk = xs[:, :].rearrange("p (c k) -> p k c", k=KD)
                for k in range(KD):
                    mm(ps[:, k, 0:128], xpk[:, 0, k, :], T1[:, 0, 0:128], start=True, stop=True)
                    mm(ps[:, k, 128:256], xpk[:, 1, k, :], T1[:, 1, 0:128], start=True, stop=True)
                    mm(ps[:, k, 256:264], xsk[:, k, :], T1[0:NS, 2, 0:NS], start=True, stop=True)\
                        .then_inc(norm_p.sem, norm_p.mark(f"xT {k}"))
                pe.wait_ge(norm_v.sem, norm_v(l, "hT 7"))

                def project(name):
                    slot, use, dmas = SLOT_AT[name]
                    v = slab_view(name)
                    pe.wait_ge(slab_in[slot], (l * SLOT_DMAS[slot] + dmas) * 16)
                    jobs = SLAB_OF[name][2]
                    for j, job in enumerate(jobs):
                        n = JOB_AT[name, j]
                        pe.wait_ge(proj_free, l * NJOB + (n + 1))
                        if is_T(job):
                            for k in range(KD):
                                last = mm(ps[0:job[3], n % 2, 0:LT], v[:, k, job[2]:job[2] + job[3]], hT[:, k, :], start=(k == 0), stop=(k == KD - 1))
                            last.then_inc(proj_ready, 1)
                        else:
                            o, width = job[2], job[3]
                            for t in range(2):
                                for k in range(KD):
                                    last = mm(ps[:, n % 2, t * 256:t * 256 + width], hT[:, k, t * 128:t * 128 + 128],
                                              v[:, k, o:o + width], start=(k == 0), stop=(k == KD - 1))
                            last.then_inc(proj_ready, 1)
                            pe.wait_ge(proj_free, l * NJOB + (n + 2))
                            for k in range(KD):
                                last = mm(ps[0:NS, (n + 1) % 2, 0:width], hT[:, k, seq_cols], v[:, k, o:o + width],
                                          start=(k == 0), stop=(k == KD - 1))
                            last.then_inc(proj_ready, 1)

                for name in FRONT:
                    if name in SLAB_OF:
                        project(name)
                        continue
                    z, n, normed, _ = GROUPS[name]
                    prev = {"k": "iq", "dq": "k", "nq": "dq"}.get(name)
                    if normed:
                        pe.wait_ge(grp_a.sem, grp_a(l, f"sq {name}"))
                        pe.wait_ge(grp_v.sem, grp_v(l, f"zr {prev}"))
                        for i in range(n):
                            last = mm(ps[:, 2 + i, 0:LT], head_ones, SQ[:, i, :], start=True, stop=True)
                        last.then_inc(grp_p.sem, grp_p.mark(f"ss {name}"))
                        pe.wait_ge(grp_v.sem, grp_v(l, f"zn {name}"))
                    else:
                        jl = max(JOB_AT[nm, j] for nm in ("iq0", "iq1") for j in range(2))
                        pe.wait_ge(proj_free, l * NJOB + (jl + 3))
                    for i in range(n):
                        last = mm(ps[:, 2 + i, 0:LT], K("rot"), Z[:, z + i, :], start=True, stop=True)
                    last.then_inc(grp_p.sem, grp_p.mark(f"rot {name}"))

                pe.wait_ge(grp_v.sem, grp_v(l, "zr nq"))
                holds(pe)
                for t in range(3):
                    n = 128 if t < 2 else NS
                    cols = slice(t * 128, t * 128 + n)
                    for z, r, o, b in ((Z_DK, 128, 0, 0), (Z_IK, HD, 128, 0), (Z_NCK, 128, 192, 0), (Z_NCV, 128, 320, 0),
                                       (Z_NSK, 128, 0, 1), (Z_NWK, 128, 128, 1)):
                        last = nc.tensor.transpose(ps[0:n, 2 + 2 * t + b, o:o + r], Z[0:r, z, cols], ident[0:r, 0:r])
                last.then_inc(rows_p.sem, rows_p.mark("rows"))

                pe.wait_ge(rows_a.sem, rows_a(l, "rows"))
                holds(pe)
                for t in range(2):
                    last = nc.tensor.transpose(ps[:, 2, t * NH:t * NH + NH], Z[0:NH, Z_IW, t * 128:t * 128 + 128], ident[0:NH, 0:NH])
                last.then_inc(pidx_p.sem, pidx_p.mark("iw"))
                for h in range(NH):
                    if h >= 2:
                        pe.wait_ge(pidx_a.sem, pidx_a(l, f"relu {h - 2}"))
                    r, j, bank = halves[h // 4], h % 4, 4 + h % 2
                    mm(ps[:, bank, 0:128], Z[r, Z_IQ + j, 0:128], Z[r, Z_IK, 0:128], start=True, stop=True)
                    mm(ps[:, bank, 128:384], Z[r, Z_IQ + j, 128:256], Z[r, Z_IK, 0:256], start=True, stop=True)\
                        .then_inc(pidx_p.sem, pidx_p.mark(f"dot {h}"))

                pe.wait_ge(sidx_v.sem, sidx_v(l, "iwd"))
                mm(ps[:, 3, 0:64], ones[0:NS, :], iwD.rearrange("p s h -> p (s h)"), start=True, stop=True)\
                    .then_inc(sidx_p.sem, sidx_p.mark("iwb"))
                pe.wait_ge(sidx_a.sem, sidx_a(l, "iwb"))
                holds(pe)
                mm(ps[0:NS, 3, 0:64], Z[0:HD, Z_IK, seq_cols], QF[0:HD, 0, :], start=True, stop=True)\
                    .then_inc(sidx_p.sem, sidx_p.mark("new"))
                pe.wait_ge(sidx_a.sem, sidx_a(l, "new"))
                pe.wait_ge(pidx_a.sem, pidx_a(l, f"relu {NH - 1}"))
                holds(pe)
                with pe.Fori(0, NS // 2) as s2:
                    r = l * (NS // 2) + s2
                    for u in range(2):
                        pe.wait_ge(ik_in[u], (r + 1) * NPG * 16)
                        holds(pe)
                        for i in range(NPG):
                            last = nc.tensor.transpose(ps[0:HD, 2 + 2 * u + i // 4, (i % 4) * 128:(i % 4) * 128 + 128], ikst[:, u, i, :], ident)
                        last.then_inc(skey_p.sem, skey_p.mark(f"T {u}"))
                    for u in range(2):
                        pe.wait_ge(skey_a.sem, skey_a(r, f"T {u}"))
                        pe.wait_ge(skey_v.sem, skey_v.before(r, f"sum {u}"))
                        for i in range(NPG):
                            cols = bass.ds((s2 * 2 + u) * NH, NH)
                            last = mm(ps[:, 6 + u, i * NH:i * NH + NH], ikT[:, u, i * 128:i * 128 + 128], QF[0:HD, 0, cols],
                                      start=True, stop=True)
                        last.then_inc(skey_p.sem, skey_p.mark(f"dot {u}"))
                pe.wait_ge(skey_v.sem, skey_v(l * (NS // 2) + (NS // 2 - 1), "sum 1"))
                for i in range(NPG):
                    last = nc.tensor.transpose(ps[0:NS, 2 + i // 4, (i % 4) * 128:(i % 4) * 128 + 128], idxT[:, i, :], ident)
                last.then_inc(sidx_p.sem, sidx_p.mark("flat"))
                for name in BACK:
                    project(name)

                Zq = Z[:, Z_HQ:Z_HQ + 4, :]
                pe.wait_ge(hg_v.sem, hg_v(l, "f"))
                pe.wait_ge(sidx_a.sem, sidx_a(l, "flat"))
                for t in range(2):
                    for h in range(4):
                        last = mm(ps[:, 2 + t, h * 128:h * 128 + 128], kT[:, h, t * 128:t * 128 + 128], Zq[:, h, t * 128:t * 128 + 128], start=True, stop=True)
                last.then_inc(hg_p.sem, hg_p.mark("a diag"))
                for i in range(8):
                    pe.wait_ge(hg_v.sem, hg_v(l, f"m {i}"))
                    b = 4 if i % 2 == 0 else 2
                    m = M_[:, i % 2, :].rearrange("p (h t) -> p h t", h=4)
                    if i < 7:
                        pe.wait_ge(hg_v.sem, hg_v(l, f"a {i - 2}" if i >= 2 else "a diag"))
                        for t in range(2):
                            for h in range(4):
                                x = m[:, h, t * 128:t * 128 + 128]
                                last = mm(ps[:, b + t, h * 128:h * 128 + 128], x, x, start=True, stop=True)
                    else:
                        for h in range(4):
                            last = mm(ps[:, 6, h * 128:h * 128 + 128], m[:, h, 0:128], m[:, h, 128:256], start=True, stop=True)
                    last.then_inc(hg_p.sem, hg_p.mark(f"a {i}"))
                pe.wait_ge(hg_v.sem, hg_v(l, "a 6"))
                pe.wait_ge(hg_a.sem, hg_a(l, "far"))
                pe.wait_ge(proj_free, (l + 1) * NJOB + 2)
                for h in range(4):
                    c = slice(h * 128, h * 128 + 128)
                    mm(ps[:, 0, c], HV[:, 0, c], AT[:, 0, h, :], start=True, stop=True)
                    mm(ps[:, 1, c], HV[:, 0, c], AT[:, 2, h, :], start=True, stop=False)
                    last = mm(ps[:, 1, c], HV[:, 1, c], AT[:, 1, h, :], start=False, stop=True)
                last.then_inc(hg_p.sem, hg_p.mark("o"))
                pe.wait_ge(hg_v.sem, hg_v(l, "m 8"))
                kf = M_[:, 0, :].rearrange("p (h t) -> p h t", h=4)
                for t in range(2):
                    for h in range(4):
                        last = nc.tensor.transpose(ps[:, 2 + t, h * 128:h * 128 + 128], kf[:, h, t * 128:t * 128 + 128], ident)
                last.then_inc(hg_p.sem, hg_p.mark("kfT"))
                pe.wait_ge(hg_a.sem, hg_a(l, "kfT"))
                kft = M_[:, 1, :].rearrange("p (t c) -> p t c", t=2)
                for h in range(4):
                    c = slice(h * 128, h * 128 + 128)
                    mm(ps[:, 4, c], kft[:, 0, c], HV[:, 0, c], start=True, stop=False)
                    last = mm(ps[:, 4, c], kft[:, 1, c], HV[:, 1, c], start=False, stop=True)
                last.then_inc(hg_p.sem, hg_p.mark("sfin"))
                for h in range(4):
                    last = nc.tensor.transpose(ps[0:NS, 5, h * 128:h * 128 + 128], kT[:, h, seq_cols], ident)
                last.then_inc(hg_p.sem, hg_p.mark("kd"))
                pe.wait_ge(hg_a.sem, hg_a(l, "kd"))
                for h in range(4):
                    pe.wait_ge(hg_v.sem, hg_v(l, f"vd {h}"))
                    for i in range(2):
                        last = mm(ps[:, 6 + i, :], HK[:, h * 128:h * 128 + 128], VD[:, 4 * i:4 * i + 4, :], start=True, stop=True)
                    last.then_inc(hg_p.sem, hg_p.mark(f"kv {h}"))
                pe.wait_ge(hg_v.sem, hg_v(l, "sn 3"))
                for h in range(4):
                    for s in range(NS):
                        last = mm(ps[:, 2, h * NS + s:h * NS + s + 1], S[:, s, h, :], Zq[:, h, LP + s:LP + s + 1], start=True, stop=True)
                last.then_inc(hg_p.sem, hg_p.mark("od"))
                pe.wait_ge(hg_a.sem, hg_a(l, "sq"))
                for h in range(4):
                    last = mm(ps[:, 3 + h, 0:LT], ones, HSQ[:, h, :], start=True, stop=True)
                last.then_inc(hg_p.sem, hg_p.mark("ss"))

                def scores(u):
                    a, zq, zk = attn[u // 2]
                    r, b = halves[u % 2], 3 * (u % 2)
                    for j in range(4):
                        mm(ps[:, b, j * 128:j * 128 + 128], Z[r, zq + j, 0:128], Z[r, zk, 0:128], start=True, stop=True)
                        last = mm(ps[:, b + 1 + j // 2, (j % 2) * 256:(j % 2) * 256 + 256], Z[r, zq + j, 128:256], Z[r, zk, 0:256], start=True, stop=True)
                    last.then_inc(at_p.sem, at_p.mark(f"s {u}"))

                pe.wait_ge(hg_a.sem, hg_a(l, "rs"))
                scores(0)
                for u in range(6):
                    if u < 5:
                        if u >= 1:
                            pe.wait_ge(at_a.sem, at_a(l, f"pt {u - 1}"))
                        scores(u + 1)
                    b = 3 * (u % 2)
                    pe.wait_ge(at_v.sem, at_v(l, f"n {u}"))
                    x0 = SX[:, u % 2, 0:512].rearrange("p (j s) -> p j s", j=4)
                    x1 = SX[:, u % 2, 512:1536].rearrange("p (j s) -> p j s", j=4)
                    for j in range(4):
                        c = slice(j * 128, j * 128 + 128)
                        nc.tensor.transpose(ps[:, b, c], x0[:, j, :], ident)
                        nc.tensor.transpose(ps[:, b + 1, c], x1[:, j, 0:128], ident)
                        last = nc.tensor.transpose(ps[:, b + 2, c], x1[:, j, 128:256], ident)
                    last.then_inc(at_p.sem, at_p.mark(f"t {u}"))
                    pe.wait_ge(at_a.sem, at_a(l, f"pt {u}"))
                    if u:
                        pe.wait_ge(at_v.sem, at_v(l, f"ev {u - 1}"))
                    a = u // 2
                    mm(ps[:, 6, :], values(a, 0), PT[:, 0, :], start=True, stop=True)
                    mm(ps[:, 7, :], values(a, 0), PT[:, 1, :], start=True, stop=False)
                    mm(ps[:, 7, :], values(a, 1), PT[:, 2, :], start=False, stop=True).then_inc(at_p.sem, at_p.mark(f"o {u}"))

                pe.wait_ge(at_v.sem, at_v(l, "ev 5"))
                zc = (Z_NCK, Z_NCV)
                for kv in range(2):
                    pe.wait_ge(w1_in, (l * 6 + kv + 1) * 32)
                    if kv:
                        pe.wait_ge(cp_v.sem, cp_v(l, "h 0"))
                    for i in range(CB):
                        mm(ps[:, 0, 0:1], w1[:, i, :], peT[:, kv, i:i + 1], start=(i == 0), stop=(i == CB - 1))
                    for i in range(CB):
                        last = mm(ps[:, 1, 0:NCP], w1[:, i, :], Z[:, zc[kv], i:i + CS * (NCP - 1) + 1:CS], start=(i == 0), stop=(i == CB - 1))
                    last.then_inc(cp_p.sem, cp_p.mark(f"h {kv}"))
                    pe.wait_ge(cp_v.sem, cp_v(l, f"hid {kv}"))
                    if kv == 0:
                        last = mm(ps[:, 2, 0:NCP], w2[:, 0, :], hidP[:, 0, 0:NCP], start=True, stop=True)
                    else:
                        last = mm(ps[0:NCP, 3, 0:128], hidP[:, 1, 0:NCP], w2[:, 1, :], start=True, stop=True)
                    last.then_inc(cp_p.sem, cp_p.mark(f"out {kv}"))
                pe.wait_ge(cp_a.sem, cp_a(l, "out 1"))
                for t in range(2):
                    for h in range(NH):
                        r, j = halves[h // 4], h % 4
                        last = mm(ps[:, 4 + 2 * (h // 4) + t, j * NCP:j * NCP + NCP], Z[r, Z_NQ + j, t * 128:t * 128 + 128], ckP[r, 0:NCP], start=True, stop=True)
                last.then_inc(cp_p.sem, cp_p.mark("s"))
                pe.wait_ge(cp_v.sem, cp_v(l, "n"))
                for t in range(2):
                    for h in range(NH):
                        last = nc.tensor.transpose(ps[0:NCP, h // 2, (h % 2) * 256 + t * 128:(h % 2) * 256 + t * 128 + 128], SC[:, t, h, :], ident)
                last.then_inc(cp_p.sem, cp_p.mark("t"))
                pe.wait_ge(cp_a.sem, cp_a(l, "t"))
                for g in range(2):
                    for t in range(2):
                        last = mm(ps[:, 4 + 2 * g + t, :], cvP[0:NCP, :], PTC[0:NCP, 4 * g:4 * g + 4, t * 128:t * 128 + 128], start=True, stop=True)
                last.then_inc(cp_p.sem, cp_p.mark("o"))
                pe.wait_ge(gsel_in, l * 16 + 16)
                pe.wait_ge(cp_v.sem, cp_v(l, "nb"))
                for i in range(12):
                    if i >= 4:
                        pe.wait_ge(cp_v.sem, cp_v(l, f"gb {i - 4}"))
                    mm(ps[:, i % 4, 0:LT], gsel[0:24, i, :], nbs[0:24, :], start=True, stop=True).then_inc(cp_p.sem, cp_p.mark(f"gb {i}"))

                pe.wait_ge(cp_v.sem, cp_v(l, "prompt done"))
                for g in range(2):
                    lg = l * 2 + g
                    if g:
                        pe.wait_ge(dc_v.sem, dc_v(lg - 1, "ev"))
                    holds(pe)
                    with pe.Fori(0, GB) as b:
                        r = lg * GB + b
                        qcols = bass.ds((b + g * GB) * NH, NH)

                        def page_scores(i):
                            pe.wait_ge(pg_a.sem, pg_a(r, f"T {i}"))
                            for a in range(2):
                                last = mm(ps[:, 2, (a * NPG + i) * NH:(a * NPG + i) * NH + NH], KT[:, i % 2, a, :], QF[:, 1 + a, qcols],
                                          start=True, stop=True)
                            last.then_inc(pg_p.sem, pg_p.mark(f"s {i}"))

                        for i in range(NPG):
                            pe.wait_ge(page_in[i % 4], (r * 2 + (i // 4 + 1)) * 32)
                            if i >= 2:
                                pe.wait_ge(pg_a.sem, pg_a(r, f"T {i - 2}"))
                                pe.wait_ge(pg_v.sem, pg_v(r, f"T {i - 2}"))
                            else:
                                pe.wait_ge(pg_v.sem, pg_v.before(r, "s"))
                            for c in range(4):
                                b = (0, 4, 4, 0)[c] + i % 2
                                o = (0, 0, 128, 128)[c]
                                last = nc.tensor.transpose(ps[:, b, o:o + 128], kst[:, i % 4, c * 128:c * 128 + 128], ident)
                            last.then_inc(pg_p.sem, pg_p.mark(f"T {i}"))
                            if i:
                                page_scores(i - 1)
                        page_scores(NPG - 1)
                        pe.wait_ge(win_in, r * 16 + 16)
                        for t in range(4):
                            last = nc.tensor.transpose(ps[:, 3, t * 128:t * 128 + 128], kws[:, t, :], ident)
                        last.then_inc(pg_p.sem, pg_p.mark("T win"))
                        pe.wait_ge(pg_a.sem, pg_a(r, "T win"))
                        for t in range(4):
                            last = mm(ps[:, 2, (16 + t) * NH:(16 + t) * NH + NH], KTw[:, t, :], QF[:, 2, qcols], start=True, stop=True)
                        last.then_inc(pg_p.sem, pg_p.mark("s win"))
                    pe.wait_ge(pg_v.sem, pg_v(lg * GB + (GB - 1), "s"))
                    for kv in range(2):
                        pe.wait_ge(w1_in, (l * 6 + 2 + 2 * g + kv + 1) * 32)
                        for i in range(CB):
                            last = mm(ps[:, 4, 0:GB * 63].rearrange("p (b n) -> p b n", b=GB), w1[:, i, :],
                                      cT[:, kv, :, i:i + CS * (NCS - 1) + 1:CS], start=(i == 0), stop=(i == CB - 1))
                        last.then_inc(dc_p.sem, dc_p.mark(f"h {kv}"))
                        pe.wait_ge(dc_v.sem, dc_v(lg, f"hid {kv}"))
                        if kv == 0:
                            mm(ps[:, 5, 0:GB * 63], w2[:, 0, :], hid[:, 0], start=True, stop=True).then_inc(dc_p.sem, dc_p.mark("ck"))
                        else:
                            for b in range(GB):
                                last = mm(ps[0:63, 6, b * 128:b * 128 + 128], hid[:, 1, b, :], w2[:, 1, :], start=True, stop=True)
                            last.then_inc(dc_p.sem, dc_p.mark("cv"))
                    pe.wait_ge(dc_a.sem, dc_a(lg, "cv"))
                    for b in range(GB):
                        last = mm(ps[0:ROWS, 0, 0:63], QC[:, g, b * ROWS:(b + 1) * ROWS], ckd[:, b, :], start=(b == 0), stop=(b == GB - 1))
                    last.then_inc(dc_p.sem, dc_p.mark("s cmp"))
                    pe.wait_ge(dc_v.sem, dc_v(lg, "n cmp"))
                    holds(pe)
                    nc.tensor.transpose(ps[0:63, 1, 0:ROWS], sc4[0:ROWS, 0:63], ident[0:ROWS, 0:ROWS]).then_inc(dc_p.sem, dc_p.mark("t cmp"))
                    pe.wait_ge(dc_a.sem, dc_a(lg, "t cmp"))
                    holds(pe)
                    mm(ps[0:ROWS, 0, 0:NSEL], PTc[0:63, :], K("cover", 63), start=True, stop=True).then_inc(dc_p.sem, dc_p.mark("imp"))
                    pe.wait_ge(dc_v.sem, dc_v(lg, "imp"))
                    holds(pe)
                    mm(ps[0:ROWS, 0, 0:NSEL], K("group_sum", ROWS), dr[0:ROWS, 0:NSEL], start=True, stop=True)\
                        .then_inc(dc_p.sem, dc_p.mark("group imp"))
                    for b in range(GB):
                        last = mm(ps[0:ROWS, 7, 0:128], PTcx[0:63, b, :], CV[0:63, b, :], start=(b == 0), stop=(b == GB - 1))
                    pe.wait_ge(dc_v.sem, dc_v(lg, "drop"))
                    for i in range(20):
                        last = nc.tensor.transpose(ps[0:ROWS, 2 + i // 4, (i % 4) * 128:(i % 4) * 128 + 128], scT[:, i, :, :].rearrange("p b h -> p (b h)"), ident)
                    last.then_inc(dc_p.sem, dc_p.mark("flat"))
                    ex = K("expand", NS)[:, g * ROWS:(g + 1) * ROWS]
                    for a in range(3):
                        mm(ps[0:ROWS, 7, 128 + a * NS:128 + a * NS + NS], QF[:, 1 + min(a, 1), g * ROWS:(g + 1) * ROWS], kn[:, a, :], start=True, stop=True)
                    mm(ps[0:ROWS, 7, 160:161], ex, work[:, PAST:PAST + 1], start=True, stop=True)
                    for i in range(2):
                        last = mm(ps[0:ROWS, i, :], ex, work[:, i * 512:i * 512 + 512], start=True, stop=True)
                    last.then_inc(dc_p.sem, dc_p.mark("new"))
                    pe.wait_ge(dc_v.sem, dc_v(lg, "new p"))
                    holds(pe)
                    for i in range(20):
                        src = SS[0:ROWS, i // 8, (i % 8) * 128:(i % 8) * 128 + 128]
                        nc.tensor.transpose(ps[:, 2 + i // 10, (i % 10) * ROWS:(i % 10) * ROWS + ROWS], src, ident[0:ROWS, 0:ROWS])
                    for a in range(3):
                        last = nc.tensor.transpose(ps[0:NS, 4, a * ROWS:(a + 1) * ROWS], dr[0:ROWS, 24 + a * NS:24 + (a + 1) * NS], ident[0:ROWS, 0:ROWS])
                    last.then_inc(dc_p.sem, dc_p.mark("PT"))
                    pe.wait_ge(dc_a.sem, dc_a(lg, "PT"))
                    pe.wait_ge(v_in, (lg + 1) * GB * 17 * 16)
                    holds(pe)
                    for a, bank in ((0, 0), (1, 1), (2, 5)):
                        mm(ps[0:ROWS, bank, 0:128], pn8[0:NS, a, :], vn[:, a, :], start=True, stop=False)
                    for b in range(GB):
                        pe.wait_ge(dx_v.sem, dx_v(lg, f"x {b}"))
                        end = b == GB - 1
                        for i in range(NPG):
                            mm(ps[0:ROWS, 0, 0:128], PTx[:, i, :], V[:, b, i, 0, :], start=False, stop=end and i == NPG - 1)
                            mm(ps[0:ROWS, 1, 0:128], PTx[:, NPG + i, :], V[:, b, i, 1, :], start=False, stop=end and i == NPG - 1)
                        for i in range(4):
                            last = mm(ps[0:ROWS, 5, 0:128], PTx[:, 2 * NPG + i, :], Vw[:, b, i, :], start=False, stop=end and i == 3)
                        last.then_inc(dx_p.sem, dx_p.mark(f"x {b}"))
                    pe.wait_ge(dc_v.sem, dc_v(lg, "scaled"))
                    holds(pe)
                    for a in range(4):
                        last = nc.tensor.transpose(ps[:, 6, a * ROWS:(a + 1) * ROWS], SS[0:ROWS, 0, a * 128:a * 128 + 128], ident[0:ROWS, 0:ROWS])
                    last.then_inc(dc_p.sem, dc_p.mark("oT"))

                pe.wait_ge(dc_v.sem, dc_v(l * 2 + 1, "ev"))

                def arrived(name):
                    slot, use, dmas = SLOT_AT[name]
                    pe.wait_ge(slab_in[slot], (l * SLOT_DMAS[slot] + dmas) * 16)
                    return slab_view(name)

                for a in range(3):
                    for i in range(2):
                        v = arrived(f"g{a}{i}")
                        for jj in range(2):
                            j = 2 * i + jj
                            if a and j == 0:
                                pe.wait_ge(ga_v.sem, ga_v(l, f"b {a - 1} {KD - 1}"))
                            for k in range(KD):
                                last = mm(ps[:, j, 0:LT], v[:, k, jj * 128:jj * 128 + 128], hT[:, k, :], start=(k == 0), stop=(k == KD - 1))
                            last.then_inc(ga_p.sem, ga_p.mark(f"g {a} {j}"))
                    for i in range(4):
                        v = arrived(f"m{a}{i}")
                        for jj in range(2):
                            d = 2 * i + jj
                            bank = 4 + d % 2
                            if d >= 2:
                                pe.wait_ge(ga_a.sem, ga_a(l, f"m {a} {d - 2}"))
                            for k in range(KD):
                                last = mm(ps[:, bank, 0:LT], v[:, k, jj * 128:jj * 128 + 128], hT[:, k, :], start=(k == 0), stop=(k == KD - 1))
                            last.then_inc(ga_p.sem, ga_p.mark(f"m {a} {d}"))
                    pe.wait_ge(ga_v.sem, ga_v(l, f"y {a} 3"))
                    for i in range(2):
                        v = arrived(f"b{a}{i}")
                        for dd in range(4):
                            d = 4 * i + dd
                            if d >= 4:
                                pe.wait_ge(ga_v.sem, ga_v(l, f"b {a} {d - 4}"))
                            for j in range(4):
                                last = mm(ps[:, d % 4, 0:LT], v[:, j, dd * 128:dd * 128 + 128], Y[:, a, j, :], start=(j == 0), stop=(j == 3))
                            last.then_inc(ga_p.sem, ga_p.mark(f"b {a} {d}"))
                pe.wait_ge(ga_v.sem, ga_v(l, "b 2 7"))
                for i in range(4):
                    v = arrived(f"o{i}")
                    for t in range(3):
                        n = 3 * i + t
                        if n >= 4:
                            pe.wait_ge(ga_v.sem, ga_v(l, f"o {n - 4}"))
                        m = 128 if t < 2 else NS
                        for k in range(KD):
                            last = mm(ps[0:m, n % 4, 0:256], mT[:, k, t * 128:t * 128 + m], v[:, k, :], start=(k == 0), stop=(k == KD - 1))
                        last.then_inc(ga_p.sem, ga_p.mark(f"o {n}"))

        IW_SCALE = NH ** -0.5 * HD ** -0.5
        taken = float(np.float32(TAKEN))

        @block.scalar
        def _(act):
            A = nc.scalar.activation

            def copy(out, in_, scale=1.0):
                return A(out, in_, ACT.Copy, scale=scale)

            act.wait_ge(lb_v, 1)
            A(lbl[:, 0:DEPTH, :], lbl[:, 0:DEPTH, :], ACT.Exp).then_inc(lb_a, 1)
            act.sem_inc(proj_free, 2)
            act.wait_ge(x_in, 64)
            with act.Fori(0, DEPTH) as l:
                act.wait_ge(x_ready, l + 1)
                squares = at(18208, 3, D)
                for t in range(2):
                    A(squares[:, t, :], xp[:, t, :], ACT.Square, accum_out=sa[:, t:t + 1])
                A(squares[0:NS, 2, :], xs[:, :], ACT.Square, accum_out=sa[0:NS, 2:3])
                act.drain()
                for p, c in ((128, slice(0, 2)), (NS, slice(2, 3))):
                    A(sa[0:p, c], sa[0:p, c], ACT.Ln, scale=1.0 / D, bias=epsb[0:p, :])
                act.drain()
                for p, c in ((128, slice(0, 2)), (NS, slice(2, 3))):
                    last = A(sa[0:p, c], sa[0:p, c], ACT.Exp, scale=-0.5)
                act.drain().then_inc(norm_a.sem, norm_a.mark("rstd"))

                def evacuate(name):
                    for j, job in enumerate(SLAB_OF[name][2]):
                        n = JOB_AT[name, j]
                        act.wait_ge(proj_ready, l * NJOB + (n + 1))
                        if is_T(job):
                            copy(Z[0:job[3], job[1], :], ps[0:job[3], n % 2, 0:LT]).then_inc(proj_free, 1)
                            continue
                        dst = {"rows": row, "win": wrow, "hv": HV}[job[1]]
                        w, o = job[3], job[4]
                        copy(dst[:, 0:2, o:o + w], ps[:, n % 2, :].rearrange("p (t c) -> p t c", t=2)[:, :, 0:w]).then_inc(proj_free, 1)
                        act.wait_ge(proj_ready, l * NJOB + (n + 2))
                        copy(dst[0:NS, 2, o:o + w], ps[0:NS, (n + 1) % 2, 0:w]).then_inc(proj_free, 1)

                for name in FRONT:
                    if name in SLAB_OF:
                        evacuate(name)
                        continue
                    z, n, normed, _ = GROUPS[name]
                    if not normed:
                        continue
                    prev = {"dq": "k", "nq": "dq"}.get(name)
                    if prev:
                        act.wait_ge(grp_v.sem, grp_v(l, f"zn {prev}"))
                        A(sa[:, 63:64], sa[:, 0:1], ACT.Copy)
                    act.drain()
                    A(SQ[:, 0:n, :], Z[:, z:z + n, :], ACT.Square).then_inc(grp_a.sem, grp_a.mark(f"sq {name}"))
                    act.wait_ge(grp_p.sem, grp_p(l, f"ss {name}"))
                    A(SQ[:, 0:n, :], ps[:, 2:2 + n, 0:LT], ACT.Ln, scale=1.0 / HD, bias=epsb[:, :])
                    act.drain()
                    A(SQ[:, 0:n, :], SQ[:, 0:n, :], ACT.Exp, scale=-0.5).then_inc(grp_a.sem, grp_a.mark(f"rs {name}"))

                act.wait_ge(rows_p.sem, rows_p(l, "rows"))
                for t in range(3):
                    n = 128 if t < 2 else NS
                    b = 2 + 2 * t
                    copy(row[0:n, t, 0:128], ps[0:n, b, 0:128])
                    copy(row[0:n, t, 256:576], ps[0:n, b, 128:448])
                    copy(row[0:n, t, 576:704], ps[0:n, b + 1, 0:128])
                    copy(wrow[0:n, t, 0:128], ps[0:n, b + 1, 128:256])
                act.drain().then_inc(rows_a.sem, rows_a.mark("rows"))

                act.wait_ge(pidx_p.sem, pidx_p(l, "iw"))
                copy(iwP, ps[:, 2, 0:2 * NH].rearrange("p (t h) -> p t h", t=2), IW_SCALE).then_inc(pidx_a.sem, pidx_a.mark("iw"))
                for h in range(NH):
                    act.wait_ge(pidx_p.sem, pidx_p(l, f"dot {h}"))
                    if h >= 2:
                        act.wait_ge(pidx_v.sem, pidx_v(l, f"acc {h - 2}"))
                    A(RL[:, h % 2, :], ps[:, 4 + h % 2, 0:384], ACT.Relu).then_inc(pidx_a.sem, pidx_a.mark(f"relu {h}"))

                act.wait_ge(sidx_p.sem, sidx_p(l, "iwb"))
                copy(iwB[:, :], ps[:, 3, 0:64], IW_SCALE).then_inc(sidx_a.sem, sidx_a.mark("iwb"))
                act.wait_ge(sidx_p.sem, sidx_p(l, "new"))
                A(i2, ps[0:NS, 3, 0:64], ACT.Relu).then_inc(sidx_a.sem, sidx_a.mark("new"))
                with act.Fori(0, NS // 2) as s2:
                    r = l * (NS // 2) + s2
                    for u in range(2):
                        act.wait_ge(skey_p.sem, skey_p(r, f"T {u}"))
                        copy(ikT[:, u, :].rearrange("p (b c) -> p b c", b=2), ps[0:HD, 2 + 2 * u:4 + 2 * u, :]).then_inc(skey_a.sem, skey_a.mark(f"T {u}"))
                    for u in range(2):
                        act.wait_ge(skey_p.sem, skey_p(r, f"dot {u}"))
                        A(RD[:, u, :], ps[:, 6 + u, 0:64], ACT.Relu).then_inc(skey_a.sem, skey_a.mark(f"relu {u}"))
                act.wait_ge(sidx_p.sem, sidx_p(l, "flat"))
                copy(work[:, 0:PAST].rearrange("p (b c) -> p b c", b=2), ps[0:NS, 2:4, :]).then_inc(sidx_a.sem, sidx_a.mark("flat"))
                for name in BACK:
                    evacuate(name)

                act.drain()
                A(fT, Z[:, Z_HF:Z_HF + 4, :], ACT.Exp, scale=-1.0)
                A(kT, Z[:, Z_HF:Z_HF + 4, :], ACT.Exp)
                A(HSQ, Z[:, Z_HQ:Z_HQ + 4, :], ACT.Exp, scale=-1.0)
                act.drain().then_inc(hg_a.sem, hg_a.mark("exp"))
                act.wait_ge(hg_v.sem, hg_v(l, "f"))
                A(D_, fT[:, :, 0:LP], ACT.Ln).then_inc(hg_a.sem, hg_a.mark("ln"))
                DE = (E_, D_)
                for i in range(9):
                    act.wait_ge(hg_v.sem, hg_v(l, f"d {i}"))
                    A(DE[i % 2], DE[i % 2], ACT.Exp).then_inc(hg_a.sem, hg_a.mark(f"e {i}"))
                act.wait_ge(hg_p.sem, hg_p(l, "a 7"))
                copy(AT[:, 2, :, :], ps[:, 6, :].rearrange("p (h t) -> p h t", h=4)).then_inc(hg_a.sem, hg_a.mark("far"))
                act.wait_ge(hg_p.sem, hg_p(l, "o"))
                for t in range(2):
                    last = copy(Y[:, 0, :, t * 128:t * 128 + 128], ps[:, t, :].rearrange("p (h t) -> p h t", h=4))
                last.then_inc(hg_a.sem, hg_a.mark("o"))
                act.wait_ge(hg_p.sem, hg_p(l, "kfT"))
                copy(M_[:, 1, :].rearrange("p (b c) -> p b c", b=2), ps[:, 2:4, :]).then_inc(hg_a.sem, hg_a.mark("kfT"))
                act.wait_ge(hg_p.sem, hg_p(l, "sfin"))
                copy(cb[:, :, 0:128], ps[:, 4, :].rearrange("p (h v) -> p h v", h=4)).then_inc(hg_a.sem, hg_a.mark("sfin"))
                act.wait_ge(hg_p.sem, hg_p(l, "kd"))
                copy(HK, ps[0:NS, 5, :]).then_inc(hg_a.sem, hg_a.mark("kd"))
                act.wait_ge(hg_p.sem, hg_p(l, "od"))
                copy(Y[:, 0, :, seq_cols], ps[:, 2, 0:4 * NS].rearrange("p (h s) -> p h s", h=4)).then_inc(hg_a.sem, hg_a.mark("od"))
                act.drain()
                A(HSQ, Y[:, 0, :, :], ACT.Square).then_inc(hg_a.sem, hg_a.mark("sq"))
                act.wait_ge(hg_p.sem, hg_p(l, "ss"))
                A(HSQ, ps[:, 3:7, 0:LT], ACT.Ln, scale=1.0 / 128, bias=epsb[:, :])
                act.drain()
                A(HSQ, HSQ, ACT.Exp, scale=-0.5).then_inc(hg_a.sem, hg_a.mark("rs"))

                def exps(u):
                    act.wait_ge(at_v.sem, at_v(l, f"s {u}"))
                    x0 = SX[:, u % 2, 0:512].rearrange("p (j s) -> p j s", j=4)
                    x1 = SX[:, u % 2, 512:1536].rearrange("p (j s) -> p j s", j=4)
                    c = 8 * (u % 2)
                    for j in range(4):
                        A(x0[:, j, :], x0[:, j, :], ACT.Exp, bias=st[:, c + j:c + j + 1], accum_out=sa[:, c + j:c + j + 1])
                        A(x1[:, j, :], x1[:, j, :], ACT.Exp, bias=st[:, c + 4 + j:c + 5 + j], accum_out=sa[:, c + 4 + j:c + 5 + j])
                    act.drain().then_inc(at_a.sem, at_a.mark(f"e {u}"))

                exps(0)
                for u in range(6):
                    if u < 5:
                        exps(u + 1)
                    act.wait_ge(at_p.sem, at_p(l, f"t {u}"))
                    if u:
                        act.wait_ge(at_p.sem, at_p(l, f"o {u - 1}"))
                    else:
                        act.wait_ge(hg_out, l * 32 + 32)
                    copy(PT, ps[:, 3 * (u % 2):3 * (u % 2) + 3, :]).then_inc(at_a.sem, at_a.mark(f"pt {u}"))

                for kv in range(2):
                    act.wait_ge(cp_v.sem, cp_v(l, f"h {kv}"))
                    A(ehP[:, 0:NCP], hidP[:, kv, 0:NCP], ACT.Exp, scale=-1.0).then_inc(cp_a.sem, cp_a.mark(f"e {kv}"))
                    act.wait_ge(cp_p.sem, cp_p(l, f"out {kv}"))
                    if kv == 0:
                        last = copy(ckP[:, 0:NCP], ps[:, 2, 0:NCP])
                    else:
                        last = copy(cvP[0:NCP, :], ps[0:NCP, 3, 0:128])
                    last.then_inc(cp_a.sem, cp_a.mark(f"out {kv}"))
                act.wait_ge(cp_v.sem, cp_v(l, "s"))
                A(SC, SC, ACT.Exp).then_inc(cp_a.sem, cp_a.mark("e"))
                act.wait_ge(cp_p.sem, cp_p(l, "t"))
                copy(PTC[0:NCP].rearrange("p h t -> p (h t)").rearrange("p (b c) -> p b c", b=4), ps[0:NCP, 0:4, :]).then_inc(cp_a.sem, cp_a.mark("t"))
                A(nbs[0:24, :], Z[0:24, Z_NBG, :], ACT.Exp, scale=-1.0).then_inc(cp_a.sem, cp_a.mark("nb"))

                for g in range(2):
                    lg = l * 2 + g
                    with act.Fori(0, GB) as b:
                        r = lg * GB + b
                        for i in range(NPG):
                            act.wait_ge(pg_p.sem, pg_p(r, f"T {i}"))
                            copy(KT[:, i % 2], ps[:, i % 2, 0:256].rearrange("p (c x) -> p c x", c=2)).then_inc(pg_a.sem, pg_a.mark(f"T {i}"))
                        act.wait_ge(pg_p.sem, pg_p(r, "T win"))
                        copy(KTw, ps[:, 3, :].rearrange("p (t x) -> p t x", t=4)).then_inc(pg_a.sem, pg_a.mark("T win"))
                    for kv in range(2):
                        act.wait_ge(dc_v.sem, dc_v(lg, f"h {kv}"))
                        A(eh, hid[:, kv], ACT.Exp, scale=-1.0).then_inc(dc_a.sem, dc_a.mark(f"e {kv}"))
                        act.wait_ge(dc_p.sem, dc_p(lg, "cv" if kv else "ck"))
                        if kv == 0:
                            copy(ckd.rearrange("p b n -> p (b n)"), ps[:, 5, 0:GB * 63]).then_inc(dc_a.sem, dc_a.mark("ck"))
                        else:
                            copy(CV[0:63].rearrange("p b n -> p (b n)"), ps[0:63, 6, :]).then_inc(dc_a.sem, dc_a.mark("cv"))
                    act.wait_ge(dc_v.sem, dc_v(lg, "s cmp"))
                    A(sc4[0:ROWS, 0:63], sc4[0:ROWS, 0:63], ACT.Exp, bias=st[0:ROWS, 40:41], accum_out=sa[0:ROWS, 40:41])
                    act.drain().then_inc(dc_a.sem, dc_a.mark("e cmp"))
                    act.wait_ge(dc_p.sem, dc_p(lg, "t cmp"))
                    copy(PTc[0:63, :], ps[0:63, 1, 0:ROWS]).then_inc(dc_a.sem, dc_a.mark("t cmp"))
                    act.wait_ge(dc_p.sem, dc_p(lg, "flat"))
                    for a in range(2):
                        copy(SS[0:ROWS, a, 0:PAST].rearrange("p (b c) -> p b c", b=2), ps[0:ROWS, 2 + 2 * a:4 + 2 * a, :], SCALE)
                    copy(SS[0:ROWS, 2, 0:WIN], ps[0:ROWS, 6, :], SCALE)
                    act.drain().then_inc(dc_a.sem, dc_a.mark("flat"))
                    act.wait_ge(dc_v.sem, dc_v(lg, "masked"))
                    for a, n in enumerate((PAST + 1, PAST + 1, WIN + 1)):
                        A(SS[0:ROWS, a, 0:n], SS[0:ROWS, a, 0:n], ACT.Exp, bias=st[0:ROWS, 43 + a:44 + a], accum_out=sa[0:ROWS, 43 + a:44 + a])
                    act.drain().then_inc(dc_a.sem, dc_a.mark("e"))
                    act.wait_ge(dc_p.sem, dc_p(lg, "PT"))
                    copy(PTd.rearrange("p (b t) r -> p b (t r)", b=2), ps[:, 2:4, 0:10 * ROWS])
                    copy(pn8.rearrange("p a r -> p (a r)"), ps[0:NS, 4, 0:3 * ROWS])
                    act.drain().then_inc(dc_a.sem, dc_a.mark("PT"))

                for a in range(3):
                    for j in range(4):
                        act.wait_ge(ga_p.sem, ga_p(l, f"g {a} {j}"))
                        A(gz[:, j, :], ps[:, j, 0:LT], ACT.Sigmoid).then_inc(ga_a.sem, ga_a.mark(f"g {a} {j}"))
                    for d in range(KD):
                        act.wait_ge(ga_p.sem, ga_p(l, f"m {a} {d}"))
                        A(sig[:, d, :], ps[:, 4 + d % 2, 0:LT], ACT.Sigmoid).then_inc(ga_a.sem, ga_a.mark(f"m {a} {d}"))

        @block.vector
        def _(ve):
            TT, TS, STT, TC = nc.vector.tensor_tensor, nc.vector.tensor_scalar, nc.vector.scalar_tensor_tensor, nc.vector.tensor_copy
            RED = nc.vector.tensor_reduce

            def rest():
                ve.memset(spare[:, :], 0.0)

            ve.memset(epsb[:, :], EPS)
            ve.memset(lbl[:, DEPTH, :], 0.0)
            ve.memset(lb[:, :], 0.0)
            ve.memset(lb1[:, :], 1.0)
            ve.memset(sa[:, :], 0.0)
            ve.drain().then_inc(init_done, 1)
            ve.wait_ge(x_in, 64)
            ve.wait_ge(consts_in, 16)
            RED(st[:, 0:4], lbl[:, 0:DEPTH, :].rearrange("p l h -> p h l"), AXX, ALU.max)
            ve.drain()
            TT(lbl[:, 0:DEPTH, :], lbl[:, 0:DEPTH, :], st[:, 0:4].unsqueeze(1).to_broadcast([128, DEPTH, 4]), ALU.subtract).then_inc(lb_v, 1)
            ve.wait_ge(lb_a, 1)
            RED(st[:, 0:4], lbl[:, 0:DEPTH, :].rearrange("p l h -> p h l"), AXX, ALU.add)
            ve.drain()
            nc.vector.reciprocal(st[:, 4:8], st[:, 0:4])
            ve.drain()
            TT(lbl[:, 0:DEPTH, :], lbl[:, 0:DEPTH, :], st[:, 4:8].unsqueeze(1).to_broadcast([128, DEPTH, 4]), ALU.mult)
            for steps in (skey_v, pg_v):
                ve.sem_inc(steps.sem, steps.n)
            ve.drain().then_inc(x_ready, 1)
            with ve.Fori(0, DEPTH) as l:
                ve.wait_ge(norm_a.sem, norm_a(l, "rstd"))
                for t in range(2):
                    TS(T1[:, t, 0:128], ident, sa[:, t:t + 1], None, ALU.mult)
                TS(T1[0:NS, 2, 0:NS], ident[0:NS, 0:NS], sa[0:NS, 2:3], None, ALU.mult).then_inc(norm_v.sem, norm_v.mark("diag"))
                ve.wait_ge(norm_p.sem, norm_p(l, "small"))
                for h in halves:
                    TC(gains[h, :], ps[0:HD, 7, 0:7])
                    TC(peT[h, :, :].rearrange("p a s -> p (a s)"), ps[0:HD, 7, 8:8 + 2 * CB])
                ve.drain().then_inc(norm_v.sem, norm_v.mark("small"))
                for k in range(KD):
                    ve.wait_ge(norm_p.sem, norm_p(l, f"xT {k}"))
                    TS(hT[:, k, :], ps[:, k, 0:LT], gx[:, k:k + 1], None, ALU.mult).then_inc(norm_v.sem, norm_v.mark(f"hT {k}"))

                for name in FRONT:
                    if name in SLAB_OF:
                        continue
                    z, n, normed, cols = GROUPS[name]
                    x = Z[:, z:z + n, :]
                    if normed:
                        ve.wait_ge(grp_a.sem, grp_a(l, f"rs {name}"))
                        for i in range(n):
                            c = cols[i]
                            last = STT(Z[:, z + i, :], Z[:, z + i, :], gains[:, c:c + 1], SQ[:, i, :], ALU.mult, ALU.mult)
                        ve.drain().then_inc(grp_v.sem, grp_v.mark(f"zn {name}"))
                    ve.wait_ge(grp_p.sem, grp_p(l, f"rot {name}"))
                    TT(T1[:, 0:n, :], x, cosb(n), ALU.mult)
                    TT(T2[:, 0:n, :], ps[:, 2:2 + n, 0:LT], sinb(n), ALU.mult)
                    ve.drain()
                    TT(x, T1[:, 0:n, :], T2[:, 0:n, :], ALU.add).then_inc(grp_v.sem, grp_v.mark(f"zr {name}"))

                ve.wait_ge(rows_a.sem, rows_a(l, "rows"))
                rest()
                ve.drain()
                qf = QF[:, :, :].rearrange("p a (s h) -> p a s h", s=NS)
                for g, h in enumerate(halves):
                    hh = slice(4 * g, 4 * g + 4)
                    TC(qf[0:HD, 0, :, hh], Z[h, Z_IQ:Z_IQ + 4, seq_cols].rearrange("p j s -> p s j"))
                    TC(qf[h, 1, :, hh], Z[h, Z_DQ:Z_DQ + 4, seq_cols].rearrange("p j s -> p s j"))
                    TC(qf[h, 2, :, hh], Z[h, Z_NQ:Z_NQ + 4, seq_cols].rearrange("p j s -> p s j"))
                for i, z in enumerate((Z_DK, Z_NSK, Z_NWK)):
                    TC(kn[:, i, :], Z[:, z, seq_cols])
                    TC(vn[:, i, :], values(i, 2)[0:NS])
                ve.drain()
                for g in range(2):
                    TC(QC[:, g, :].rearrange("p (b x) -> p b x", b=GB)[:, :, 0:NH], qf[:, 2, g * GB:g * GB + GB, :])
                ve.drain().then_inc(sidx_v.sem, sidx_v.mark("qf"))
                i8 = ident[0:NS, 0:NH]
                TT(iwD, Z[0:NH, Z_IW, seq_cols].unsqueeze(2).to_broadcast([NH, NS, NH]), i8.unsqueeze(1).to_broadcast([NH, NS, NH]), ALU.mult)\
                    .then_inc(sidx_v.sem, sidx_v.mark("iwd"))

                for h in range(NH):
                    ve.wait_ge(pidx_a.sem, pidx_a(l, f"relu {h}"))
                    for t, c in enumerate((slice(0, 128), slice(128, 384))):
                        STT(acc[:, c], RL[:, h % 2, c], iwP[:, t, h:h + 1], causal[:, c] if h == 0 else acc[:, c], ALU.mult, ALU.add)
                    ve.drain().then_inc(pidx_v.sem, pidx_v.mark(f"acc {h}"))
                for c in (slice(0, 128), slice(128, 384)):
                    for _ in range(TOPK_P // 8):
                        nc.vector.max(top8[:, :], acc[:, c])
                        ve.drain()
                        nc.vector.match_replace(acc[:, c], top8[:, :], acc[:, c], taken)
                        ve.drain()
                TS(msk, acc, taken, NEG, ALU.not_equal, ALU.mult)
                ve.drain()
                TT(msk, msk, causal, ALU.add)
                ve.drain().then_inc(pidx_v.sem, pidx_v.mark("mask"))

                ve.wait_ge(sidx_a.sem, sidx_a(l, "new"))
                TT(i2, i2, iwB[0:NS, :], ALU.mult)
                ve.drain()
                TT(i2, i2, K("seq8", NS), ALU.mult)
                ve.drain()
                RED(work[:, PAST:PAST + 1], i2, AXX, ALU.add)
                ve.drain().then_inc(sidx_v.sem, sidx_v.mark("new"))
                with ve.Fori(0, NS // 2) as s2:
                    r = l * (NS // 2) + s2
                    for u in range(2):
                        s = s2 * 2 + u
                        ve.wait_ge(skey_a.sem, skey_a(r, f"relu {u}"))
                        rd = RD[:, u, :].rearrange("p (i h) -> p i h", i=NPG)
                        TT(rd, rd, iwB[:, bass.ds(s * NH, NH)].unsqueeze(1).to_broadcast([128, NPG, NH]), ALU.mult)
                        ve.drain()
                        RED(idxT[:, :, bass.ds(s, 1)], rd, AXX, ALU.add).then_inc(skey_v.sem, skey_v.mark(f"sum {u}"))
                ve.wait_ge(sidx_a.sem, sidx_a(l, "flat"))
                rest()
                for _ in range(TOPK_S // 8):
                    nc.vector.max(top8[0:NS, :], work[:, 0:PAST + 1])
                    ve.drain()
                    nc.vector.match_replace(work[:, 0:PAST + 1], top8[0:NS, :], work[:, 0:PAST + 1], taken)
                    ve.drain()
                TS(work[:, 0:PAST + 1], work[:, 0:PAST + 1], taken, None, ALU.not_equal)
                ve.drain().then_inc(sidx_v.sem, sidx_v.mark("left out"))

                ve.wait_ge(hg_a.sem, hg_a(l, "exp"))
                for x in (fT, kT, HSQ):
                    TS(x, x, 1.0, None, ALU.add)
                ve.drain()
                for x in (fT, kT, HSQ):
                    nc.vector.reciprocal(x, x)
                ve.drain()
                TT(Z[:, Z_HQ:Z_HQ + 4, :], Z[:, Z_HQ:Z_HQ + 4, :], HSQ, ALU.mult)
                for h in range(4):
                    TS(kT[:, h, :], kT[:, h, :], lb1[:, h:h + 1], None, ALU.mult)
                    TS(fT[:, h, :], fT[:, h, :], lb1[:, h:h + 1], lb[:, h:h + 1], ALU.mult, ALU.add)
                ve.memset(AT[:, 0:2, :, :], 0.0)
                ve.drain().then_inc(hg_v.sem, hg_v.mark("f"))
                ve.wait_ge(hg_a.sem, hg_a(l, "ln"))
                for h in range(4):
                    nc.vector.tensor_tensor_scan(cb[:, h, :], K("chunk_reset"), D_[:, h, :], 0.0, ALU.mult, ALU.add)
                ve.drain()
                DE = (E_, D_)
                q, k = Z[:, Z_HQ:Z_HQ + 4, 0:LP], kT[:, :, 0:LP]
                tot = cb.rearrange("p h (c t) -> p h c t", c=4)[:, :, :, 63]

                def decays(i):
                    d = DE[i % 2]
                    if i <= 6:
                        w = 1 << i
                        b = cb.rearrange("p h t -> p (h t)").rearrange("p (n z w) -> p n z w", z=2, w=w)
                        o = d.rearrange("p h t -> p (h t)").rearrange("p (n z w) -> p n z w", z=2, w=w)
                        mid = b[:, :, 0, w - 1:w].to_broadcast([128, 1024 // (2 * w), w])
                        TT(o[:, :, 0, :], mid, b[:, :, 0, :], ALU.subtract)
                        if i < 6:
                            TT(o[:, :, 1, :], b[:, :, 1, :], mid, ALU.subtract)
                        else:
                            TC(o[:, :, 1, :], b[:, :, 1, :])
                    else:
                        b = cb.rearrange("p h (c t) -> p h c t", c=4)
                        o = d.rearrange("p h (c t) -> p h c t", c=4)
                        T = lambda c: tot[:, :, c:c + 1].to_broadcast([128, 4, 64])
                        m = 4 if i == 8 else 2
                        TT(o[:, :, 0:m, :], tot[:, :, 0:m].unsqueeze(3).to_broadcast([128, 4, m, 64]), b[:, :, 0:m, :], ALU.subtract)
                        if i == 7:
                            TC(o[:, :, 2, :], b[:, :, 2, :])
                            TT(o[:, :, 3, :], b[:, :, 3, :], T(2), ALU.add)
                            ve.drain()
                            TT(o[:, :, 0, :], o[:, :, 0, :], T(1), ALU.add)
                        else:
                            TT(st[:, 0:4], tot[:, :, 3], tot[:, :, 2], ALU.add)
                            ve.drain()
                            TT(st[:, 4:8], st[:, 0:4], tot[:, :, 1], ALU.add)
                            TT(o[:, :, 2, :], o[:, :, 2, :], T(3), ALU.add)
                            TT(o[:, :, 1, :], o[:, :, 1, :], st[:, 0:4].unsqueeze(2).to_broadcast([128, 4, 64]), ALU.add)
                            ve.drain()
                            TT(o[:, :, 0, :], o[:, :, 0, :], st[:, 4:8].unsqueeze(2).to_broadcast([128, 4, 64]), ALU.add)
                    ve.drain().then_inc(hg_v.sem, hg_v.mark(f"d {i}"))

                def merge(i, banks, level):
                    ve.wait_ge(hg_p.sem, hg_p(l, "a diag" if i < 0 else f"a {i}"))
                    rest()
                    for t in range(2):
                        nc.vector.copy_predicated(AT[:, t, :, :], lvl[:, level:level + 1, :].to_broadcast([128, 4, 128]),
                                                  ps[:, banks + t, :].rearrange("p (h t) -> p h t", h=4))
                    ve.drain().then_inc(hg_v.sem, hg_v.mark("a diag" if i < 0 else f"a {i}"))

                decays(0)
                merge(-1, 2, 7)
                for i in range(9):
                    if i < 8:
                        decays(i + 1)
                    ve.wait_ge(hg_a.sem, hg_a(l, f"e {i}"))
                    m = M_[:, i % 2, :].rearrange("p (h t) -> p h t", h=4)
                    if i == 8:
                        TT(m, DE[i % 2], k, ALU.mult)
                    else:
                        w = 1 << i
                        cut = lambda x, z: x.rearrange("p h (n z w) -> p h n z w", z=2, w=w)[:, :, :, z, :]
                        TT(cut(m, 0), cut(DE[i % 2], 0), cut(k, 0), ALU.mult)
                        TT(cut(m, 1), cut(DE[i % 2], 1), cut(q, 1), ALU.mult)
                    ve.drain().then_inc(hg_v.sem, hg_v.mark(f"m {i}"))
                    if 1 <= i <= 7:
                        merge(i - 1, 4 if (i - 1) % 2 == 0 else 2, i - 1)
                ve.wait_ge(S_in, l * 64 + 64)
                for h in range(4):
                    TT(VD, HV[0:NS, 2:3, h * 128:h * 128 + 128].to_broadcast([NS, NS, 128]),
                       ident[0:NS, 0:NS].unsqueeze(2).to_broadcast([NS, NS, 128]), ALU.mult).then_inc(hg_v.sem, hg_v.mark(f"vd {h}"))
                    ve.wait_ge(hg_p.sem, hg_p(l, f"kv {h}"))
                    for s in range(NS):
                        STT(S[:, s, h, :], S[:, s, h, :], fT[:, h, LP + s:LP + s + 1], ps[:, 6 + s // 4, (s % 4) * 128:(s % 4) * 128 + 128],
                            ALU.mult, ALU.add)
                    ve.drain().then_inc(hg_v.sem, hg_v.mark(f"sn {h}"))
                ve.wait_ge(hg_a.sem, hg_a(l, "rs"))
                for h in range(4):
                    STT(Y[:, 0, h, :], Y[:, 0, h, :], gho[:, h:h + 1], HSQ[:, h, :], ALU.mult, ALU.mult)
                ve.drain().then_inc(hg_v.sem, hg_v.mark("done"))

                def masked(u):
                    if u >= 2:
                        ve.wait_ge(at_p.sem, at_p(l, f"t {u - 2}"))
                    ve.wait_ge(at_p.sem, at_p(l, f"s {u}"))
                    b, c = 3 * (u % 2), 8 * (u % 2)
                    m = msk if u < 2 else causal
                    x0 = SX[:, u % 2, 0:512].rearrange("p (j s) -> p j s", j=4)
                    x1 = SX[:, u % 2, 512:1536].rearrange("p (j s) -> p j s", j=4)
                    STT(x0, ps[:, b, :].rearrange("p (j s) -> p j s", j=4), SCALE, m[:, 0:128].unsqueeze(1).to_broadcast([128, 4, 128]), ALU.mult, ALU.add)
                    STT(x1, ps[:, b + 1:b + 3, :].rearrange("p c (j s) -> p (c j) s", j=2), SCALE, m[:, 128:384].unsqueeze(1).to_broadcast([128, 4, 256]), ALU.mult, ALU.add)
                    ve.drain()
                    RED(st[:, c:c + 4], x0, AXX, ALU.max, negate=True)
                    RED(st[:, c + 4:c + 8], x1, AXX, ALU.max, negate=True)
                    ve.drain().then_inc(at_v.sem, at_v.mark(f"s {u}"))

                def out_of_psum(u):
                    ve.wait_ge(at_p.sem, at_p(l, f"o {u}"))
                    r, a = halves[u % 2], u // 2
                    for t in range(2):
                        dst = (Y[:, 1] if a == 0 else OC[:, a])[r, :, t * 128:t * 128 + 128]
                        last = TC(dst, ps[r, 6 + t, :].rearrange("p (j t) -> p j t", j=4))
                    last.then_inc(at_v.sem, at_v.mark(f"ev {u}"))

                masked(0)
                for u in range(6):
                    if u < 5:
                        masked(u + 1)
                    ve.wait_ge(at_a.sem, at_a(l, f"e {u}"))
                    c = 8 * (u % 2)
                    x0 = SX[:, u % 2, 0:512].rearrange("p (j s) -> p j s", j=4)
                    x1 = SX[:, u % 2, 512:1536].rearrange("p (j s) -> p j s", j=4)
                    nc.vector.reciprocal(st[:, 16:24], sa[:, c:c + 8])
                    ve.drain()
                    TT(x0, x0, st[:, 16:20].unsqueeze(2).to_broadcast([128, 4, 128]), ALU.mult)
                    TT(x1, x1, st[:, 20:24].unsqueeze(2).to_broadcast([128, 4, 256]), ALU.mult)
                    ve.drain().then_inc(at_v.sem, at_v.mark(f"n {u}"))
                    if u:
                        out_of_psum(u - 1)
                out_of_psum(5)

                for kv in range(2):
                    ve.wait_ge(cp_p.sem, cp_p(l, f"h {kv}"))
                    TT(hbias[:, kv:kv + 1], ps[:, 0, 0:1], b1[:, kv:kv + 1], ALU.add)
                    ve.drain()
                    TS(hidP[:, kv, 0:NCP], ps[:, 1, 0:NCP], hbias[:, kv:kv + 1], None, ALU.add).then_inc(cp_v.sem, cp_v.mark(f"h {kv}"))
                    ve.wait_ge(cp_a.sem, cp_a(l, f"e {kv}"))
                    TS(ehP[:, 0:NCP], ehP[:, 0:NCP], 1.0, None, ALU.add)
                    ve.drain()
                    nc.vector.reciprocal(ehP[:, 0:NCP], ehP[:, 0:NCP])
                    ve.drain()
                    TT(hidP[:, kv, 0:NCP], hidP[:, kv, 0:NCP], ehP[:, 0:NCP], ALU.mult).then_inc(cp_v.sem, cp_v.mark(f"hid {kv}"))
                ve.wait_ge(cp_p.sem, cp_p(l, "s"))
                for t in range(2):
                    for g in range(2):
                        STT(SC[:, t, 4 * g:4 * g + 4], ps[:, 4 + 2 * g + t, 0:4 * NCP].rearrange("p (h c) -> p h c", h=4), SCALE,
                            K("cmp_add")[:, t * NCP:(t + 1) * NCP].unsqueeze(1).to_broadcast([128, 4, NCP]), ALU.mult, ALU.add)
                ve.drain()
                RED(st[:, 0:16].rearrange("p (t h) -> p t h", t=2), SC, AXX, ALU.max)
                ve.drain()
                scb = SC.rearrange("p t h c -> p (t h) c")
                TT(scb, scb, st[:, 0:16].unsqueeze(2).to_broadcast([128, 16, NCP]), ALU.subtract).then_inc(cp_v.sem, cp_v.mark("s"))
                ve.wait_ge(cp_a.sem, cp_a(l, "e"))
                RED(st[:, 16:32].rearrange("p (t h) -> p t h", t=2), SC, AXX, ALU.add)
                ve.drain()
                nc.vector.reciprocal(st[:, 32:48], st[:, 16:32])
                ve.drain()
                TT(scb, scb, st[:, 32:48].unsqueeze(2).to_broadcast([128, 16, NCP]), ALU.mult)
                ve.drain()
                TT(SC, SC, K("cmp_mul").rearrange("p (t c) -> p t c", t=2).unsqueeze(2).to_broadcast([128, 2, NH, NCP]), ALU.mult)\
                    .then_inc(cp_v.sem, cp_v.mark("n"))
                ve.wait_ge(cp_a.sem, cp_a(l, "nb"))
                TS(nbs[0:24, :], nbs[0:24, :], 1.0, None, ALU.add)
                ve.drain()
                nc.vector.reciprocal(nbs[0:24, :], nbs[0:24, :]).then_inc(cp_v.sem, cp_v.mark("nb"))
                ve.wait_ge(cp_p.sem, cp_p(l, "o"))
                for g, r in enumerate(halves):
                    for t in range(2):
                        TC(OC[r, 0, :, t * 128:t * 128 + 128], ps[r, 4 + 2 * g + t, :].rearrange("p (j t) -> p j t", j=4))
                ve.drain().then_inc(cp_v.sem, cp_v.mark("ev"))
                for i in range(12):
                    c, j = i // 4, i % 4
                    ve.wait_ge(cp_p.sem, cp_p(l, f"gb {i}"))
                    if c == 0:
                        TT(Y[:, 2, j, 0:LP], ps[:, i % 4, 0:LP], OC[:, 0, j, :], ALU.mult)
                    else:
                        TT(SX[:, 0, 0:LP], ps[:, i % 4, 0:LP], OC[:, c, j, :], ALU.mult)
                        ve.drain()
                        TT(Y[:, 2, j, 0:LP], Y[:, 2, j, 0:LP], SX[:, 0, 0:LP], ALU.add)
                    TC(gbs[:, i, :], ps[:, i % 4, seq_cols])
                    ve.drain().then_inc(cp_v.sem, cp_v.mark(f"gb {i}"))
                ve.drain().then_inc(cp_v.sem, cp_v.mark("prompt done"))

                for g in range(2):
                    lg = l * 2 + g
                    with ve.Fori(0, GB) as b:
                        r = lg * GB + b
                        b1_ = bass.ds(b, 1)
                        for i in range(NPG):
                            ve.wait_ge(pg_p.sem, pg_p(r, f"T {i}"))
                            TS(cT[:, :, b1_, i * 128:i * 128 + 128].rearrange("p k b c -> p k (b c)"),
                               ps[:, 4 + i % 2, 0:256].rearrange("p (k c) -> p k c", k=2), 1.0, None, ALU.mult).then_inc(pg_v.sem, pg_v.mark(f"T {i}"))
                        ve.wait_ge(pg_p.sem, pg_p(r, "s win"))
                        TS(scT[:, :, b1_, :].rearrange("p i b h -> p i (b h)"), ps[:, 2, 0:160].rearrange("p (i h) -> p i h", h=NH), 1.0, None,
                           ALU.mult).then_inc(pg_v.sem, pg_v.mark("s"))
                    for kv in range(2):
                        ve.wait_ge(dc_p.sem, dc_p(lg, f"h {kv}"))
                        TS(hid[:, kv].rearrange("p b n -> p (b n)"), ps[:, 4, 0:GB * 63], hbias[:, kv:kv + 1], None, ALU.add).then_inc(dc_v.sem, dc_v.mark(f"h {kv}"))
                        ve.wait_ge(dc_a.sem, dc_a(lg, f"e {kv}"))
                        TS(eh, eh, 1.0, None, ALU.add)
                        ve.drain()
                        nc.vector.reciprocal(eh, eh)
                        ve.drain()
                        TT(hid[:, kv], hid[:, kv], eh, ALU.mult).then_inc(dc_v.sem, dc_v.mark(f"hid {kv}"))
                    ve.wait_ge(dc_p.sem, dc_p(lg, "s cmp"))
                    c4, c40 = sc4[0:ROWS, 0:63], st[0:ROWS, 40:41]
                    TS(c4, ps[0:ROWS, 0, 0:63], SCALE, None, ALU.mult)
                    ve.drain()
                    RED(c40, c4, AXX, ALU.max, negate=True).then_inc(dc_v.sem, dc_v.mark("s cmp"))
                    ve.wait_ge(dc_a.sem, dc_a(lg, "e cmp"))
                    nc.vector.reciprocal(c40, sa[0:ROWS, 40:41])
                    ve.drain()
                    TS(c4, c4, c40, None, ALU.mult).then_inc(dc_v.sem, dc_v.mark("n cmp"))
                    ve.wait_ge(dc_a.sem, dc_a(lg, "t cmp"))
                    TT(PTcx[0:63], PTc[0:63].unsqueeze(1).to_broadcast([63, GB, ROWS]), K("own4", 63).rearrange("p (b r) -> p b r", b=GB), ALU.mult)\
                        .then_inc(dc_v.sem, dc_v.mark("ptx cmp"))
                    ve.wait_ge(dc_p.sem, dc_p(lg, "imp"))
                    d17 = dr[0:ROWS, 0:NSEL]
                    TC(d17, ps[0:ROWS, 0, 0:NSEL]).then_inc(dc_v.sem, dc_v.mark("imp"))
                    ve.wait_ge(dc_p.sem, dc_p(lg, "group imp"))
                    TT(d17, ps[0:ROWS, 0, 0:NSEL], K("not_forced", ROWS), ALU.mult)
                    ve.drain()
                    TT(d17, d17, K("forced", ROWS), ALU.add)
                    ve.drain()
                    RED(st[0:ROWS, 41:42], d17, AXX, ALU.min)
                    ve.drain()
                    STT(d17, d17, st[0:ROWS, 41:42], K("order", ROWS), ALU.is_equal, ALU.mult)
                    ve.drain()
                    RED(st[0:ROWS, 42:43], d17, AXX, ALU.max)
                    ve.drain()
                    TS(d17, d17, st[0:ROWS, 42:43], None, ALU.is_equal).then_inc(dc_v.sem, dc_v.mark("drop"))
                    ve.wait_ge(dc_a.sem, dc_a(lg, "flat"))
                    ve.wait_ge(dc_p.sem, dc_p(lg, "new"))
                    own = K("own_s", ROWS)[:, g * NS:(g + 1) * NS]
                    ncol = (PAST, PAST, WIN)
                    dn = dr[0:ROWS, 24:48].rearrange("p (a s) -> p a s", a=3)
                    TT(dn, ps[0:ROWS, 7, 128:152].rearrange("p (a s) -> p a s", a=3), own.unsqueeze(1).to_broadcast([ROWS, 3, NS]), ALU.mult)
                    for i in range(2):
                        x = SS[0:ROWS, 0, i * 512:i * 512 + 512]
                        STT(x, ps[0:ROWS, i, :], NEG, x, ALU.mult, ALU.add)
                    x = SS[0:ROWS, 1, 0:PAST].rearrange("p (j c) -> p j c", c=SB)
                    STT(x, dr[0:ROWS, 0:NSEL - 1].unsqueeze(2).to_broadcast([ROWS, NSEL - 1, SB]), NEG, x, ALU.mult, ALU.add)
                    ve.memset(SS[0:ROWS, 2, 0:1], NEG)
                    ve.drain()
                    RED(st[0:ROWS, 49:52], dn, AXX, ALU.add)
                    ve.drain()
                    for a in range(3):
                        TS(SS[0:ROWS, a, ncol[a]:ncol[a] + 1], st[0:ROWS, 49 + a:50 + a], SCALE, None, ALU.mult)
                    ve.drain()
                    x = SS[0:ROWS, 0, PAST:PAST + 1]
                    STT(x, ps[0:ROWS, 7, 160:161], NEG, x, ALU.mult, ALU.add)
                    ve.drain()
                    for a in range(3):
                        RED(st[0:ROWS, 43 + a:44 + a], SS[0:ROWS, a, 0:ncol[a] + 1], AXX, ALU.max, negate=True)
                    ve.drain().then_inc(dc_v.sem, dc_v.mark("masked"))
                    ve.wait_ge(dc_a.sem, dc_a(lg, "e"))
                    nc.vector.reciprocal(st[0:ROWS, 46:49], sa[0:ROWS, 43:46])
                    for a in range(3):
                        TS(dn[:, a, :], own, SS[0:ROWS, a, ncol[a]:ncol[a] + 1], None, ALU.mult)
                    ve.drain().then_inc(dc_v.sem, dc_v.mark("new p"))
                    ve.wait_ge(dc_a.sem, dc_a(lg, "PT"))
                    for b in range(GB):
                        if b:
                            ve.wait_ge(dx_p.sem, dx_p(lg, f"x {b - 1}"))
                        TT(PTx, PTd, K("own4")[:, b * ROWS:(b + 1) * ROWS].unsqueeze(1).to_broadcast([128, 20, ROWS]), ALU.mult)\
                            .then_inc(dx_v.sem, dx_v.mark(f"x {b}"))
                    ve.wait_ge(dx_p.sem, dx_p(lg, "x 3"))
                    for a, bank in enumerate((0, 1, 5)):
                        TS(SS[0:ROWS, 0, a * 128:a * 128 + 128], ps[0:ROWS, bank, 0:128], st[0:ROWS, 46 + a:47 + a], None, ALU.mult)
                    TC(SS[0:ROWS, 0, 384:512], ps[0:ROWS, 7, 0:128])
                    ve.drain().then_inc(dc_v.sem, dc_v.mark("scaled"))
                    ve.wait_ge(dc_p.sem, dc_p(lg, "oT"))
                    for gg, r in enumerate(halves):
                        o = ps[:, 6, 0:4 * ROWS].rearrange("p (a b g j) -> p a g j b", a=4, b=GB, g=2)[r, :, gg]
                        sc = slice(LP + g * GB, LP + g * GB + GB)
                        TC(Y[r, 1, :, sc], o[:, 0])
                        tmp = st[r, 0:48].rearrange("p (c j b) -> p c j b", c=3, j=4)
                        for c, a in enumerate((3, 1, 2)):
                            TT(tmp[:, c], gbs[r, 4 * c:4 * c + 4, g * GB:g * GB + GB], o[:, a], ALU.mult)
                        ve.drain()
                        TT(tmp[:, 0], tmp[:, 0], tmp[:, 1], ALU.add)
                        ve.drain()
                        TT(Y[r, 2, :, sc], tmp[:, 0], tmp[:, 2], ALU.add)
                    ve.drain().then_inc(dc_v.sem, dc_v.mark("ev"))

                for a in range(3):
                    for j in range(4):
                        ve.wait_ge(ga_a.sem, ga_a(l, f"g {a} {j}"))
                        TT(gz[:, j, :], ps[:, j, 0:LT], gz[:, j, :], ALU.mult)
                        ve.drain()
                        TT(Y[:, a, j, :], Y[:, a, j, :], gz[:, j, :], ALU.mult).then_inc(ga_v.sem, ga_v.mark(f"y {a} {j}"))
                    for d in range(KD):
                        ve.wait_ge(ga_a.sem, ga_a(l, f"m {a} {d}"))
                        ve.wait_ge(ga_p.sem, ga_p(l, f"b {a} {d}"))
                        if a == 0:
                            TT(mT[:, d, :], ps[:, d % 4, 0:LT], sig[:, d, :], ALU.mult)
                        else:
                            TT(mtmp[:, d % 2, :], ps[:, d % 4, 0:LT], sig[:, d, :], ALU.mult)
                            ve.drain()
                            TT(mT[:, d, :], mT[:, d, :], mtmp[:, d % 2, :], ALU.add)
                        ve.drain().then_inc(ga_v.sem, ga_v.mark(f"b {a} {d}"))
                for i in range(4):
                    for t in range(3):
                        n = 3 * i + t
                        ve.wait_ge(ga_p.sem, ga_p(l, f"o {n}"))
                        m = 128 if t < 2 else NS
                        x = xp[:, t, i * 256:i * 256 + 256] if t < 2 else xs[:, i * 256:i * 256 + 256]
                        TT(x, x, ps[0:m, n % 4, 0:256], ALU.add).then_inc(ga_v.sem, ga_v.mark(f"o {n}"))
                TT(lb[:, :], lb[:, :], lbl[:, bass.ds(l + 1, 1), :].rearrange("p a h -> p (a h)"), ALU.add)
                ve.drain()
                TS(lb1[:, :], lb[:, :], -1.0, 1.0, ALU.mult, ALU.add)
                ve.drain().then_inc(x_ready, 1)

        for steps in all_steps:
            assert steps.done and steps.done % steps.n == 0, (steps.steps[0], steps.done, steps.n)


_INS = ['x_prompt', 'x_sample', 'cache_kv', 'page_table', 'state_win', 'state_hgrn', 'norm_g', 'w_in',
        'hgrn_lb_logits', 'hgrn_onorm_g', 'dsa_qk_norm_g', 'dsa_idx_k_norm_g', 'nsa_qk_norm_g', 'nsa_cmp_pe',
        'nsa_cmp_w1', 'nsa_cmp_b1', 'nsa_cmp_w2', 'w_branch', 'w_out']
_OUTS = [(1, LP, D), (NS, 1, D), (DEPTH, 1, LP, CW), (DEPTH, 1, LP, 256), (DEPTH, 1, 4, 128, 128),
         (DEPTH, NS, 1, CW), (DEPTH, NS, WIN, 256), (DEPTH, NS, 4, 128, 128)]


def kernel(**inputs):
    import numpy as _np
    import concourse.bacc as _bacc
    from concourse import mybir as _mybir
    from concourse.bass_utils import run_bass_kernel_spmd as _run

    nc = _bacc.Bacc("TRN2", target_bir_lowering=False, num_devices=1)
    given = {name: _np.ascontiguousarray(inputs[name]) for name in _INS}
    given["const"] = constants()
    given["gate_rows"] = branch_gate_rows()
    arrays, args = {}, []
    for name, a in given.items():
        arrays[f"in_{name}_dram"] = a
        args.append(nc.dram_tensor(f"in_{name}_dram", a.shape, _mybir.dt.from_np(a.dtype), kind="ExternalInput").ap())
    for i, shape in enumerate(_OUTS):
        args.append(nc.dram_tensor(f"out_{i}_dram", shape, _mybir.dt.float32, kind="ExternalOutput").ap())
    hybrid_step(nc, *args)
    r = _run(nc, [arrays], core_ids=[0])
    return tuple(r.results[0][f"out_{i}_dram"] for i in range(len(_OUTS)))
```

```python
import numpy as np
import concourse.bass as bass
from concourse import mybir
from contextlib import ExitStack

F32 = mybir.dt.float32
I32 = mybir.dt.int32
ALU = mybir.AluOpType
ACT = mybir.ActivationFunctionType
AXX = mybir.AxisListType.X

D = 1024
LP = 256
NS = 8
LT = LP + NS
DEPTH = 2
PAST = 1024
PAGE = 128
NPG = PAST // PAGE
BW = D // 2
HD = 64
NH = 8
KD = D // 128
TOPK_P, TOPK_S = 64, 256
CB, CS = 32, 16
NCP = (LP - CB) // CS + 1
NCS = (PAST - CB) // CS + 1
SB = 64
NSEL = PAST // SB + 1
WIN = 512
CW = 832
NEG, FORCE, TAKEN = -1e30, 1e9, -3e38
EPS = 1e-6
SCALE = HD ** -0.5
GB = 4
ROWS = NS * NH

C_HQ, C_HF, C_HI, C_HG = 0, 512, 1024, 1536
C_DQ, C_DK, C_IQ, C_IK, C_DG = 2048, 2560, 2816, 3328, 3400
C_NQ, C_NCK, C_NSK, C_NWK, C_NBG, C_NG, C_MA = 3912, 4424, 4680, 4936, 5192, 5216, 5728

Z_IQ, Z_DQ, Z_NQ, Z_IK, Z_DK, Z_NCK, Z_NSK, Z_NWK, Z_NCV, Z_IW, Z_NBG, Z_HF, Z_HQ = (
    0, 4, 8, 12, 13, 14, 15, 16, 17, 18, 19, 20, 24)
NZ = 28

def _pair(name, col, z, g, kind="T"):
    segs = [(col + 128 * g, 128), (col + 256 + 128 * g, 128)]
    return (name, segs, [(kind, z + 2 * g, 0, 128), (kind, z + 2 * g + 1, 128, 128)])


SLABS = [
    _pair("iq0", C_IQ, Z_IQ, 0), _pair("iq1", C_IQ, Z_IQ, 1),
    ("ikw", [(C_IK, HD), (C_IK, HD + NH)], [("T", Z_IK, 0, 128), ("T", Z_IW, 128, NH)]),
    ("dkv", [(C_DK, 256)], [("T", Z_DK, 0, 128), ("V", "rows", 128, 128, 128)]),
    ("n1", [(C_NCK, 256)], [("T", Z_NCK, 0, 128), ("T", Z_NCV, 128, 128)]),
    ("n2", [(C_NSK, 256)], [("T", Z_NSK, 0, 128), ("V", "rows", 128, 128, 704)]),
    ("n3", [(C_NWK, 256)], [("T", Z_NWK, 0, 128), ("V", "win", 128, 128, 128)]),
    ("n4", [(C_NBG, 24)], [("T", Z_NBG, 0, 24)]),
    _pair("dq0", C_DQ, Z_DQ, 0), _pair("dq1", C_DQ, Z_DQ, 1),
    _pair("nq0", C_NQ, Z_NQ, 0), _pair("nq1", C_NQ, Z_NQ, 1),
    ("hf0", [(C_HF, 256)], [("T", Z_HF, 0, 128), ("T", Z_HF + 1, 128, 128)]),
    ("hf1", [(C_HF + 256, 256)], [("T", Z_HF + 2, 0, 128), ("T", Z_HF + 3, 128, 128)]),
    ("hq0", [(C_HQ, 256)], [("T", Z_HQ, 0, 128), ("T", Z_HQ + 1, 128, 128)]),
    ("hq1", [(C_HQ + 256, 256)], [("T", Z_HQ + 2, 0, 128), ("T", Z_HQ + 3, 128, 128)]),
    ("hi0", [(C_HI, 256)], [("V", "hv", 0, 256, 0)]),
    ("hi1", [(C_HI + 256, 256)], [("V", "hv", 0, 256, 256)]),
    ("g00", [(C_HG, 256)], [("Y", 0, 0, 128), ("Y", 1, 128, 128)]),
    ("g01", [(C_HG + 256, 256)], [("Y", 2, 0, 128), ("Y", 3, 128, 128)]),
    _pair("g10", C_DG, 4, 0, "Y"), _pair("g11", C_DG, 4, 1, "Y"),
    _pair("g20", C_NG, 8, 0, "Y"), _pair("g21", C_NG, 8, 1, "Y"),
]
PAIRS = ("iq", "dq", "nq", "g1", "g2")
GROUPS = {"iq": (Z_IQ, 4, False, None), "k": (Z_IK, 5, True, [2, 1, 4, 5, 6]),
          "dq": (Z_DQ, 4, True, [0] * 4), "nq": (Z_NQ, 4, True, [3] * 4)}
FRONT = ["iq0", "iq1", "ikw", "dkv", "n1", "iq", "n2", "n3", "n4", "k", "dq0", "dq1", "nq0", "dq", "nq1", "nq"]
BACK = ["hf0", "hf1", "hq0", "hq1", "hi0", "hi1"]
GATES = ["g00", "g01", "g10", "g11", "g20", "g21"]
GATE_JOBS = [(n, j) for n in GATES for j in range(2)]
EARLY_GATES = 4

GATE_SLABS = []
for _a in range(3):
    GATE_SLABS += [(f"m{_a}{i}", "mix", _a, i) for i in range(4)]
    GATE_SLABS += [(f"b{_a}{i}", "branch", _a, i) for i in range(2)]
OUT_SLABS = [(f"o{i}", "out", 0, i) for i in range(4)]
STREAM = ([n for n in FRONT + BACK + GATES if n not in GROUPS] + [s[0] for s in GATE_SLABS] + [s[0] for s in OUT_SLABS])
NSLOT = 3
SLAB_OF = {s[0]: s for s in SLABS}


def slab_dmas(name):
    if name in SLAB_OF:
        return len(SLAB_OF[name][1])
    if name[0] == "b":
        return 1 if name[1] == "0" else 2
    return 1


SLOT_AT, SLOT_USES, SLOT_DMAS = {}, [0] * NSLOT, [0] * NSLOT
for _i, _n in enumerate(STREAM):
    _s = _i % NSLOT
    SLOT_USES[_s] += 1
    SLOT_DMAS[_s] += slab_dmas(_n)
    SLOT_AT[_n] = (_s, SLOT_USES[_s], SLOT_DMAS[_s])

JOB_AT, LAST_JOB, NJOB = {}, {}, 0
for _n in FRONT + BACK + GATES:
    if _n in SLAB_OF:
        for _j, _job in enumerate(SLAB_OF[_n][2]):
            JOB_AT[_n, _j] = NJOB
            NJOB += 2 if _job[0] == "V" else 1
        LAST_JOB[_n] = NJOB
LAST_USE = {}
for _n, _kind, _a, _i in GATE_SLABS + OUT_SLABS:
    LAST_USE[_n] = {"mix": f"m {_a} {2 * _i + 1}", "branch": f"b {_a} {4 * _i + 3}",
                    "out": f"o {3 * _i + 2}"}[_kind]

CONST = {}
_off = 0
for _name, _w in (("ident", 128), ("head_ones", 128), ("ones", 128), ("rot", 128), ("cos", LT), ("sin", LT),
                  ("levels", 8 * 128), ("causal", 384), ("cmp_add", 2 * NCP), ("cmp_mul", 2 * NCP),
                  ("chunk_reset", LP), ("seq_rows", ROWS), ("own_s", NS),
                  ("cover", NSEL), ("group_sum", ROWS), ("not_forced", NSEL), ("forced", NSEL), ("order", NSEL), ("zeros", ROWS)):
    CONST[_name] = (_off, _w)
    _off += _w
NCONST = _off


def constants():
    c = {n: np.zeros((128, w), np.float32) for n, (_, w) in CONST.items()}
    p = np.arange(128)
    c["ident"][:] = np.eye(128)
    c["head_ones"][:] = p[:, None] // HD == p[None, :] // HD
    c["ones"][:] = 1
    half = HD // 8
    for b in (0, HD):
        for i in range(half):
            c["rot"][b + half + i, b + i] = -1
            c["rot"][b + i, b + half + i] = 1
    pos = np.concatenate([np.arange(LP), np.full(NS, PAST)]).astype(np.float32)
    inv = np.float32(500000.0) ** (-np.arange(half, dtype=np.float32) / half)
    ang = (pos[None, :] * inv[:, None]).astype(np.float32).astype(np.float64)
    c["cos"][:] = 1
    for b in (0, HD):
        for r in (0, half):
            c["cos"][b + r:b + r + half] = np.cos(ang)
            c["sin"][b + r:b + r + half] = np.sin(ang)
    s, t = p[:, None], p[None, :]
    lv = c["levels"].reshape(128, 8, 128)
    for i in range(7):
        w = 1 << i
        lv[:, i] = (s // (2 * w) == t // (2 * w)) & (s % (2 * w) < w) & (t % (2 * w) >= w)
    lv[:, 7] = s == t
    q, k = p[:, None], np.arange(LP)[None, :]
    c["causal"][:, :128] = np.where(k[:, :128] <= q, 0, NEG)
    c["causal"][:, 128:] = np.where(k <= q + 128, 0, NEG)
    end = np.arange(NCP) * CS + CB - 1
    for i in range(2):
        ok = end[None, :] <= q + 128 * i
        c["cmp_add"][:, i * NCP:(i + 1) * NCP] = np.where(ok, 0, NEG)
        c["cmp_mul"][:, i * NCP:(i + 1) * NCP] = ok
    c["chunk_reset"][:] = (np.arange(LP) % 64 != 0)
    c["seq_rows"][:NS] = np.arange(NS)[:, None] == np.arange(ROWS)[None, :] // NH
    c["own_s"][:ROWS] = np.arange(ROWS)[:, None] // NH == np.arange(NS)[None, :]
    cs, ss = np.arange(NCS) * CS, np.arange(NSEL) * SB
    c["cover"][:NCS] = np.clip(np.minimum(cs[:, None] + CB, ss[None, :] + SB)
                               - np.maximum(cs[:, None], ss[None, :]), 0, None) / CB
    r = np.arange(ROWS)
    c["group_sum"][:ROWS] = r[:, None] // 4 == r[None, :] // 4
    forced = np.isin(np.arange(NSEL), (0, NSEL - 2, NSEL - 1))
    c["not_forced"][:] = ~forced
    c["forced"][:] = forced * FORCE
    c["order"][:] = np.arange(NSEL) + 1
    return np.concatenate([c[n] for n in CONST], axis=1)


def branch_gate_rows():
    m = np.zeros((24, 3, 4, 128), np.float32)
    for h in range(NH):
        for c in range(3):
            m[h * 3 + c, c, h % 4, (h // 4) * HD:(h // 4 + 1) * HD] = 1
    return m.reshape(24, 12 * 128)


def hybrid_step(nc, x_prompt, x_sample, cache_kv, page_table, state_win, state_hgrn, norm_g, w_in,
                hgrn_lb_logits, hgrn_onorm_g, dsa_qk_norm_g, dsa_idx_k_norm_g, nsa_qk_norm_g, nsa_cmp_pe,
                nsa_cmp_w1, nsa_cmp_b1, nsa_cmp_w2, w_branch, w_out, const, gate_rows,
                y_prompt, y_sample, p_rows, p_win, p_hgrn, s_rows, s_win, s_hgrn):
    ctx = ExitStack()
    with ctx:
        def sb(name, shape, dt=F32):
            return ctx.enter_context(nc.sbuf_tensor(name, shape, dt))

        def sem(name):
            return ctx.enter_context(nc.semaphore(name))

        ctx.enter_context(nc.allow_non_contiguous_dma(reason="gains and biases of a few hundred elements"))
        cst = sb("cst", [128, NCONST])
        xp = sb("xp", [128, 2, D])
        xs = sb("xs", [NS, D])
        hT = sb("hT", [128, KD, LT])
        slab = sb("slab", [128, NSLOT, 2048])
        w1 = sb("w1", [128, CB, 128])
        w2 = sb("w2", [128, 2, 128])
        Y = sb("Y", [128, 3, 4, LT])
        QF = sb("QF", [128, 3, 64])
        QC = sb("QC", [128, 2, NS * (ROWS + NH)])
        QP = sb("QP", [128, 2, ROWS])
        iwB = sb("iwB", [128, 64])
        work = sb("work", [NS, PAST + 8])
        top8 = sb("top8", [128, 8])
        kn = sb("kn", [128, 3, NS])
        vn = sb("vn", [NS, 3, 128])
        gbs = sb("gbs", [128, 12, NS])
        gx = sb("gx", [128, KD])
        gains = sb("gains", [128, 7])
        gains_row = sb("gains_row", [8, HD])
        gho = sb("gho", [128, 4])
        pe_row = sb("pe_row", [CB, 2, HD])
        peT = sb("peT", [128, 2, CB])
        b1 = sb("b1", [128, 2])
        hbias = sb("hbias", [128, 2])
        lbl = sb("lbl", [128, DEPTH + 1, 4])
        lb = sb("lb", [128, 4])
        lb1 = sb("lb1", [128, 4])
        pt = sb("pt", [1, NS * NPG], I32)
        st = sb("st", [128, 64])
        spare = sb("spare", [128, 1])
        epsb = sb("epsb", [128, 1])
        sa = sb("sa", [128, 64])
        ARENA = 27600
        arena = sb("arena", [128, ARENA])

        def at(off, *shape, rows=128):
            n = int(np.prod(shape))
            assert off + n <= ARENA, (off, shape)
            v = arena[0:rows, off:off + n]
            if len(shape) == 2:
                v = v.rearrange("p (a b) -> p a b", a=shape[0])
            if len(shape) == 3:
                v = v.rearrange("p (a b c) -> p a b c", a=shape[0], b=shape[1])
            if len(shape) == 4:
                v = v.rearrange("p (a b c d) -> p a b c d", a=shape[0], b=shape[1], c=shape[2])
            return v

        Z = at(0, NZ, LT)
        row = at(7392, 3, CW)
        wrow = at(9888, 3, 2 * 128)
        HK = at(12192, 512)[0:NS]
        VD = at(12704, NS, 128)[0:NS]
        HSQ = at(18208, 4, LT)
        HO = at(25472, 4, LT)
        HV = at(10656, 3, BW)
        RL = at(12192, 2, 384)
        acc = at(12960, 384)
        msk = at(13728, 384)
        ikst = at(14112, 2, NPG, HD)
        ikT = at(15136, 2, PAST, rows=HD)
        RD = at(17184, 2, 64)
        idxT = at(17312, NPG, NS)
        iwD = at(17376, NS, NH)[0:NS]
        iwP = at(17440, 2, NH)
        i2 = at(17456, 64)[0:NS]
        SQ = at(18208, 5, LT)
        T1 = at(19528, 5, LT)
        T2 = at(20848, 5, LT)
        S = at(14112, NS, 4, 128)
        E_ = at(18208, 4, LP)
        D_ = at(19232, 4, LP)
        M_ = at(20256, 2, 1024)
        cb = at(22304, 4, LP)
        kT = at(23360, 4, LT)
        fT = at(24416, 4, LT)
        AT = at(25472, 3, 4, 128)
        SX = at(18208, 2, 1536)
        PT = at(21280, 3, 512)
        OC = at(22816, 3, 4, LP)
        SC = at(25888, 2, NH, NCP)
        XW = at(12192, 2, 2, 16, CS)
        hc = at(13216, 2, 128)[0:16]
        hidP = at(26368, 2, 16)
        ckP = at(26400, 16)
        cvP = at(26416, 128)
        PTC = at(10656, NH, LP)
        nbs = at(14112, LT)
        gsel = at(14376, 12, 128)
        V = at(0, NS, NPG, 2, 128)
        cT = at(8192, 2, GB, PAST)
        Vw = at(16384, NS, 4, 128)
        kst = at(18432, 4, 512)
        kws = at(20480, 4, 128)
        KT = at(20992, 2, 2, 128)
        KTw = at(21504, 4, 128)
        PTd = at(22016, 20, ROWS)
        PTcx = at(22016, NS * (ROWS + NH))[0:NCS]
        ckd = at(23296, NS, NCS)
        CV = at(23800, NS, 128)
        SSx = at(24824, 2 * 1032 + 520)
        SS = [SSx[:, 1032 * a:1032 * a + n] for a, n in enumerate((PAST + 1, PAST + 1, WIN + 1))]
        hid = at(24824, 2, GB, NCS)
        PTx = (at(20480, 20, ROWS), at(24824, 20, ROWS))
        so = at(26104, 4, 128)
        o3 = at(26616, 4, 4, NS)
        PTc = at(21760, ROWS)
        sc4 = at(21824, 64)
        dr = at(21888, 64)
        pn8 = at(27408, 3, ROWS)[0:NS]
        w1v = slab[:, 1:3, :].rearrange("p s (i c) -> p (s i) c", c=128)
        sig = at(0, KD, LT)
        mT = at(2112, KD, LT)
        mtmp = at(5280, 2, LT)

        def K(name, rows=128):
            o, w = CONST[name]
            return cst[0:rows, o:o + w]

        ident, head_ones, ones, rot = K("ident"), K("head_ones"), K("ones"), K("rot")
        lvl = K("levels").rearrange("p (l t) -> p l t", l=8).bitcast(I32)
        causal = K("causal")
        ps = ctx.enter_context(nc.psum_tensor("ps", [128, 8, 512], F32))


        all_steps = []

        class Steps:

            def __init__(self, name, steps, lead=0):
                self.sem, self.steps, self.done, self.lead = sem(name), list(steps), 0, lead
                self.n = len(self.steps)
                all_steps.append(self)

            def __call__(self, r, step):
                return r * self.n + (self.steps.index(step) + 1 + self.lead * self.n)

            def before(self, r, step):
                assert self.lead
                return r * self.n + (self.steps.index(step) + 1)

            def mark(self, step):
                assert self.steps[self.done % len(self.steps)] == step, (step, self.steps, self.done)
                self.done += 1
                return 1

        consts_in, x_in, pages_in, small_in = sem("consts_in"), sem("x_in"), sem("pages_in"), sem("small_in")
        w1_in = [sem(f"w1_in{i}") for i in range(2)]
        S_in, gsel_in, v_in, v1_in = sem("S_in"), sem("gsel_in"), sem("v_in"), sem("v1_in")
        slab_in = [sem(f"slab_in{i}") for i in range(NSLOT)]
        ik_in = [sem(f"ik_in{i}") for i in range(2)]
        page_in = [sem(f"page_in{i}") for i in range(4)]
        win_in, rows_out, hg_out, y_out, win_out = (sem("win_in"), sem("rows_out"), sem("hg_out"), sem("y_out"),
                                                    sem("win_out"))
        init_done, w1v_zero, windows = sem("init_done"), sem("w1v_zero"), sem("windows")
        waited = sem("waited")
        x_ready = sem("x_ready")
        lb_v, lb_a = sem("lb_v"), sem("lb_a")
        proj_ready, proj_free = sem("proj_ready"), sem("proj_free")
        norm_a = Steps("norm_a", ["rstd"])
        norm_v = Steps("norm_v", ["diag", "small"] + [f"hT {k}" for k in range(KD)])
        norm_p = Steps("norm_p", ["small"] + [f"xT {k}" for k in range(KD)])
        grp_a = Steps("grp_a", ["sq k", "rs k", "sq dq", "rs dq", "sq nq", "rs nq"])
        grp_p = Steps("grp_p", ["rot iq", "ss k", "rot k", "ss dq", "rot dq", "ss nq", "rot nq"])
        grp_v = Steps("grp_v", ["zr iq", "zn k", "zr k", "zn dq", "zr dq", "zn nq", "zr nq"])
        rows_p = Steps("rows_p", ["rows"])
        rows_a = Steps("rows_a", ["rows"])
        pidx_p = Steps("pidx_p", ["iw"] + [f"dot {h}" for h in range(NH)])
        pidx_a = Steps("pidx_a", ["iw"] + [f"relu {h}" for h in range(NH)])
        pidx_v = Steps("pidx_v", [f"acc {h}" for h in range(NH)] + ["mask"])
        sidx_v = Steps("sidx_v", ["qf", "iwd", "new", "left out"])
        sidx_p = Steps("sidx_p", ["iwb", "new", "flat"])
        sidx_a = Steps("sidx_a", ["iwb", "new", "flat"])
        skey_p = Steps("skey_p", ["T 0", "T 1", "dot 0", "dot 1"], lead=1)
        skey_a = Steps("skey_a", ["T 0", "T 1", "relu 0", "relu 1"])
        skey_v = Steps("skey_v", ["sum 0", "sum 1"], lead=1)
        LV = list(range(9))
        hg_a = Steps("hg_a", ["gates", "ln"] + [f"e {i}" for i in LV] + ["far", "o", "kfT", "sfin", "kd", "od", "sq", "rs"])
        hg_v = Steps("hg_v", ["f", "d 0", "a diag"] + sum([[f"d {i + 1}"] * (i < 8) + [f"m {i}"]
                     + [f"a {i - 1}"] * (1 <= i <= 7) for i in LV], []) + sum([[f"vd {h}", f"sn {h}"] for h in range(4)], []) + ["done"])
        hg_p = Steps("hg_p", ["a diag"] + [f"a {i}" for i in range(8)] + ["o", "kfT", "sfin", "kd"]
                     + [f"kv {h}" for h in range(4)] + ["od", "ss"])
        U = list(range(6))
        at_p = Steps("at_p", ["s 0"] + sum([[f"s {u + 1}"] * (u < 5) + [f"t {u}", f"o {u}"] for u in U], []))
        at_a = Steps("at_a", ["e 0"] + sum([[f"e {u + 1}"] * (u < 5) + [f"pt {u}"] for u in U], []))
        at_v = Steps("at_v", ["s 0"] + sum([[f"s {u + 1}"] * (u < 5) + [f"n {u}"] + [f"ev {u - 1}"] * (u > 0)
                                            for u in U], []) + ["ev 5"])
        cp_p = Steps("cp_p", ["h 0", "h 1", "hT 0", "hT 1", "out 0", "out 1", "s", "t", "o"] + [f"gb {i}" for i in range(12)])
        cp_v = Steps("cp_v", ["bias 0", "bias 1", "s", "n", "nb", "ev"] + [f"gb {i}" for i in range(12)]
                     + ["prompt done"])
        cp_a = Steps("cp_a", ["h 0", "h 1", "hid 0", "hid 1", "out 0", "out 1", "e", "t", "nb"])
        pg_p = Steps("pg_p", sum([[f"T {i}"] + [f"s {i - 1}"] * (i > 0) for i in range(NPG)], []) + ["s 7", "T win", "s win"], lead=1)
        pg_a = Steps("pg_a", [f"T {i}" for i in range(0, NPG, 2)] + ["T win"])
        pg_v = Steps("pg_v", ["q"] + [f"T {i}" for i in range(1, NPG, 2)], lead=1)
        dc_p = Steps("dc_p", sum([[f"h {g} 0", f"h {g} 1", f"ck {g}", f"cv {g}"] for g in range(2)], [])
                     + ["scores", "s cmp", "t cmp", "imp", "group imp", "new", "PT", "oT"])
        dc_v = Steps("dc_v", ["s cmp", "n cmp", "ptx cmp", "imp", "drop", "masked", "new p", "scaled", "ev"])
        dc_a = Steps("dc_a", sum([[f"h {g} 0", f"h {g} 1", f"ck {g}", f"cv {g}"] for g in range(2)], [])
                     + ["scores", "e cmp", "t cmp", "e", "PT"])
        dx_v = Steps("dx_v", [f"x {b}" for b in range(NS)])
        dx_p = Steps("dx_p", [f"x {b}" for b in range(NS)])
        ga_p = Steps("ga_p", sum([[f"m {a} {d}" for d in range(KD)]
                                  + [f"b {a} {d}" for d in range(KD)] for a in range(3)], []) + [f"o {i}" for i in range(12)])
        ga_a = Steps("ga_a", [f"m {a} {d}" for a in range(3) for d in range(KD)])
        ga_v = Steps("ga_v", [f"b {a} {d}" for a in range(3) for d in range(KD)] + [f"o {i}" for i in range(12)])

        block = ctx.enter_context(nc.Block())
        cosb = lambda n: K("cos").unsqueeze(1).to_broadcast([128, n, LT])
        sinb = lambda n: K("sin").unsqueeze(1).to_broadcast([128, n, LT])
        halves = (slice(0, HD), slice(HD, 128))
        seq_cols = slice(LP, LT)
        attn = [(0, Z_DQ, Z_DK), (1, Z_NQ, Z_NSK), (2, Z_NQ, Z_NWK)]

        def values(a, t):
            return (row[:, t, 128:256], row[:, t, 704:832], wrow[:, t, 128:256])[a]

        def slab_view(name):
            slot = SLOT_AT[name][0]
            k = 4 if name[0] == "b" else KD
            return slab[:, slot, :].rearrange("p (k c) -> p k c", k=k)

        def pair_half(v, g, src):
            return (v.rearrange("p k (j g c) -> p k j g c", j=2, g=2)[:, :, :, g, :],
                    src.rearrange("p k (j c) -> p k j c", j=2))

        def slab_sources(name, l):
            v = slab_view(name)
            wl = w_in[bass.ds(l, 1), :, :].rearrange("a (p k) c -> p (a k) c", k=KD)
            if name in SLAB_OF:
                out, o = [], 0
                for g, (col, width) in enumerate(SLAB_OF[name][1]):
                    src = wl[:, :, col:col + width]
                    if name[:2] in PAIRS:
                        out.append(pair_half(v, g, src))
                    else:
                        out.append((v[:, :, o:o + width], src))
                    o += width
                return out
            a, i = int(name[1]) if name[0] != "o" else 0, int(name[-1])
            if name[0] == "m":
                c = C_MA + D * a + 256 * i
                return [(v[:, :, :], wl[:, :, c:c + 256])]
            if name[0] == "b":
                wb = w_branch[bass.ds(l, 1), a, :, 512 * i:512 * i + 512]
                if a == 0:
                    return [(v[:, :, :], wb.rearrange("a (j p) d -> p (a j) d", j=4))]
                w = wb.rearrange("a (g j p) d -> g p (a j) d", g=2, j=4)
                return [(v[h, :, :], w[g]) for g, h in enumerate(halves)]
            wo = w_out[bass.ds(l, 1), :, 256 * i:256 * i + 256]
            return [(v[:, :, :], wo.rearrange("a (k p) c -> p (a k) c", k=KD))]

        def holds(engine):
            engine.sem_inc(waited, 1)

        def load_values(engine, arrived, l1, s, kinds):
            for i in range(NPG):
                page = engine.value_load(pt[0:1, bass.ds(s * NPG + i, 1)], min_val=0, max_val=cache_kv.shape[1] - 1)
                pg = cache_kv[l1, bass.ds(page, 1), :, :].rearrange("a b p c -> p (a b) c")
                for a in kinds:
                    c = (128, 704)[a]
                    engine.dma_start(V[:, bass.ds(s, 1), i, a, :].rearrange("p a c -> p (a c)"), pg[:, 0, c:c + 128]).then_inc(arrived, 16)

        @block.sync
        def _(sp):
            sp.dma_start(cst[:, :], const).then_inc(consts_in, 16)
            sp.dma_start(xp[:, :, :], x_prompt[0].rearrange("(t p) d -> p t d", t=2)).then_inc(x_in, 16)
            sp.dma_start(xs[:, :], x_sample.rearrange("s o d -> s (o d)")).then_inc(x_in, 16)
            for i in range(DEPTH):
                sp.dma_start(lbl[:, i, :], hgrn_lb_logits[i].rearrange("(h k) -> k h", h=4)).then_inc(x_in, 16)
            sp.dma_start(pt[:, :], page_table.rearrange("(o a) b -> o (a b)", o=1)).then_inc(pages_in, 16)
            sp.wait_ge(pages_in, 16)
            sp.wait_ge(init_done, 2)
            with sp.Fori(0, DEPTH) as l:
                l1 = bass.ds(l, 1)

                def send(name):
                    slot = SLOT_AT[name][0]
                    at_ = STREAM.index(name)
                    if at_ >= NSLOT:
                        old = STREAM[at_ - NSLOT]
                        if old in SLAB_OF:
                            sp.wait_ge(proj_ready, l * NJOB + LAST_JOB[old])
                        else:
                            sp.wait_ge(ga_p.sem, ga_p(l, LAST_USE[old]))
                        holds(sp)
                    for dst, src in slab_sources(name, l):
                        sp.dma_start(dst, src).then_inc(slab_in[slot], 16)

                sp.wait_ge(x_ready, l + 1)
                sp.dma_start(gx[:, :], norm_g[l1, :].rearrange("a (p k) -> p (a k)", k=KD)).then_inc(small_in, 16)
                sp.dma_start(gho[:, :], hgrn_onorm_g[l1, :].rearrange("a (h v) -> v (a h)", h=4)).then_inc(small_in, 16)
                sp.dma_start(gains_row[0:2, :], dsa_qk_norm_g[l1].rearrange("a g d -> (a g) d")).then_inc(small_in, 16)
                sp.dma_start(gains_row[2:3, :], dsa_idx_k_norm_g[l1]).then_inc(small_in, 16)
                sp.dma_start(gains_row[3:7, :], nsa_qk_norm_g[l1].rearrange("a g d -> (a g) d")).then_inc(small_in, 16)
                sp.dma_start(pe_row[:, :, :], nsa_cmp_pe[l1].rearrange("a k s d -> s (a k) d")).then_inc(small_in, 16)
                for h in halves:
                    sp.dma_start(b1[h, :], nsa_cmp_b1[l1].rearrange("a k d -> d (a k)")).then_inc(small_in, 16)
                    sp.dma_start(w2[h, :, h], nsa_cmp_w2[l1].rearrange("a k c d -> c (a k) d")).then_inc(small_in, 16)
                for name in FRONT:
                    if name in SLAB_OF:
                        send(name)
                with sp.Fori(0, NS // 2) as s2:
                    r = l * (NS // 2) + s2
                    for u in range(2):
                        for i in range(NPG):
                            if i == 0:
                                holds(sp)
                            page = sp.value_load(pt[0:1, bass.ds((s2 * 2 + u) * NPG + i, 1)], min_val=0, max_val=cache_kv.shape[1] - 1)
                            if i == 0:
                                sp.wait_ge(skey_p.sem, skey_p.before(r, f"T {u}"))
                            src = cache_kv[l1, bass.ds(page, 1), :, :].rearrange("a b p c -> p (a b) c")[:, 0, 256:320]
                            sp.dma_start(ikst[:, u, i, :], src).then_inc(ik_in[u], 16)
                for name in BACK:
                    if name in SLAB_OF:
                        send(name)
                sp.wait_ge(sidx_v.sem, sidx_v(l, "new"))
                for h in range(4):
                    sp.dma_start(S[:, :, h, :], state_hgrn[l1, :, h].rearrange("a s k v -> k (a s) v")).then_inc(S_in, 16)

                for name in GATES + STREAM[len(SLABS):len(SLABS) + 1]:
                    send(name)
                for kv, w in enumerate((w1, w1v)):
                    if kv:
                        sp.wait_ge(w1v_zero, l + 1)
                    for h in halves:
                        sp.dma_start(w[h, :, h], nsa_cmp_w1[l1, kv].rearrange("a (s d) c -> d (a s) c", d=HD)).then_inc(w1_in[kv], 16)
                sp.wait_ge(hg_p.sem, hg_p(l, "od"))
                sp.wait_ge(hg_out, l * 32 + 32)
                sp.dma_start(gsel[0:24], gate_rows.rearrange("r (n c) -> r n c", n=12)).then_inc(gsel_in, 16)
                sp.wait_ge(cp_v.sem, cp_v(l, "prompt done"))
                holds(sp)
                with sp.Fori(0, NS) as s:
                    r = l * NS + s
                    for i in range(NPG):
                        page = sp.value_load(pt[0:1, bass.ds(s * NPG + i, 1)], min_val=0, max_val=cache_kv.shape[1] - 1)
                        pg = cache_kv[l1, bass.ds(page, 1), :, :].rearrange("a b p c -> p (a b) c")
                        sp.wait_ge(pg_p.sem, pg_p(r, f"T {i - 4}") if i >= 4 else pg_p.before(r, f"T {i + 4}"))
                        sp.dma_start(kst[:, i % 4, 0:128], pg[:, 0, 0:128]).then_inc(page_in[i % 4], 16)
                        sp.dma_start(kst[:, i % 4, 128:512], pg[:, 0, 320:704]).then_inc(page_in[i % 4], 16)
                    sw = state_win[l1, bass.ds(s, 1), :, :].rearrange("a b (t p) c -> p (a b t) c", t=4)
                    sp.wait_ge(pg_p.sem, pg_p.before(r, "T win"))
                    sp.dma_start(kws[:, :, :], sw[:, :, 0:128]).then_inc(win_in, 16)
                sp.wait_ge(dc_p.sem, dc_p(l, "h 1 1"))
                holds(sp)
                with sp.Fori(GB, NS) as s:
                    load_values(sp, v1_in, l1, s, (0,))
                for name in STREAM[len(SLABS) + 1:]:
                    send(name)
            sp.wait_ge(y_out, 32)

        @block.gpsimd
        def _(pool):
            nc.gpsimd.memset(w1[:, :, :], 0.0)
            nc.gpsimd.memset(w2[:, :, :], 0.0)
            nc.gpsimd.memset(QF[:, :, :], 0.0)
            nc.gpsimd.memset(QC[:, :, :], 0.0)
            pool.drain().then_inc(init_done, 1)
            pool.wait_ge(pages_in, 16)
            with pool.Fori(0, DEPTH) as l:
                l1 = bass.ds(l, 1)
                one = lambda ap: ap.rearrange("a t c -> (a t) c")
                pool.wait_ge(rows_a.sem, rows_a(l, "rows"))
                for t in range(2):
                    pool.dma_start(one(p_rows[l1, 0, t * 128:t * 128 + 128, :]), row[:, t, :]).then_inc(rows_out, 16)
                    pool.dma_start(one(p_win[l1, 0, t * 128:t * 128 + 128, :]), wrow[:, t, :]).then_inc(rows_out, 16)
                pool.dma_start(one(s_rows[l1, :, 0, :]), row[0:NS, 2, :]).then_inc(rows_out, 16)
                pool.dma_start(one(s_win[l1, :, WIN - 1, :]), wrow[0:NS, 2, :]).then_inc(rows_out, 16)
                pool.dma_start(s_win[l1, :, 0:WIN - 1, :].rearrange("a s w c -> (a s) w c"),
                               state_win[l1, :, 1:WIN, :].rearrange("a s w c -> (a s) w c")).then_inc(win_out, 16)
                pool.wait_ge(proj_ready, (l + 1) * NJOB)
                holds(pool)
                for h, other in (halves, halves[::-1]):
                    nc.gpsimd.memset(w1v[h, :, other], 0.0)
                pool.drain().then_inc(w1v_zero, 1)
                pool.wait_ge(hg_a.sem, hg_a(l, "sfin"))
                holds(pool)
                pool.dma_start(p_hgrn[l1, 0].rearrange("a h k v -> k (a h) v"), cb[:, :, 0:128]).then_inc(hg_out, 16)
                pool.wait_ge(hg_v.sem, hg_v(l, "sn 3"))
                pool.dma_start(s_hgrn[l1].rearrange("a s h k v -> k (a s) h v"), S[:, :, :, :]).then_inc(hg_out, 16)
                for kv, z in enumerate((Z_NCK, Z_NCV)):
                    for i in range(2):
                        nc.gpsimd.tensor_copy(XW[:, kv, i, 0:NCP, :], Z[:, z, i * CS:i * CS + NCP * CS].rearrange("p (n c) -> p n c", c=CS))
                        nc.gpsimd.tensor_copy(XW[:, kv, i, NCP, :], peT[:, kv, i * CS:(i + 1) * CS])
                pool.drain().then_inc(windows, 1)
                pool.wait_ge(cp_v.sem, cp_v(l, "prompt done"))
                pool.wait_ge(rows_out, l * 96 + 96)
                for g in range(2):
                    if g:
                        pool.wait_ge(dc_p.sem, dc_p(l, "h 1 1"))
                    holds(pool)
                    with pool.Fori(g * GB, (g + 1) * GB) as s:
                        s1 = bass.ds(s, 1)
                        load_values(pool, v_in, l1, s, (1,) if g else (0, 1))
                        sw = state_win[l1, s1, :, :].rearrange("a b (t p) c -> p (a b t) c", t=4)
                        pool.dma_start(Vw[:, s1, :, :].rearrange("p a t c -> p (a t) c"), sw[:, :, 128:256]).then_inc(v_in, 16)
            pool.wait_ge(rows_out, DEPTH * 96)
            pool.wait_ge(win_out, DEPTH * 16)
            pool.wait_ge(hg_out, DEPTH * 32)
            pool.wait_ge(x_ready, DEPTH + 1)
            pool.dma_start(y_prompt[0].rearrange("(t p) d -> p t d", t=2), xp[:, :, :]).then_inc(y_out, 16)
            pool.dma_start(y_sample.rearrange("s o d -> s (o d)"), xs[:, :]).then_inc(y_out, 16)
            pool.wait_ge(y_out, 32)

        def is_T(job):
            return job[0] != "V"

        @block.tensor
        def _(pe):
            mm = nc.tensor.matmul
            pe.wait_ge(consts_in, 16)
            pe.wait_ge(init_done, 2)
            for steps in (skey_p, pg_p):
                pe.sem_inc(steps.sem, steps.n)
            with pe.Fori(0, DEPTH) as l:
                pe.wait_ge(small_in, l * 160 + 160)
                pe.wait_ge(x_ready, l + 1)
                holds(pe)
                nc.tensor.transpose(ps[0:HD, 7, 0:7], gains_row[0:7, :], ident[0:7, 0:7])
                for kv in range(2):
                    last = nc.tensor.transpose(ps[0:HD, 7, 8 + CB * kv:8 + CB * (kv + 1)], pe_row[:, kv, :], ident[0:CB, 0:CB])
                last.then_inc(norm_p.sem, norm_p.mark("small"))
                pe.wait_ge(norm_v.sem, norm_v(l, "small"))
                xpk = xp[:, :, :].rearrange("p t (c k) -> p t k c", k=KD)
                xsk = xs[:, :].rearrange("p (c k) -> p k c", k=KD)
                for k in range(KD):
                    mm(ps[:, k, 0:128], xpk[:, 0, k, :], T1[:, 0, 0:128], start=True, stop=True)
                    mm(ps[:, k, 128:256], xpk[:, 1, k, :], T1[:, 1, 0:128], start=True, stop=True)
                    mm(ps[:, k, 256:264], xsk[:, k, :], T1[0:NS, 2, 0:NS], start=True, stop=True)\
                        .then_inc(norm_p.sem, norm_p.mark(f"xT {k}"))
                pe.wait_ge(norm_v.sem, norm_v(l, "hT 7"))

                def project(name, only=None):
                    slot, use, dmas = SLOT_AT[name]
                    v = slab_view(name)
                    pe.wait_ge(slab_in[slot], (l * SLOT_DMAS[slot] + dmas) * 16)
                    jobs = SLAB_OF[name][2]
                    for j, job in enumerate(jobs):
                        if only not in (None, j):
                            continue
                        n = JOB_AT[name, j]
                        pe.wait_ge(proj_free, l * NJOB + (n + 1))
                        if is_T(job):
                            for k in range(KD):
                                last = mm(ps[0:job[3], n % 2, 0:LT], v[:, k, job[2]:job[2] + job[3]], hT[:, k, :], start=(k == 0), stop=(k == KD - 1))
                            last.then_inc(proj_ready, 1)
                        else:
                            o, width = job[2], job[3]
                            for t in range(2):
                                for k in range(KD):
                                    last = mm(ps[:, n % 2, t * 256:t * 256 + width], hT[:, k, t * 128:t * 128 + 128],
                                              v[:, k, o:o + width], start=(k == 0), stop=(k == KD - 1))
                            last.then_inc(proj_ready, 1)
                            pe.wait_ge(proj_free, l * NJOB + (n + 2))
                            for k in range(KD):
                                last = mm(ps[0:NS, (n + 1) % 2, 0:width], hT[:, k, seq_cols], v[:, k, o:o + width],
                                          start=(k == 0), stop=(k == KD - 1))
                            last.then_inc(proj_ready, 1)

                for name in FRONT:
                    if name in SLAB_OF:
                        project(name)
                        continue
                    z, n, normed, _ = GROUPS[name]
                    prev = {"k": "iq", "dq": "k", "nq": "dq"}.get(name)
                    if normed:
                        pe.wait_ge(grp_a.sem, grp_a(l, f"sq {name}"))
                        pe.wait_ge(grp_v.sem, grp_v(l, f"zr {prev}"))
                        for i in range(n):
                            last = mm(ps[:, 2 + i, 0:LT], head_ones, SQ[:, i, :], start=True, stop=True)
                        last.then_inc(grp_p.sem, grp_p.mark(f"ss {name}"))
                        pe.wait_ge(grp_v.sem, grp_v(l, f"zn {name}"))
                    else:
                        jl = max(JOB_AT[nm, j] for nm in ("iq0", "iq1") for j in range(2))
                        pe.wait_ge(proj_free, l * NJOB + (jl + 3))
                    for i in range(n):
                        last = mm(ps[:, 2 + i, 0:LT], K("rot"), Z[:, z + i, :], start=True, stop=True)
                    last.then_inc(grp_p.sem, grp_p.mark(f"rot {name}"))

                pe.wait_ge(grp_v.sem, grp_v(l, "zr nq"))
                holds(pe)
                for t in range(3):
                    n = 128 if t < 2 else NS
                    cols = slice(t * 128, t * 128 + n)
                    for z, r, o, b in ((Z_DK, 128, 0, 0), (Z_IK, HD, 128, 0), (Z_NCK, 128, 192, 0), (Z_NCV, 128, 320, 0),
                                       (Z_NSK, 128, 0, 1), (Z_NWK, 128, 128, 1)):
                        last = nc.tensor.transpose(ps[0:n, 2 + 2 * t + b, o:o + r], Z[0:r, z, cols], ident[0:r, 0:r])
                last.then_inc(rows_p.sem, rows_p.mark("rows"))

                pe.wait_ge(rows_a.sem, rows_a(l, "rows"))
                holds(pe)
                for t in range(2):
                    last = nc.tensor.transpose(ps[:, 2, t * NH:t * NH + NH], Z[0:NH, Z_IW, t * 128:t * 128 + 128], ident[0:NH, 0:NH])
                last.then_inc(pidx_p.sem, pidx_p.mark("iw"))
                for h in range(NH):
                    if h >= 2:
                        pe.wait_ge(pidx_a.sem, pidx_a(l, f"relu {h - 2}"))
                    r, j, bank = halves[h // 4], h % 4, 4 + h % 2
                    mm(ps[:, bank, 0:128], Z[r, Z_IQ + j, 0:128], Z[r, Z_IK, 0:128], start=True, stop=True)
                    mm(ps[:, bank, 128:384], Z[r, Z_IQ + j, 128:256], Z[r, Z_IK, 0:256], start=True, stop=True)\
                        .then_inc(pidx_p.sem, pidx_p.mark(f"dot {h}"))

                pe.wait_ge(sidx_v.sem, sidx_v(l, "iwd"))
                mm(ps[:, 3, 0:64], ones[0:NS, :], iwD.rearrange("p s h -> p (s h)"), start=True, stop=True)\
                    .then_inc(sidx_p.sem, sidx_p.mark("iwb"))
                pe.wait_ge(sidx_a.sem, sidx_a(l, "iwb"))
                holds(pe)
                mm(ps[0:NS, 3, 0:64], Z[0:HD, Z_IK, seq_cols], QF[0:HD, 0, :], start=True, stop=True)\
                    .then_inc(sidx_p.sem, sidx_p.mark("new"))
                pe.wait_ge(sidx_a.sem, sidx_a(l, "new"))
                pe.wait_ge(pidx_a.sem, pidx_a(l, f"relu {NH - 1}"))
                holds(pe)
                with pe.Fori(0, NS // 2) as s2:
                    r = l * (NS // 2) + s2
                    for u in range(2):
                        pe.wait_ge(ik_in[u], (r + 1) * NPG * 16)
                        holds(pe)
                        for i in range(NPG):
                            last = nc.tensor.transpose(ps[0:HD, 2 + 2 * u + i // 4, (i % 4) * 128:(i % 4) * 128 + 128], ikst[:, u, i, :], ident)
                        last.then_inc(skey_p.sem, skey_p.mark(f"T {u}"))
                    for u in range(2):
                        pe.wait_ge(skey_a.sem, skey_a(r, f"T {u}"))
                        pe.wait_ge(skey_v.sem, skey_v.before(r, f"sum {u}"))
                        for i in range(NPG):
                            cols = bass.ds((s2 * 2 + u) * NH, NH)
                            last = mm(ps[:, 6 + u, i * NH:i * NH + NH], ikT[:, u, i * 128:i * 128 + 128], QF[0:HD, 0, cols],
                                      start=True, stop=True)
                        last.then_inc(skey_p.sem, skey_p.mark(f"dot {u}"))
                pe.wait_ge(skey_v.sem, skey_v(l * (NS // 2) + (NS // 2 - 1), "sum 1"))
                for i in range(NPG):
                    last = nc.tensor.transpose(ps[0:NS, 2 + i // 4, (i % 4) * 128:(i % 4) * 128 + 128], idxT[:, i, :], ident)
                last.then_inc(sidx_p.sem, sidx_p.mark("flat"))
                for name in BACK:
                    project(name)
                gates = iter(GATE_JOBS)
                for _ in range(EARLY_GATES):
                    project(*next(gates))

                Zq = Z[:, Z_HQ:Z_HQ + 4, :]
                pe.wait_ge(hg_v.sem, hg_v(l, "f"))
                pe.wait_ge(sidx_a.sem, sidx_a(l, "flat"))
                for t in range(2):
                    for h in range(4):
                        last = mm(ps[:, 2 + t, h * 128:h * 128 + 128], kT[:, h, t * 128:t * 128 + 128], Zq[:, h, t * 128:t * 128 + 128], start=True, stop=True)
                last.then_inc(hg_p.sem, hg_p.mark("a diag"))
                for i in range(8):
                    pe.wait_ge(hg_v.sem, hg_v(l, f"m {i}"))
                    b = 4 if i % 2 == 0 else 2
                    m = M_[:, i % 2, :].rearrange("p (h t) -> p h t", h=4)
                    if i < 7:
                        pe.wait_ge(hg_v.sem, hg_v(l, f"a {i - 2}" if i >= 2 else "a diag"))
                        for t in range(2):
                            for h in range(4):
                                x = m[:, h, t * 128:t * 128 + 128]
                                last = mm(ps[:, b + t, h * 128:h * 128 + 128], x, x, start=True, stop=True)
                    else:
                        for h in range(4):
                            last = mm(ps[:, 6, h * 128:h * 128 + 128], m[:, h, 0:128], m[:, h, 128:256], start=True, stop=True)
                    last.then_inc(hg_p.sem, hg_p.mark(f"a {i}"))
                    project(*next(gates))
                pe.wait_ge(hg_v.sem, hg_v(l, "a 6"))
                pe.wait_ge(hg_a.sem, hg_a(l, "far"))
                pe.wait_ge(proj_free, (l + 1) * NJOB + 2)
                for h in range(4):
                    c = slice(h * 128, h * 128 + 128)
                    mm(ps[:, 0, c], HV[:, 0, c], AT[:, 0, h, :], start=True, stop=True)
                    mm(ps[:, 1, c], HV[:, 0, c], AT[:, 2, h, :], start=True, stop=False)
                    last = mm(ps[:, 1, c], HV[:, 1, c], AT[:, 1, h, :], start=False, stop=True)
                last.then_inc(hg_p.sem, hg_p.mark("o"))
                pe.wait_ge(hg_v.sem, hg_v(l, "m 8"))
                kf = M_[:, 0, :].rearrange("p (h t) -> p h t", h=4)
                for t in range(2):
                    for h in range(4):
                        last = nc.tensor.transpose(ps[:, 2 + t, h * 128:h * 128 + 128], kf[:, h, t * 128:t * 128 + 128], ident)
                last.then_inc(hg_p.sem, hg_p.mark("kfT"))
                pe.wait_ge(hg_a.sem, hg_a(l, "kfT"))
                kft = M_[:, 1, :].rearrange("p (t c) -> p t c", t=2)
                for h in range(4):
                    c = slice(h * 128, h * 128 + 128)
                    mm(ps[:, 4, c], kft[:, 0, c], HV[:, 0, c], start=True, stop=False)
                    last = mm(ps[:, 4, c], kft[:, 1, c], HV[:, 1, c], start=False, stop=True)
                last.then_inc(hg_p.sem, hg_p.mark("sfin"))
                for h in range(4):
                    last = nc.tensor.transpose(ps[0:NS, 5, h * 128:h * 128 + 128], kT[:, h, seq_cols], ident)
                last.then_inc(hg_p.sem, hg_p.mark("kd"))
                pe.wait_ge(hg_a.sem, hg_a(l, "kd"))
                for h in range(4):
                    pe.wait_ge(hg_v.sem, hg_v(l, f"vd {h}"))
                    for i in range(2):
                        last = mm(ps[:, 6 + i, :], HK[:, h * 128:h * 128 + 128], VD[:, 4 * i:4 * i + 4, :], start=True, stop=True)
                    last.then_inc(hg_p.sem, hg_p.mark(f"kv {h}"))
                pe.wait_ge(hg_v.sem, hg_v(l, "sn 3"))
                for h in range(4):
                    for s in range(NS):
                        last = mm(ps[:, 2, h * NS + s:h * NS + s + 1], S[:, s, h, :], Zq[:, h, LP + s:LP + s + 1], start=True, stop=True)
                last.then_inc(hg_p.sem, hg_p.mark("od"))
                pe.wait_ge(hg_a.sem, hg_a(l, "sq"))
                for h in range(4):
                    last = mm(ps[:, 3 + h, 0:LT], ones, HSQ[:, h, :], start=True, stop=True)
                last.then_inc(hg_p.sem, hg_p.mark("ss"))

                def scores(u):
                    a, zq, zk = attn[u // 2]
                    r, b = halves[u % 2], 3 * (u % 2)
                    for j in range(4):
                        mm(ps[:, b, j * 128:j * 128 + 128], Z[r, zq + j, 0:128], Z[r, zk, 0:128], start=True, stop=True)
                        last = mm(ps[:, b + 1 + j // 2, (j % 2) * 256:(j % 2) * 256 + 256], Z[r, zq + j, 128:256], Z[r, zk, 0:256], start=True, stop=True)
                    last.then_inc(at_p.sem, at_p.mark(f"s {u}"))

                pe.wait_ge(hg_a.sem, hg_a(l, "rs"))
                scores(0)
                for u in range(6):
                    if u < 5:
                        if u >= 1:
                            pe.wait_ge(at_a.sem, at_a(l, f"pt {u - 1}"))
                        scores(u + 1)
                    b = 3 * (u % 2)
                    pe.wait_ge(at_v.sem, at_v(l, f"n {u}"))
                    x0 = SX[:, u % 2, 0:512].rearrange("p (j s) -> p j s", j=4)
                    x1 = SX[:, u % 2, 512:1536].rearrange("p (j s) -> p j s", j=4)
                    for j in range(4):
                        c = slice(j * 128, j * 128 + 128)
                        nc.tensor.transpose(ps[:, b, c], x0[:, j, :], ident)
                        nc.tensor.transpose(ps[:, b + 1, c], x1[:, j, 0:128], ident)
                        last = nc.tensor.transpose(ps[:, b + 2, c], x1[:, j, 128:256], ident)
                    last.then_inc(at_p.sem, at_p.mark(f"t {u}"))
                    pe.wait_ge(at_a.sem, at_a(l, f"pt {u}"))
                    if u:
                        pe.wait_ge(at_v.sem, at_v(l, f"ev {u - 1}"))
                    a = u // 2
                    mm(ps[:, 6, :], values(a, 0), PT[:, 0, :], start=True, stop=True)
                    mm(ps[:, 7, :], values(a, 0), PT[:, 1, :], start=True, stop=False)
                    mm(ps[:, 7, :], values(a, 1), PT[:, 2, :], start=False, stop=True).then_inc(at_p.sem, at_p.mark(f"o {u}"))

                pe.wait_ge(at_v.sem, at_v(l, "ev 5"))
                w1s = (w1, w1v)
                pe.wait_ge(windows, l + 1)
                for kv in range(2):
                    pe.wait_ge(w1_in[kv], l * 32 + 32)
                    for i in range(CB):
                        last = mm(ps[0:16, kv, 0:128], XW[:, kv, i // CS, :, i % CS], w1s[kv][:, i, :], start=(i == 0), stop=(i == CB - 1))
                    last.then_inc(cp_p.sem, cp_p.mark(f"h {kv}"))
                for kv in range(2):
                    pe.wait_ge(cp_a.sem, cp_a(l, f"h {kv}"))
                    holds(pe)
                    nc.tensor.transpose(ps[:, 2 + kv, 0:16], hc[:, kv, :], ident[0:16, 0:16]).then_inc(cp_p.sem, cp_p.mark(f"hT {kv}"))
                for kv in range(2):
                    pe.wait_ge(cp_a.sem, cp_a(l, f"hid {kv}"))
                    if kv == 0:
                        last = mm(ps[:, 4, 0:NCP], w2[:, 0, :], hidP[:, 0, 0:NCP], start=True, stop=True)
                    else:
                        last = mm(ps[0:NCP, 5, 0:128], hidP[:, 1, 0:NCP], w2[:, 1, :], start=True, stop=True)
                    last.then_inc(cp_p.sem, cp_p.mark(f"out {kv}"))
                pe.wait_ge(cp_a.sem, cp_a(l, "out 1"))
                for t in range(2):
                    for h in range(NH):
                        r, j = halves[h // 4], h % 4
                        last = mm(ps[:, 4 + 2 * (h // 4) + t, j * NCP:j * NCP + NCP], Z[r, Z_NQ + j, t * 128:t * 128 + 128], ckP[r, 0:NCP], start=True, stop=True)
                last.then_inc(cp_p.sem, cp_p.mark("s"))
                pe.wait_ge(cp_v.sem, cp_v(l, "n"))
                for t in range(2):
                    for h in range(NH):
                        last = nc.tensor.transpose(ps[0:NCP, h // 2, (h % 2) * 256 + t * 128:(h % 2) * 256 + t * 128 + 128], SC[:, t, h, :], ident)
                last.then_inc(cp_p.sem, cp_p.mark("t"))
                pe.wait_ge(cp_a.sem, cp_a(l, "t"))
                for g in range(2):
                    for t in range(2):
                        last = mm(ps[:, 4 + 2 * g + t, :], cvP[0:NCP, :], PTC[0:NCP, 4 * g:4 * g + 4, t * 128:t * 128 + 128], start=True, stop=True)
                last.then_inc(cp_p.sem, cp_p.mark("o"))
                pe.wait_ge(gsel_in, l * 16 + 16)
                pe.wait_ge(cp_v.sem, cp_v(l, "nb"))
                for i in range(12):
                    if i >= 4:
                        pe.wait_ge(cp_v.sem, cp_v(l, f"gb {i - 4}"))
                    mm(ps[:, i % 4, 0:LT], gsel[0:24, i, :], nbs[0:24, :], start=True, stop=True).then_inc(cp_p.sem, cp_p.mark(f"gb {i}"))

                pe.wait_ge(cp_v.sem, cp_v(l, "prompt done"))
                for i in range(5):
                    mm(ps[0:ROWS, i, :], K("zeros"), cst[:, 0:512], start=True, stop=False)
                for g in range(2):
                    if g:
                        pe.wait_ge(dc_a.sem, dc_a(l, f"cv {g - 1}"))
                    holds(pe)
                    with pe.Fori(g * GB, (g + 1) * GB) as s:
                        r = l * NS + s

                        def page_scores(i):
                            pe.wait_ge(*copied(i))
                            if i == 0:
                                pe.wait_ge(pg_v.sem, pg_v(r, "q"))
                            for a in range(2):
                                last = mm(ps[0:ROWS, 2 * a + i // 4, (i % 4) * 128:(i % 4) * 128 + 128], QP[:, a, :], KT[:, i % 2, a, :],
                                          start=False, stop=False)
                            last.then_inc(pg_p.sem, pg_p.mark(f"s {i}"))

                        def copied(i):
                            steps = pg_v if i % 2 else pg_a
                            return steps.sem, steps(r, f"T {i}")

                        for i in range(NPG):
                            pe.wait_ge(page_in[i % 4], (r * 2 + (i // 4 + 1)) * 32)
                            if i >= 2:
                                pe.wait_ge(*copied(i - 2))
                            for c in range(4):
                                last = nc.tensor.transpose(ps[:, 5 + i % 2, c * 128:c * 128 + 128], kst[:, i % 4, c * 128:c * 128 + 128], ident)
                            last.then_inc(pg_p.sem, pg_p.mark(f"T {i}"))
                            if i:
                                page_scores(i - 1)
                        page_scores(NPG - 1)
                        pe.wait_ge(win_in, r * 16 + 16)
                        for t in range(4):
                            last = nc.tensor.transpose(ps[:, 7, t * 128:t * 128 + 128], kws[:, t, :], ident)
                        last.then_inc(pg_p.sem, pg_p.mark("T win"))
                        pe.wait_ge(pg_a.sem, pg_a(r, "T win"))
                        mm(ps[0:ROWS, 4, :], QP[:, 1, :], KTw.rearrange("p t c -> p (t c)"), start=False, stop=False)\
                            .then_inc(pg_p.sem, pg_p.mark("s win"))
                    for kv in range(2):
                        for i in range(CB):
                            last = mm(ps[:, 7 - 2 * kv, 0:GB * NCS].rearrange("p (b n) -> p b n", b=GB), w1s[kv][:, i, :],
                                      cT[:, kv, :, i:i + CS * (NCS - 1) + 1:CS], start=(i == 0), stop=(i == CB - 1))
                        last.then_inc(dc_p.sem, dc_p.mark(f"h {g} {kv}"))
                    pe.wait_ge(dc_a.sem, dc_a(l, f"h {g} 0"))
                    mm(ps[:, 6, 0:GB * NCS], w2[:, 0, :], hid[:, 0], start=True, stop=True).then_inc(dc_p.sem, dc_p.mark(f"ck {g}"))
                    pe.wait_ge(dc_a.sem, dc_a(l, f"h {g} 1"))
                    for b in range(GB):
                        last = mm(ps[0:NCS, 7, b * 128:b * 128 + 128], hid[:, 1, b, :], w2[:, 1, :], start=True, stop=True)
                    last.then_inc(dc_p.sem, dc_p.mark(f"cv {g}"))

                for i in range(5):
                    last = mm(ps[0:ROWS, i, 0:64], K("zeros"), cst[:, 0:64], start=False, stop=True)
                last.then_inc(dc_p.sem, dc_p.mark("scores"))
                pe.wait_ge(dc_a.sem, dc_a(l, "cv 1"))
                for b in range(NS):
                    last = mm(ps[0:ROWS, 5, 0:NCS], QC[:, 1, b * ROWS:(b + 1) * ROWS], ckd[:, b, :], start=(b == 0), stop=(b == NS - 1))
                last.then_inc(dc_p.sem, dc_p.mark("s cmp"))
                pe.wait_ge(dc_v.sem, dc_v(l, "n cmp"))
                holds(pe)
                nc.tensor.transpose(ps[0:NCS, 6, 0:ROWS], sc4[0:ROWS, 0:NCS], ident[0:ROWS, 0:ROWS]).then_inc(dc_p.sem, dc_p.mark("t cmp"))
                pe.wait_ge(dc_a.sem, dc_a(l, "t cmp"))
                holds(pe)
                mm(ps[0:ROWS, 5, 0:NSEL], PTc[0:NCS, :], K("cover", NCS), start=True, stop=True).then_inc(dc_p.sem, dc_p.mark("imp"))
                pe.wait_ge(dc_v.sem, dc_v(l, "ptx cmp"))
                holds(pe)
                for b in range(NS):
                    mm(ps[0:ROWS, 7, 0:128], PTcx[:, b * ROWS:(b + 1) * ROWS], CV[0:NCS, b, :], start=(b == 0), stop=(b == NS - 1))
                pe.wait_ge(dc_v.sem, dc_v(l, "imp"))
                holds(pe)
                mm(ps[0:ROWS, 5, 0:NSEL], K("group_sum", ROWS), dr[0:ROWS, 0:NSEL], start=True, stop=True)\
                    .then_inc(dc_p.sem, dc_p.mark("group imp"))
                ex = K("seq_rows", NS)
                for a in range(3):
                    mm(ps[0:ROWS, 6, a * NS:a * NS + NS], QF[:, 1 + min(a, 1), :], kn[:, a, :], start=True, stop=True)
                mm(ps[0:ROWS, 6, 32:33], ex, work[:, PAST:PAST + 1], start=True, stop=True)
                pe.wait_ge(dc_a.sem, dc_a(l, "scores"))
                holds(pe)
                for i in range(2):
                    last = mm(ps[0:ROWS, i, :], ex, work[:, i * 512:i * 512 + 512], start=True, stop=True)
                last.then_inc(dc_p.sem, dc_p.mark("new"))
                pe.wait_ge(dc_v.sem, dc_v(l, "new p"))
                holds(pe)
                for i in range(20):
                    src = SS[i // 8][0:ROWS, (i % 8) * 128:(i % 8) * 128 + 128]
                    nc.tensor.transpose(ps[:, 2 + i // 8, (i % 8) * ROWS:(i % 8) * ROWS + ROWS], src, ident[0:ROWS, 0:ROWS])
                for a in range(3):
                    last = nc.tensor.transpose(ps[0:NS, 6, a * ROWS:(a + 1) * ROWS], dr[0:ROWS, 24 + a * NS:24 + (a + 1) * NS], ident[0:ROWS, 0:ROWS])
                last.then_inc(dc_p.sem, dc_p.mark("PT"))
                pe.wait_ge(dc_a.sem, dc_a(l, "PT"))
                holds(pe)
                banks = (0, 1, 5)
                for a, bank in enumerate(banks):
                    mm(ps[0:ROWS, bank, 0:128], pn8[0:NS, a, :], vn[:, a, :], start=True, stop=False)
                pe.wait_ge(v_in, (l + 1) * (GB * 3 * NPG + NS) * 16)
                pe.wait_ge(v1_in, (l + 1) * GB * NPG * 16)
                for b in range(NS):
                    pe.wait_ge(dx_v.sem, dx_v(l, f"x {b}"))
                    holds(pe)
                    end = b == NS - 1
                    for i in range(NPG):
                        for a in range(2):
                            mm(ps[0:ROWS, banks[a], 0:128], PTx[b % 2][:, a * NPG + i, :], V[:, b, i, a, :], start=False, stop=end and i == NPG - 1)
                    for i in range(4):
                        last = mm(ps[0:ROWS, banks[2], 0:128], PTx[b % 2][:, 2 * NPG + i, :], Vw[:, b, i, :], start=False, stop=end and i == 3)
                    last.then_inc(dx_p.sem, dx_p.mark(f"x {b}"))
                pe.wait_ge(dc_v.sem, dc_v(l, "scaled"))
                holds(pe)
                for a in range(4):
                    last = nc.tensor.transpose(ps[:, 6, a * ROWS:(a + 1) * ROWS], so[0:ROWS, a, :], ident[0:ROWS, 0:ROWS])
                last.then_inc(dc_p.sem, dc_p.mark("oT"))

                def arrived(name):
                    slot, use, dmas = SLOT_AT[name]
                    pe.wait_ge(slab_in[slot], (l * SLOT_DMAS[slot] + dmas) * 16)
                    return slab_view(name)

                for a in range(3):
                    for i in range(4):
                        v = arrived(f"m{a}{i}")
                        for jj in range(2):
                            d = 2 * i + jj
                            bank = 4 + d % 2
                            if a or d >= 2:
                                pe.wait_ge(ga_a.sem, ga_a(l, f"m {a} {d - 2}" if d >= 2 else f"m {a - 1} {d + 6}"))
                            for k in range(KD):
                                last = mm(ps[:, bank, 0:LT], v[:, k, jj * 128:jj * 128 + 128], hT[:, k, :], start=(k == 0), stop=(k == KD - 1))
                            last.then_inc(ga_p.sem, ga_p.mark(f"m {a} {d}"))
                    if a == 0:
                        pe.wait_ge(dc_v.sem, dc_v(l, "ev"))
                    for i in range(2):
                        v = arrived(f"b{a}{i}")
                        for dd in range(4):
                            d = 4 * i + dd
                            if a or d >= 4:
                                pe.wait_ge(ga_v.sem, ga_v(l, f"b {a} {d - 4}" if d >= 4 else f"b {a - 1} {d + 4}"))
                            for j in range(4):
                                last = mm(ps[:, d % 4, 0:LT], v[:, j, dd * 128:dd * 128 + 128], Y[:, a, j, :], start=(j == 0), stop=(j == 3))
                            last.then_inc(ga_p.sem, ga_p.mark(f"b {a} {d}"))
                pe.wait_ge(ga_v.sem, ga_v(l, "b 2 7"))
                for i in range(4):
                    v = arrived(f"o{i}")
                    for t in range(3):
                        n = 3 * i + t
                        if n >= 4:
                            pe.wait_ge(ga_v.sem, ga_v(l, f"o {n - 4}"))
                        m = 128 if t < 2 else NS
                        for k in range(KD):
                            last = mm(ps[0:m, n % 4, 0:256], mT[:, k, t * 128:t * 128 + m], v[:, k, :], start=(k == 0), stop=(k == KD - 1))
                        last.then_inc(ga_p.sem, ga_p.mark(f"o {n}"))

        IW_SCALE = NH ** -0.5 * HD ** -0.5
        taken = float(np.float32(TAKEN))

        @block.scalar
        def _(act):
            A = nc.scalar.activation

            def copy(out, in_, scale=1.0):
                return A(out, in_, ACT.Copy, scale=scale)

            act.wait_ge(lb_v, 1)
            A(lbl[:, 0:DEPTH, :], lbl[:, 0:DEPTH, :], ACT.Exp).then_inc(lb_a, 1)
            act.sem_inc(proj_free, 2)
            act.wait_ge(x_in, 64)
            with act.Fori(0, DEPTH) as l:
                act.wait_ge(x_ready, l + 1)
                squares = at(18208, 3, D)
                for t in range(2):
                    A(squares[:, t, :], xp[:, t, :], ACT.Square, accum_out=sa[:, t:t + 1])
                A(squares[0:NS, 2, :], xs[:, :], ACT.Square, accum_out=sa[0:NS, 2:3])
                act.drain()
                for p, c in ((128, slice(0, 2)), (NS, slice(2, 3))):
                    A(sa[0:p, c], sa[0:p, c], ACT.Ln, scale=1.0 / D, bias=epsb[0:p, :])
                act.drain()
                for p, c in ((128, slice(0, 2)), (NS, slice(2, 3))):
                    last = A(sa[0:p, c], sa[0:p, c], ACT.Exp, scale=-0.5)
                act.drain().then_inc(norm_a.sem, norm_a.mark("rstd"))

                def evacuate(name, only=None):
                    for j, job in enumerate(SLAB_OF[name][2]):
                        if only not in (None, j):
                            continue
                        n = JOB_AT[name, j]
                        act.wait_ge(proj_ready, l * NJOB + (n + 1))
                        src = ps[0:min(job[3], 128), n % 2, 0:LT]
                        if name[:2] == "hf":
                            A(fT[:, job[1] - Z_HF, :], src, ACT.Sigmoid)
                            A(kT[:, job[1] - Z_HF, :], src, ACT.Sigmoid, scale=-1.0).then_inc(proj_free, 1)
                            continue
                        if job[0] == "Y":
                            A(Y[:, job[1] // 4, job[1] % 4, :], src, ACT.Silu).then_inc(proj_free, 1)
                            continue
                        if job[0] == "T":
                            A(Z[0:job[3], job[1], :], src, ACT.Silu if name[:2] == "hq" else ACT.Copy).then_inc(proj_free, 1)
                            continue
                        dst = {"rows": row, "win": wrow, "hv": HV}[job[1]]
                        w, o = job[3], job[4]
                        copy(dst[:, 0:2, o:o + w], ps[:, n % 2, :].rearrange("p (t c) -> p t c", t=2)[:, :, 0:w]).then_inc(proj_free, 1)
                        act.wait_ge(proj_ready, l * NJOB + (n + 2))
                        copy(dst[0:NS, 2, o:o + w], ps[0:NS, (n + 1) % 2, 0:w]).then_inc(proj_free, 1)

                for name in FRONT:
                    if name in SLAB_OF:
                        evacuate(name)
                        continue
                    z, n, normed, _ = GROUPS[name]
                    if not normed:
                        continue
                    prev = {"dq": "k", "nq": "dq"}.get(name)
                    if prev:
                        act.wait_ge(grp_v.sem, grp_v(l, f"zn {prev}"))
                        A(sa[:, 63:64], sa[:, 0:1], ACT.Copy)
                    act.drain()
                    A(SQ[:, 0:n, :], Z[:, z:z + n, :], ACT.Square).then_inc(grp_a.sem, grp_a.mark(f"sq {name}"))
                    act.wait_ge(grp_p.sem, grp_p(l, f"ss {name}"))
                    A(SQ[:, 0:n, :], ps[:, 2:2 + n, 0:LT], ACT.Ln, scale=1.0 / HD, bias=epsb[:, :])
                    act.drain()
                    A(SQ[:, 0:n, :], SQ[:, 0:n, :], ACT.Exp, scale=-0.5).then_inc(grp_a.sem, grp_a.mark(f"rs {name}"))

                act.wait_ge(rows_p.sem, rows_p(l, "rows"))
                for t in range(3):
                    n = 128 if t < 2 else NS
                    b = 2 + 2 * t
                    copy(row[0:n, t, 0:128], ps[0:n, b, 0:128])
                    copy(row[0:n, t, 256:576], ps[0:n, b, 128:448])
                    copy(row[0:n, t, 576:704], ps[0:n, b + 1, 0:128])
                    copy(wrow[0:n, t, 0:128], ps[0:n, b + 1, 128:256])
                act.drain().then_inc(rows_a.sem, rows_a.mark("rows"))

                act.wait_ge(pidx_p.sem, pidx_p(l, "iw"))
                copy(iwP, ps[:, 2, 0:2 * NH].rearrange("p (t h) -> p t h", t=2), IW_SCALE).then_inc(pidx_a.sem, pidx_a.mark("iw"))
                for h in range(NH):
                    act.wait_ge(pidx_p.sem, pidx_p(l, f"dot {h}"))
                    if h >= 2:
                        act.wait_ge(pidx_v.sem, pidx_v(l, f"acc {h - 2}"))
                    A(RL[:, h % 2, :], ps[:, 4 + h % 2, 0:384], ACT.Relu).then_inc(pidx_a.sem, pidx_a.mark(f"relu {h}"))

                act.wait_ge(sidx_p.sem, sidx_p(l, "iwb"))
                copy(iwB[:, :], ps[:, 3, 0:64], IW_SCALE).then_inc(sidx_a.sem, sidx_a.mark("iwb"))
                act.wait_ge(sidx_p.sem, sidx_p(l, "new"))
                A(i2, ps[0:NS, 3, 0:64], ACT.Relu).then_inc(sidx_a.sem, sidx_a.mark("new"))
                with act.Fori(0, NS // 2) as s2:
                    r = l * (NS // 2) + s2
                    for u in range(2):
                        act.wait_ge(skey_p.sem, skey_p(r, f"T {u}"))
                        copy(ikT[:, u, :].rearrange("p (b c) -> p b c", b=2), ps[0:HD, 2 + 2 * u:4 + 2 * u, :]).then_inc(skey_a.sem, skey_a.mark(f"T {u}"))
                    for u in range(2):
                        act.wait_ge(skey_p.sem, skey_p(r, f"dot {u}"))
                        A(RD[:, u, :], ps[:, 6 + u, 0:64], ACT.Relu).then_inc(skey_a.sem, skey_a.mark(f"relu {u}"))
                act.wait_ge(sidx_p.sem, sidx_p(l, "flat"))
                copy(work[:, 0:PAST].rearrange("p (b c) -> p b c", b=2), ps[0:NS, 2:4, :]).then_inc(sidx_a.sem, sidx_a.mark("flat"))
                for name in BACK:
                    evacuate(name)

                act.drain().then_inc(hg_a.sem, hg_a.mark("gates"))
                gates = iter(GATE_JOBS)
                for _ in range(EARLY_GATES):
                    evacuate(*next(gates))
                act.wait_ge(hg_v.sem, hg_v(l, "f"))
                A(D_, fT[:, :, 0:LP], ACT.Ln).then_inc(hg_a.sem, hg_a.mark("ln"))
                DE = (E_, D_)
                for i in range(9):
                    act.wait_ge(hg_v.sem, hg_v(l, f"d {i}"))
                    A(DE[i % 2], DE[i % 2], ACT.Exp).then_inc(hg_a.sem, hg_a.mark(f"e {i}"))
                    if i:
                        evacuate(*next(gates))
                act.wait_ge(hg_p.sem, hg_p(l, "a 7"))
                copy(AT[:, 2, :, :], ps[:, 6, :].rearrange("p (h t) -> p h t", h=4)).then_inc(hg_a.sem, hg_a.mark("far"))
                act.wait_ge(hg_p.sem, hg_p(l, "o"))
                for t in range(2):
                    last = copy(HO[:, :, t * 128:t * 128 + 128], ps[:, t, :].rearrange("p (h t) -> p h t", h=4))
                last.then_inc(hg_a.sem, hg_a.mark("o"))
                act.wait_ge(hg_p.sem, hg_p(l, "kfT"))
                copy(M_[:, 1, :].rearrange("p (b c) -> p b c", b=2), ps[:, 2:4, :]).then_inc(hg_a.sem, hg_a.mark("kfT"))
                act.wait_ge(hg_p.sem, hg_p(l, "sfin"))
                copy(cb[:, :, 0:128], ps[:, 4, :].rearrange("p (h v) -> p h v", h=4)).then_inc(hg_a.sem, hg_a.mark("sfin"))
                act.wait_ge(hg_p.sem, hg_p(l, "kd"))
                copy(HK, ps[0:NS, 5, :]).then_inc(hg_a.sem, hg_a.mark("kd"))
                act.wait_ge(hg_p.sem, hg_p(l, "od"))
                copy(HO[:, :, seq_cols], ps[:, 2, 0:4 * NS].rearrange("p (h s) -> p h s", h=4)).then_inc(hg_a.sem, hg_a.mark("od"))
                act.drain()
                A(HSQ, HO, ACT.Square).then_inc(hg_a.sem, hg_a.mark("sq"))
                act.wait_ge(hg_p.sem, hg_p(l, "ss"))
                A(HSQ, ps[:, 3:7, 0:LT], ACT.Ln, scale=1.0 / 128, bias=epsb[:, :])
                act.drain()
                A(HSQ, HSQ, ACT.Exp, scale=-0.5).then_inc(hg_a.sem, hg_a.mark("rs"))

                def exps(u):
                    act.wait_ge(at_v.sem, at_v(l, f"s {u}"))
                    x0 = SX[:, u % 2, 0:512].rearrange("p (j s) -> p j s", j=4)
                    x1 = SX[:, u % 2, 512:1536].rearrange("p (j s) -> p j s", j=4)
                    c = 8 * (u % 2)
                    for j in range(4):
                        A(x0[:, j, :], x0[:, j, :], ACT.Exp, bias=st[:, c + j:c + j + 1], accum_out=sa[:, c + j:c + j + 1])
                        A(x1[:, j, :], x1[:, j, :], ACT.Exp, bias=st[:, c + 4 + j:c + 5 + j], accum_out=sa[:, c + 4 + j:c + 5 + j])
                    act.drain().then_inc(at_a.sem, at_a.mark(f"e {u}"))

                exps(0)
                for u in range(6):
                    if u < 5:
                        exps(u + 1)
                    act.wait_ge(at_p.sem, at_p(l, f"t {u}"))
                    if u:
                        act.wait_ge(at_p.sem, at_p(l, f"o {u - 1}"))
                    else:
                        act.wait_ge(hg_out, l * 32 + 32)
                    copy(PT, ps[:, 3 * (u % 2):3 * (u % 2) + 3, :]).then_inc(at_a.sem, at_a.mark(f"pt {u}"))

                for kv in range(2):
                    act.wait_ge(cp_p.sem, cp_p(l, f"h {kv}"))
                    copy(hc[:, kv, :], ps[0:16, kv, 0:128]).then_inc(cp_a.sem, cp_a.mark(f"h {kv}"))
                for kv in range(2):
                    act.wait_ge(cp_v.sem, cp_v(l, f"bias {kv}"))
                    A(hidP[:, kv, 0:NCP], ps[:, 2 + kv, 0:NCP], ACT.Silu, bias=hbias[:, kv:kv + 1]).then_inc(cp_a.sem, cp_a.mark(f"hid {kv}"))
                for kv in range(2):
                    act.wait_ge(cp_p.sem, cp_p(l, f"out {kv}"))
                    if kv == 0:
                        last = copy(ckP[:, 0:NCP], ps[:, 4, 0:NCP])
                    else:
                        last = copy(cvP[0:NCP, :], ps[0:NCP, 5, 0:128])
                    last.then_inc(cp_a.sem, cp_a.mark(f"out {kv}"))
                act.wait_ge(cp_v.sem, cp_v(l, "s"))
                A(SC, SC, ACT.Exp).then_inc(cp_a.sem, cp_a.mark("e"))
                act.wait_ge(cp_p.sem, cp_p(l, "t"))
                copy(PTC[0:NCP].rearrange("p h t -> p (h t)").rearrange("p (b c) -> p b c", b=4), ps[0:NCP, 0:4, :]).then_inc(cp_a.sem, cp_a.mark("t"))
                A(nbs[0:24, :], Z[0:24, Z_NBG, :], ACT.Exp, scale=-1.0).then_inc(cp_a.sem, cp_a.mark("nb"))

                for g in range(2):
                    with act.Fori(0, GB) as b:
                        r = l * NS + (b + g * GB)
                        for i in range(0, NPG, 2):
                            act.wait_ge(pg_p.sem, pg_p(r, f"T {i}"))
                            x = ps[:, 5, :].rearrange("p (c x) -> p c x", c=4)
                            copy(KT[:, 0], x[:, 0:4:3, :])
                            copy(cT[:, :, bass.ds(b, 1), i * 128:i * 128 + 128].rearrange("p k b c -> p k (b c)"), x[:, 1:3, :])\
                                .then_inc(pg_a.sem, pg_a.mark(f"T {i}"))
                        act.wait_ge(pg_p.sem, pg_p(r, "T win"))
                        copy(KTw, ps[:, 7, :].rearrange("p (t x) -> p t x", t=4)).then_inc(pg_a.sem, pg_a.mark("T win"))
                    for kv in range(2):
                        act.wait_ge(dc_p.sem, dc_p(l, f"h {g} {kv}"))
                        A(hid[:, kv].rearrange("p b n -> p (b n)"), ps[:, 7 - 2 * kv, 0:GB * NCS], ACT.Silu, bias=hbias[:, kv:kv + 1])\
                            .then_inc(dc_a.sem, dc_a.mark(f"h {g} {kv}"))
                    act.wait_ge(dc_p.sem, dc_p(l, f"ck {g}"))
                    copy(ckd[:, g * GB:(g + 1) * GB].rearrange("p b n -> p (b n)"), ps[:, 6, 0:GB * NCS]).then_inc(dc_a.sem, dc_a.mark(f"ck {g}"))
                    act.wait_ge(dc_p.sem, dc_p(l, f"cv {g}"))
                    copy(CV[0:NCS, g * GB:(g + 1) * GB].rearrange("p b n -> p (b n)"), ps[0:NCS, 7, :]).then_inc(dc_a.sem, dc_a.mark(f"cv {g}"))
                act.wait_ge(dc_p.sem, dc_p(l, "scores"))
                for a in range(2):
                    copy(SS[a][0:ROWS, 0:PAST].rearrange("p (b c) -> p b c", b=2), ps[0:ROWS, 2 * a:2 * a + 2, :], SCALE)
                copy(SS[2][0:ROWS, 0:WIN], ps[0:ROWS, 4, :], SCALE)
                act.drain().then_inc(dc_a.sem, dc_a.mark("scores"))
                act.wait_ge(dc_v.sem, dc_v(l, "s cmp"))
                A(sc4[0:ROWS, 0:NCS], sc4[0:ROWS, 0:NCS], ACT.Exp, bias=st[0:ROWS, 40:41], accum_out=sa[0:ROWS, 40:41])
                act.drain().then_inc(dc_a.sem, dc_a.mark("e cmp"))
                act.wait_ge(dc_p.sem, dc_p(l, "t cmp"))
                copy(PTc[0:NCS, :], ps[0:NCS, 6, 0:ROWS]).then_inc(dc_a.sem, dc_a.mark("t cmp"))
                act.wait_ge(dc_v.sem, dc_v(l, "masked"))
                for a, n in enumerate((PAST + 1, PAST + 1, WIN + 1)):
                    A(SS[a][0:ROWS, 0:n], SS[a][0:ROWS, 0:n], ACT.Exp, bias=st[0:ROWS, 43 + a:44 + a], accum_out=sa[0:ROWS, 43 + a:44 + a])
                act.drain().then_inc(dc_a.sem, dc_a.mark("e"))
                act.wait_ge(dc_p.sem, dc_p(l, "PT"))
                for i in range(3):
                    n = min(8, 20 - 8 * i) * ROWS
                    copy(PTd.rearrange("p i r -> p (i r)")[:, 8 * i * ROWS:8 * i * ROWS + n], ps[:, 2 + i, 0:n])
                copy(pn8.rearrange("p a r -> p (a r)"), ps[0:NS, 6, 0:3 * ROWS])
                act.drain().then_inc(dc_a.sem, dc_a.mark("PT"))

                for a in range(3):
                    for d in range(KD):
                        act.wait_ge(ga_p.sem, ga_p(l, f"m {a} {d}"))
                        if a:
                            act.wait_ge(ga_v.sem, ga_v(l, f"b {a - 1} {d}"))
                        A(sig[:, d, :], ps[:, 4 + d % 2, 0:LT], ACT.Sigmoid).then_inc(ga_a.sem, ga_a.mark(f"m {a} {d}"))

        @block.vector
        def _(ve):
            TT, TS, STT, TC = nc.vector.tensor_tensor, nc.vector.tensor_scalar, nc.vector.scalar_tensor_tensor, nc.vector.tensor_copy
            RED = nc.vector.tensor_reduce

            def rest():
                ve.memset(spare[:, :], 0.0)

            ve.memset(epsb[:, :], EPS)
            ve.memset(lbl[:, DEPTH, :], 0.0)
            ve.memset(lb[:, :], 0.0)
            ve.memset(lb1[:, :], 1.0)
            ve.memset(sa[:, :], 0.0)
            ve.drain().then_inc(init_done, 1)
            ve.wait_ge(x_in, 64)
            ve.wait_ge(consts_in, 16)
            RED(st[:, 0:4], lbl[:, 0:DEPTH, :].rearrange("p l h -> p h l"), AXX, ALU.max)
            ve.drain()
            TT(lbl[:, 0:DEPTH, :], lbl[:, 0:DEPTH, :], st[:, 0:4].unsqueeze(1).to_broadcast([128, DEPTH, 4]), ALU.subtract).then_inc(lb_v, 1)
            ve.wait_ge(lb_a, 1)
            RED(st[:, 0:4], lbl[:, 0:DEPTH, :].rearrange("p l h -> p h l"), AXX, ALU.add)
            ve.drain()
            nc.vector.reciprocal(st[:, 4:8], st[:, 0:4])
            ve.drain()
            TT(lbl[:, 0:DEPTH, :], lbl[:, 0:DEPTH, :], st[:, 4:8].unsqueeze(1).to_broadcast([128, DEPTH, 4]), ALU.mult)
            for steps in (skey_v, pg_v):
                ve.sem_inc(steps.sem, steps.n)
            ve.drain().then_inc(x_ready, 1)
            with ve.Fori(0, DEPTH) as l:
                ve.wait_ge(norm_a.sem, norm_a(l, "rstd"))
                for t in range(2):
                    TS(T1[:, t, 0:128], ident, sa[:, t:t + 1], None, ALU.mult)
                TS(T1[0:NS, 2, 0:NS], ident[0:NS, 0:NS], sa[0:NS, 2:3], None, ALU.mult).then_inc(norm_v.sem, norm_v.mark("diag"))
                ve.wait_ge(norm_p.sem, norm_p(l, "small"))
                for h in halves:
                    TC(gains[h, :], ps[0:HD, 7, 0:7])
                    TC(peT[h, :, :].rearrange("p a s -> p (a s)"), ps[0:HD, 7, 8:8 + 2 * CB])
                ve.drain().then_inc(norm_v.sem, norm_v.mark("small"))
                for k in range(KD):
                    ve.wait_ge(norm_p.sem, norm_p(l, f"xT {k}"))
                    TS(hT[:, k, :], ps[:, k, 0:LT], gx[:, k:k + 1], None, ALU.mult).then_inc(norm_v.sem, norm_v.mark(f"hT {k}"))

                for name in FRONT:
                    if name in SLAB_OF:
                        continue
                    z, n, normed, cols = GROUPS[name]
                    x = Z[:, z:z + n, :]
                    if normed:
                        ve.wait_ge(grp_a.sem, grp_a(l, f"rs {name}"))
                        for i in range(n):
                            c = cols[i]
                            last = STT(Z[:, z + i, :], Z[:, z + i, :], gains[:, c:c + 1], SQ[:, i, :], ALU.mult, ALU.mult)
                        ve.drain().then_inc(grp_v.sem, grp_v.mark(f"zn {name}"))
                    ve.wait_ge(grp_p.sem, grp_p(l, f"rot {name}"))
                    TT(T1[:, 0:n, :], x, cosb(n), ALU.mult)
                    TT(T2[:, 0:n, :], ps[:, 2:2 + n, 0:LT], sinb(n), ALU.mult)
                    ve.drain()
                    TT(x, T1[:, 0:n, :], T2[:, 0:n, :], ALU.add).then_inc(grp_v.sem, grp_v.mark(f"zr {name}"))

                ve.wait_ge(rows_a.sem, rows_a(l, "rows"))
                rest()
                ve.drain()
                qf = QF[:, :, :].rearrange("p a (s h) -> p a s h", s=NS)
                for g, h in enumerate(halves):
                    hh = slice(4 * g, 4 * g + 4)
                    TC(qf[0:HD, 0, :, hh], Z[h, Z_IQ:Z_IQ + 4, seq_cols].rearrange("p j s -> p s j"))
                    TC(qf[h, 1, :, hh], Z[h, Z_DQ:Z_DQ + 4, seq_cols].rearrange("p j s -> p s j"))
                    TC(qf[h, 2, :, hh], Z[h, Z_NQ:Z_NQ + 4, seq_cols].rearrange("p j s -> p s j"))
                for i, z in enumerate((Z_DK, Z_NSK, Z_NWK)):
                    TC(kn[:, i, :], Z[:, z, seq_cols])
                    TC(vn[:, i, :], values(i, 2)[0:NS])
                ve.drain()
                for a in range(2):
                    TC(QC[:, a, :].rearrange("p (b x) -> p b x", b=NS)[:, :, 0:NH], qf[:, 1 + a, :, :])
                ve.drain().then_inc(sidx_v.sem, sidx_v.mark("qf"))
                i8 = ident[0:NS, 0:NH]
                TT(iwD, Z[0:NH, Z_IW, seq_cols].unsqueeze(2).to_broadcast([NH, NS, NH]), i8.unsqueeze(1).to_broadcast([NH, NS, NH]), ALU.mult)\
                    .then_inc(sidx_v.sem, sidx_v.mark("iwd"))

                for h in range(NH):
                    ve.wait_ge(pidx_a.sem, pidx_a(l, f"relu {h}"))
                    for t, c in enumerate((slice(0, 128), slice(128, 384))):
                        STT(acc[:, c], RL[:, h % 2, c], iwP[:, t, h:h + 1], causal[:, c] if h == 0 else acc[:, c], ALU.mult, ALU.add)
                    ve.drain().then_inc(pidx_v.sem, pidx_v.mark(f"acc {h}"))
                for c in (slice(0, 128), slice(128, 384)):
                    for _ in range(TOPK_P // 8):
                        nc.vector.max(top8[:, :], acc[:, c])
                        ve.drain()
                        nc.vector.match_replace(acc[:, c], top8[:, :], acc[:, c], taken)
                        ve.drain()
                TS(msk, acc, taken, NEG, ALU.not_equal, ALU.mult)
                ve.drain()
                TT(msk, msk, causal, ALU.add)
                ve.drain().then_inc(pidx_v.sem, pidx_v.mark("mask"))

                ve.wait_ge(sidx_a.sem, sidx_a(l, "new"))
                TT(i2, i2, iwB[0:NS, :], ALU.mult)
                ve.drain()
                TT(i2, i2, K("seq_rows", NS), ALU.mult)
                ve.drain()
                RED(work[:, PAST:PAST + 1], i2, AXX, ALU.add)
                ve.drain().then_inc(sidx_v.sem, sidx_v.mark("new"))
                with ve.Fori(0, NS // 2) as s2:
                    r = l * (NS // 2) + s2
                    for u in range(2):
                        s = s2 * 2 + u
                        ve.wait_ge(skey_a.sem, skey_a(r, f"relu {u}"))
                        rd = RD[:, u, :].rearrange("p (i h) -> p i h", i=NPG)
                        TT(rd, rd, iwB[:, bass.ds(s * NH, NH)].unsqueeze(1).to_broadcast([128, NPG, NH]), ALU.mult)
                        ve.drain()
                        RED(idxT[:, :, bass.ds(s, 1)], rd, AXX, ALU.add).then_inc(skey_v.sem, skey_v.mark(f"sum {u}"))
                ve.wait_ge(sidx_a.sem, sidx_a(l, "flat"))
                rest()
                for _ in range(TOPK_S // 8):
                    nc.vector.max(top8[0:NS, :], work[:, 0:PAST + 1])
                    ve.drain()
                    nc.vector.match_replace(work[:, 0:PAST + 1], top8[0:NS, :], work[:, 0:PAST + 1], taken)
                    ve.drain()
                TS(work[:, 0:PAST + 1], work[:, 0:PAST + 1], taken, None, ALU.not_equal)
                ve.drain().then_inc(sidx_v.sem, sidx_v.mark("left out"))

                ve.wait_ge(hg_a.sem, hg_a(l, "gates"))
                for h in range(4):
                    TS(kT[:, h, :], kT[:, h, :], lb1[:, h:h + 1], None, ALU.mult)
                    TS(fT[:, h, :], fT[:, h, :], lb1[:, h:h + 1], lb[:, h:h + 1], ALU.mult, ALU.add)
                ve.memset(AT[:, 0:2, :, :], 0.0)
                ve.drain().then_inc(hg_v.sem, hg_v.mark("f"))
                ve.wait_ge(hg_a.sem, hg_a(l, "ln"))
                for h in range(4):
                    nc.vector.tensor_tensor_scan(cb[:, h, :], K("chunk_reset"), D_[:, h, :], 0.0, ALU.mult, ALU.add)
                ve.drain()
                DE = (E_, D_)
                q, k = Z[:, Z_HQ:Z_HQ + 4, 0:LP], kT[:, :, 0:LP]
                tot = cb.rearrange("p h (c t) -> p h c t", c=4)[:, :, :, 63]

                def decays(i):
                    d = DE[i % 2]
                    if i <= 6:
                        w = 1 << i
                        b = cb.rearrange("p h t -> p (h t)").rearrange("p (n z w) -> p n z w", z=2, w=w)
                        o = d.rearrange("p h t -> p (h t)").rearrange("p (n z w) -> p n z w", z=2, w=w)
                        mid = b[:, :, 0, w - 1:w].to_broadcast([128, 1024 // (2 * w), w])
                        TT(o[:, :, 0, :], mid, b[:, :, 0, :], ALU.subtract)
                        if i < 6:
                            TT(o[:, :, 1, :], b[:, :, 1, :], mid, ALU.subtract)
                        else:
                            TC(o[:, :, 1, :], b[:, :, 1, :])
                    else:
                        b = cb.rearrange("p h (c t) -> p h c t", c=4)
                        o = d.rearrange("p h (c t) -> p h c t", c=4)
                        T = lambda c: tot[:, :, c:c + 1].to_broadcast([128, 4, 64])
                        m = 4 if i == 8 else 2
                        TT(o[:, :, 0:m, :], tot[:, :, 0:m].unsqueeze(3).to_broadcast([128, 4, m, 64]), b[:, :, 0:m, :], ALU.subtract)
                        if i == 7:
                            TC(o[:, :, 2, :], b[:, :, 2, :])
                            TT(o[:, :, 3, :], b[:, :, 3, :], T(2), ALU.add)
                            ve.drain()
                            TT(o[:, :, 0, :], o[:, :, 0, :], T(1), ALU.add)
                        else:
                            TT(st[:, 0:4], tot[:, :, 3], tot[:, :, 2], ALU.add)
                            ve.drain()
                            TT(st[:, 4:8], st[:, 0:4], tot[:, :, 1], ALU.add)
                            TT(o[:, :, 2, :], o[:, :, 2, :], T(3), ALU.add)
                            TT(o[:, :, 1, :], o[:, :, 1, :], st[:, 0:4].unsqueeze(2).to_broadcast([128, 4, 64]), ALU.add)
                            ve.drain()
                            TT(o[:, :, 0, :], o[:, :, 0, :], st[:, 4:8].unsqueeze(2).to_broadcast([128, 4, 64]), ALU.add)
                    ve.drain().then_inc(hg_v.sem, hg_v.mark(f"d {i}"))

                def merge(i, banks, level):
                    ve.wait_ge(hg_p.sem, hg_p(l, "a diag" if i < 0 else f"a {i}"))
                    rest()
                    for t in range(2):
                        nc.vector.copy_predicated(AT[:, t, :, :], lvl[:, level:level + 1, :].to_broadcast([128, 4, 128]),
                                                  ps[:, banks + t, :].rearrange("p (h t) -> p h t", h=4))
                    ve.drain().then_inc(hg_v.sem, hg_v.mark("a diag" if i < 0 else f"a {i}"))

                decays(0)
                merge(-1, 2, 7)
                for i in range(9):
                    if i < 8:
                        decays(i + 1)
                    ve.wait_ge(hg_a.sem, hg_a(l, f"e {i}"))
                    m = M_[:, i % 2, :].rearrange("p (h t) -> p h t", h=4)
                    if i == 8:
                        TT(m, DE[i % 2], k, ALU.mult)
                    else:
                        w = 1 << i
                        cut = lambda x, z: x.rearrange("p h (n z w) -> p h n z w", z=2, w=w)[:, :, :, z, :]
                        TT(cut(m, 0), cut(DE[i % 2], 0), cut(k, 0), ALU.mult)
                        TT(cut(m, 1), cut(DE[i % 2], 1), cut(q, 1), ALU.mult)
                    ve.drain().then_inc(hg_v.sem, hg_v.mark(f"m {i}"))
                    if 1 <= i <= 7:
                        merge(i - 1, 4 if (i - 1) % 2 == 0 else 2, i - 1)
                ve.wait_ge(S_in, l * 64 + 64)
                for h in range(4):
                    TT(VD, HV[0:NS, 2:3, h * 128:h * 128 + 128].to_broadcast([NS, NS, 128]),
                       ident[0:NS, 0:NS].unsqueeze(2).to_broadcast([NS, NS, 128]), ALU.mult).then_inc(hg_v.sem, hg_v.mark(f"vd {h}"))
                    ve.wait_ge(hg_p.sem, hg_p(l, f"kv {h}"))
                    for s in range(NS):
                        STT(S[:, s, h, :], S[:, s, h, :], fT[:, h, LP + s:LP + s + 1], ps[:, 6 + s // 4, (s % 4) * 128:(s % 4) * 128 + 128],
                            ALU.mult, ALU.add)
                    ve.drain().then_inc(hg_v.sem, hg_v.mark(f"sn {h}"))
                ve.wait_ge(hg_a.sem, hg_a(l, "rs"))
                for h in range(4):
                    STT(HO[:, h, :], HO[:, h, :], gho[:, h:h + 1], HSQ[:, h, :], ALU.mult, ALU.mult)
                ve.drain()
                TT(Y[:, 0], Y[:, 0], HO, ALU.mult)
                ve.drain().then_inc(hg_v.sem, hg_v.mark("done"))

                def masked(u):
                    if u >= 2:
                        ve.wait_ge(at_p.sem, at_p(l, f"t {u - 2}"))
                    ve.wait_ge(at_p.sem, at_p(l, f"s {u}"))
                    b, c = 3 * (u % 2), 8 * (u % 2)
                    m = msk if u < 2 else causal
                    x0 = SX[:, u % 2, 0:512].rearrange("p (j s) -> p j s", j=4)
                    x1 = SX[:, u % 2, 512:1536].rearrange("p (j s) -> p j s", j=4)
                    STT(x0, ps[:, b, :].rearrange("p (j s) -> p j s", j=4), SCALE, m[:, 0:128].unsqueeze(1).to_broadcast([128, 4, 128]), ALU.mult, ALU.add)
                    STT(x1, ps[:, b + 1:b + 3, :].rearrange("p c (j s) -> p (c j) s", j=2), SCALE, m[:, 128:384].unsqueeze(1).to_broadcast([128, 4, 256]), ALU.mult, ALU.add)
                    ve.drain()
                    RED(st[:, c:c + 4], x0, AXX, ALU.max, negate=True)
                    RED(st[:, c + 4:c + 8], x1, AXX, ALU.max, negate=True)
                    ve.drain().then_inc(at_v.sem, at_v.mark(f"s {u}"))

                def out_of_psum(u):
                    ve.wait_ge(at_p.sem, at_p(l, f"o {u}"))
                    r, a = halves[u % 2], u // 2
                    for t in range(2):
                        o, c = ps[r, 6 + t, :].rearrange("p (j t) -> p j t", j=4), slice(t * 128, t * 128 + 128)
                        last = TT(Y[r, 1, :, c], o, Y[r, 1, :, c], ALU.mult) if a == 0 else TC(OC[r, a, :, c], o)
                    last.then_inc(at_v.sem, at_v.mark(f"ev {u}"))

                masked(0)
                for u in range(6):
                    if u < 5:
                        masked(u + 1)
                    ve.wait_ge(at_a.sem, at_a(l, f"e {u}"))
                    c = 8 * (u % 2)
                    x0 = SX[:, u % 2, 0:512].rearrange("p (j s) -> p j s", j=4)
                    x1 = SX[:, u % 2, 512:1536].rearrange("p (j s) -> p j s", j=4)
                    nc.vector.reciprocal(st[:, 16:24], sa[:, c:c + 8])
                    ve.drain()
                    TT(x0, x0, st[:, 16:20].unsqueeze(2).to_broadcast([128, 4, 128]), ALU.mult)
                    TT(x1, x1, st[:, 20:24].unsqueeze(2).to_broadcast([128, 4, 256]), ALU.mult)
                    ve.drain().then_inc(at_v.sem, at_v.mark(f"n {u}"))
                    if u:
                        out_of_psum(u - 1)
                out_of_psum(5)

                for kv in range(2):
                    ve.wait_ge(cp_p.sem, cp_p(l, f"hT {kv}"))
                    TT(hbias[:, kv:kv + 1], ps[:, 2 + kv, NCP:NCP + 1], b1[:, kv:kv + 1], ALU.add).then_inc(cp_v.sem, cp_v.mark(f"bias {kv}"))
                ve.wait_ge(cp_p.sem, cp_p(l, "s"))
                for t in range(2):
                    for g in range(2):
                        STT(SC[:, t, 4 * g:4 * g + 4], ps[:, 4 + 2 * g + t, 0:4 * NCP].rearrange("p (h c) -> p h c", h=4), SCALE,
                            K("cmp_add")[:, t * NCP:(t + 1) * NCP].unsqueeze(1).to_broadcast([128, 4, NCP]), ALU.mult, ALU.add)
                ve.drain()
                RED(st[:, 0:16].rearrange("p (t h) -> p t h", t=2), SC, AXX, ALU.max)
                ve.drain()
                scb = SC.rearrange("p t h c -> p (t h) c")
                TT(scb, scb, st[:, 0:16].unsqueeze(2).to_broadcast([128, 16, NCP]), ALU.subtract).then_inc(cp_v.sem, cp_v.mark("s"))
                ve.wait_ge(cp_a.sem, cp_a(l, "e"))
                RED(st[:, 16:32].rearrange("p (t h) -> p t h", t=2), SC, AXX, ALU.add)
                ve.drain()
                nc.vector.reciprocal(st[:, 32:48], st[:, 16:32])
                ve.drain()
                TT(scb, scb, st[:, 32:48].unsqueeze(2).to_broadcast([128, 16, NCP]), ALU.mult)
                ve.drain()
                TT(SC, SC, K("cmp_mul").rearrange("p (t c) -> p t c", t=2).unsqueeze(2).to_broadcast([128, 2, NH, NCP]), ALU.mult)\
                    .then_inc(cp_v.sem, cp_v.mark("n"))
                ve.wait_ge(cp_a.sem, cp_a(l, "nb"))
                TS(nbs[0:24, :], nbs[0:24, :], 1.0, None, ALU.add)
                ve.drain()
                nc.vector.reciprocal(nbs[0:24, :], nbs[0:24, :]).then_inc(cp_v.sem, cp_v.mark("nb"))
                ve.wait_ge(cp_p.sem, cp_p(l, "o"))
                for g, r in enumerate(halves):
                    for t in range(2):
                        TC(OC[r, 0, :, t * 128:t * 128 + 128], ps[r, 4 + 2 * g + t, :].rearrange("p (j t) -> p j t", j=4))
                ve.drain().then_inc(cp_v.sem, cp_v.mark("ev"))
                for i in range(12):
                    c, j = i // 4, i % 4
                    ve.wait_ge(cp_p.sem, cp_p(l, f"gb {i}"))
                    if c == 0:
                        TT(OC[:, 0, j, :], ps[:, i % 4, 0:LP], OC[:, 0, j, :], ALU.mult)
                    else:
                        TT(OC[:, c, j, :], ps[:, i % 4, 0:LP], OC[:, c, j, :], ALU.mult)
                        ve.drain()
                        TT(OC[:, 0, j, :], OC[:, 0, j, :], OC[:, c, j, :], ALU.add)
                    TC(gbs[:, i, :], ps[:, i % 4, seq_cols])
                    ve.drain().then_inc(cp_v.sem, cp_v.mark(f"gb {i}"))
                TT(Y[:, 2, :, 0:LP], Y[:, 2, :, 0:LP], OC[:, 0], ALU.mult)
                ve.drain().then_inc(cp_v.sem, cp_v.mark("prompt done"))

                for g in range(2):
                    with ve.Fori(0, GB) as b:
                        s = b + g * GB
                        r = l * NS + s
                        ve.wait_ge(pg_p.sem, pg_p.before(r, "s win"))
                        TS(QP[:, :, :], QC[:, :, bass.ds(s * ROWS, ROWS)], 1.0, None, ALU.mult).then_inc(pg_v.sem, pg_v.mark("q"))
                        for i in range(1, NPG, 2):
                            ve.wait_ge(pg_p.sem, pg_p(r, f"T {i}"))
                            x = ps[:, 6, :].rearrange("p (c x) -> p c x", c=4)
                            TC(KT[:, 1], x[:, 0:4:3, :])
                            TS(cT[:, :, bass.ds(b, 1), i * 128:i * 128 + 128].rearrange("p k b c -> p k (b c)"), x[:, 1:3, :], 1.0, None,
                               ALU.mult)
                            ve.drain().then_inc(pg_v.sem, pg_v.mark(f"T {i}"))
                ve.memset(PTcx, 0.0)
                ve.wait_ge(dc_p.sem, dc_p(l, "s cmp"))
                c4, c40 = sc4[0:ROWS, 0:NCS], st[0:ROWS, 40:41]
                TS(c4, ps[0:ROWS, 5, 0:NCS], SCALE, None, ALU.mult)
                ve.drain()
                RED(c40, c4, AXX, ALU.max, negate=True).then_inc(dc_v.sem, dc_v.mark("s cmp"))
                ve.memset(PTx[0], 0.0)
                ve.wait_ge(dc_a.sem, dc_a(l, "e cmp"))
                nc.vector.reciprocal(c40, sa[0:ROWS, 40:41])
                ve.drain()
                TS(c4, c4, c40, None, ALU.mult).then_inc(dc_v.sem, dc_v.mark("n cmp"))
                ve.wait_ge(dc_a.sem, dc_a(l, "t cmp"))
                TC(PTcx.rearrange("p (b x) -> p b x", b=NS)[:, :, 0:NH], PTc[0:NCS].rearrange("p (b h) -> p b h", b=NS))\
                    .then_inc(dc_v.sem, dc_v.mark("ptx cmp"))
                ve.wait_ge(dc_p.sem, dc_p(l, "imp"))
                d17 = dr[0:ROWS, 0:NSEL]
                TC(d17, ps[0:ROWS, 5, 0:NSEL]).then_inc(dc_v.sem, dc_v.mark("imp"))
                ve.wait_ge(dc_p.sem, dc_p(l, "group imp"))
                TT(d17, ps[0:ROWS, 5, 0:NSEL], K("not_forced", ROWS), ALU.mult)
                ve.drain()
                TT(d17, d17, K("forced", ROWS), ALU.add)
                ve.drain()
                RED(st[0:ROWS, 41:42], d17, AXX, ALU.min)
                ve.drain()
                STT(d17, d17, st[0:ROWS, 41:42], K("order", ROWS), ALU.is_equal, ALU.mult)
                ve.drain()
                RED(st[0:ROWS, 42:43], d17, AXX, ALU.max)
                ve.drain()
                TS(d17, d17, st[0:ROWS, 42:43], None, ALU.is_equal)
                ve.drain().then_inc(dc_v.sem, dc_v.mark("drop"))
                ve.wait_ge(dc_a.sem, dc_a(l, "scores"))
                ve.wait_ge(dc_p.sem, dc_p(l, "new"))
                own = K("own_s", ROWS)
                ncol = (PAST, PAST, WIN)
                dn = dr[0:ROWS, 24:48].rearrange("p (a s) -> p a s", a=3)
                TT(dn, ps[0:ROWS, 6, 0:24].rearrange("p (a s) -> p a s", a=3), own.unsqueeze(1).to_broadcast([ROWS, 3, NS]), ALU.mult)
                for i in range(2):
                    x = SS[0][0:ROWS, i * 512:i * 512 + 512]
                    STT(x, ps[0:ROWS, i, :], NEG, x, ALU.mult, ALU.add)
                x = SS[1][0:ROWS, 0:PAST].rearrange("p (j c) -> p j c", c=SB)
                STT(x, dr[0:ROWS, 0:NSEL - 1].unsqueeze(2).to_broadcast([ROWS, NSEL - 1, SB]), NEG, x, ALU.mult, ALU.add)
                ve.memset(SS[2][0:ROWS, 0:1], NEG)
                ve.drain()
                RED(st[0:ROWS, 49:52], dn, AXX, ALU.add)
                ve.drain()
                for a in range(3):
                    TS(SS[a][0:ROWS, ncol[a]:ncol[a] + 1], st[0:ROWS, 49 + a:50 + a], SCALE, None, ALU.mult)
                ve.drain()
                x = SS[0][0:ROWS, PAST:PAST + 1]
                STT(x, ps[0:ROWS, 6, 32:33], NEG, x, ALU.mult, ALU.add)
                ve.drain()
                for a in range(3):
                    RED(st[0:ROWS, 43 + a:44 + a], SS[a][0:ROWS, 0:ncol[a] + 1], AXX, ALU.max, negate=True)
                ve.drain().then_inc(dc_v.sem, dc_v.mark("masked"))
                ve.wait_ge(dc_a.sem, dc_a(l, "e"))
                nc.vector.reciprocal(st[0:ROWS, 46:49], sa[0:ROWS, 43:46])
                for a in range(3):
                    TS(dn[:, a, :], own, SS[a][0:ROWS, ncol[a]:ncol[a] + 1], None, ALU.mult)
                ve.drain().then_inc(dc_v.sem, dc_v.mark("new p"))
                ve.wait_ge(dc_p.sem, dc_p(l, "PT"))
                ve.memset(PTx[1], 0.0)
                ve.wait_ge(dc_a.sem, dc_a(l, "PT"))
                rest()
                for b in range(NS):
                    own_cols = lambda x, b: x[:, :, b * NH:b * NH + NH]
                    if b >= 2:
                        ve.wait_ge(dx_p.sem, dx_p(l, f"x {b - 2}"))
                        ve.memset(own_cols(PTx[b % 2], b - 2), 0.0)
                    TC(own_cols(PTx[b % 2], b), own_cols(PTd, b))
                    ve.drain().then_inc(dx_v.sem, dx_v.mark(f"x {b}"))
                ve.wait_ge(dx_p.sem, dx_p(l, f"x {NS - 1}"))
                for a, bank in enumerate((0, 1, 5)):
                    TS(so[0:ROWS, a, :], ps[0:ROWS, bank, 0:128], st[0:ROWS, 46 + a:47 + a], None, ALU.mult)
                TC(so[0:ROWS, 3, :], ps[0:ROWS, 7, 0:128])
                ve.drain().then_inc(dc_v.sem, dc_v.mark("scaled"))
                ve.wait_ge(dc_p.sem, dc_p(l, "oT"))
                for gg, r in enumerate(halves):
                    o = ps[:, 6, 0:4 * ROWS].rearrange("p (a s g j) -> p a g j s", a=4, g=2, j=4)[r, :, gg]
                    TT(Y[r, 1, :, seq_cols], Y[r, 1, :, seq_cols], o[:, 0], ALU.mult)
                    for c, a in enumerate((3, 1, 2)):
                        TT(o3[r, c], gbs[r, 4 * c:4 * c + 4, :], o[:, a], ALU.mult)
                ve.drain()
                TT(o3[:, 0], o3[:, 0], o3[:, 1], ALU.add)
                ve.drain()
                TT(o3[:, 3], o3[:, 0], o3[:, 2], ALU.add)
                ve.drain()
                TT(Y[:, 2, :, seq_cols], Y[:, 2, :, seq_cols], o3[:, 3], ALU.mult)
                ve.drain().then_inc(dc_v.sem, dc_v.mark("ev"))

                for a in range(3):
                    for d in range(KD):
                        ve.wait_ge(ga_a.sem, ga_a(l, f"m {a} {d}"))
                        ve.wait_ge(ga_p.sem, ga_p(l, f"b {a} {d}"))
                        if a == 0:
                            TT(mT[:, d, :], ps[:, d % 4, 0:LT], sig[:, d, :], ALU.mult)
                        else:
                            TT(mtmp[:, d % 2, :], ps[:, d % 4, 0:LT], sig[:, d, :], ALU.mult)
                            ve.drain()
                            TT(mT[:, d, :], mT[:, d, :], mtmp[:, d % 2, :], ALU.add)
                        ve.drain().then_inc(ga_v.sem, ga_v.mark(f"b {a} {d}"))
                for i in range(4):
                    for t in range(3):
                        n = 3 * i + t
                        ve.wait_ge(ga_p.sem, ga_p(l, f"o {n}"))
                        m = 128 if t < 2 else NS
                        x = xp[:, t, i * 256:i * 256 + 256] if t < 2 else xs[:, i * 256:i * 256 + 256]
                        TT(x, x, ps[0:m, n % 4, 0:256], ALU.add).then_inc(ga_v.sem, ga_v.mark(f"o {n}"))
                TT(lb[:, :], lb[:, :], lbl[:, bass.ds(l + 1, 1), :].rearrange("p a h -> p (a h)"), ALU.add)
                ve.drain()
                TS(lb1[:, :], lb[:, :], -1.0, 1.0, ALU.mult, ALU.add)
                ve.drain().then_inc(x_ready, 1)

        for steps in all_steps:
            assert steps.done and steps.done % steps.n == 0, (steps.steps[0], steps.done, steps.n)


_INS = ['x_prompt', 'x_sample', 'cache_kv', 'page_table', 'state_win', 'state_hgrn', 'norm_g', 'w_in',
        'hgrn_lb_logits', 'hgrn_onorm_g', 'dsa_qk_norm_g', 'dsa_idx_k_norm_g', 'nsa_qk_norm_g', 'nsa_cmp_pe',
        'nsa_cmp_w1', 'nsa_cmp_b1', 'nsa_cmp_w2', 'w_branch', 'w_out']
_OUTS = [(1, LP, D), (NS, 1, D), (DEPTH, 1, LP, CW), (DEPTH, 1, LP, 256), (DEPTH, 1, 4, 128, 128),
         (DEPTH, NS, 1, CW), (DEPTH, NS, WIN, 256), (DEPTH, NS, 4, 128, 128)]


def kernel(**inputs):
    import numpy as _np
    import concourse.bacc as _bacc
    from concourse import mybir as _mybir
    from concourse.bass_utils import run_bass_kernel_spmd as _run

    nc = _bacc.Bacc("TRN2", target_bir_lowering=False, num_devices=1)
    given = {name: _np.ascontiguousarray(inputs[name]) for name in _INS}
    given["const"] = constants()
    given["gate_rows"] = branch_gate_rows()
    arrays, args = {}, []
    for name, a in given.items():
        arrays[f"in_{name}_dram"] = a
        args.append(nc.dram_tensor(f"in_{name}_dram", a.shape, _mybir.dt.from_np(a.dtype), kind="ExternalInput").ap())
    for i, shape in enumerate(_OUTS):
        args.append(nc.dram_tensor(f"out_{i}_dram", shape, _mybir.dt.float32, kind="ExternalOutput").ap())
    hybrid_step(nc, *args)
    r = _run(nc, [arrays], core_ids=[0])
    return tuple(r.results[0][f"out_{i}_dram"] for i in range(len(_OUTS)))
```
